# Optimizing a Trainium2 kernel written in Bass

```python
import jax
import jax.numpy as jnp
from jax import lax
import numpy as np

D_MODEL = 1024
BATCH = 1
SEQ = 512
DEPTH = 2

N_META = 16
BLOCK = 128
EPS = 1e-6
FOX_HEADS = 8
FOX_HEAD_DIM = 64
MLA_HEADS = 8
MLA_Q_RANK = 256
MLA_KV_RANK = 128
MLA_NOPE_DIM = 64
MLA_ROPE_DIM = 32
MLA_V_DIM = 64
ROPE_THETA = 10000.0
SWA_Q_HEADS = 8
SWA_KV_HEADS = 2
SWA_HEAD_DIM = 64
WINDOW = 128
N_BRANCH = 3
BRANCH_WIDTH = FOX_HEADS * FOX_HEAD_DIM
D_FF = 2816
CONV_WIDTH = 3
IN_SPLITS = (FOX_HEADS * FOX_HEAD_DIM, FOX_HEADS * FOX_HEAD_DIM, FOX_HEADS * FOX_HEAD_DIM, FOX_HEADS,
             MLA_Q_RANK, MLA_KV_RANK, MLA_ROPE_DIM,
             SWA_Q_HEADS * SWA_HEAD_DIM, SWA_KV_HEADS * SWA_HEAD_DIM, SWA_KV_HEADS * SWA_HEAD_DIM,
             N_BRANCH * D_MODEL)
IN_WIDTH = sum(IN_SPLITS)

kernel_name = 'hybrid_fox_mla_swa_convffn'

def rms_norm(x, g):
    xf = x.astype(jnp.float32)
    y = xf * lax.rsqrt(jnp.mean(xf * xf, axis=-1, keepdims=True) + EPS)
    return (y * g.astype(jnp.float32)).astype(x.dtype)

def rope(x, pos):
    half = x.shape[-1] // 2
    freqs = ROPE_THETA ** (-jnp.arange(half, dtype=jnp.float32) / half)
    ang = pos.astype(jnp.float32)[:, None] * freqs[None, :]
    cos = jnp.cos(ang)[:, None, :]
    sin = jnp.sin(ang)[:, None, :]
    xf = x.astype(jnp.float32)
    x1, x2 = xf[..., :half], xf[..., half:]
    return jnp.concatenate([x1 * cos - x2 * sin, x2 * cos + x1 * sin], axis=-1).astype(x.dtype)

def alibi_slopes(n_heads):
    return jnp.exp2(-8.0 * jnp.arange(1, n_heads + 1, dtype=jnp.float32) / n_heads)

def causal_block_attention(q, k, v, log_decay=None):
    B, L, H, dk = q.shape
    M = N_META
    nb = (L - M) // BLOCK
    scale = dk ** -0.5
    pos = jnp.arange(L)

    def attend(qb, qpos, kk, vv, kpos, qdec=None, kdec=None):
        s = jnp.einsum('bqhd,bkhd->bhqk', qb, kk, preferred_element_type=jnp.float32) * scale
        if qdec is not None:
            s = s + jnp.swapaxes(qdec, 1, 2)[..., :, None] - jnp.swapaxes(kdec, 1, 2)[..., None, :]
        s = jnp.where(kpos[None, :] <= qpos[:, None], s, -jnp.inf)
        p = jax.nn.softmax(s, axis=-1).astype(vv.dtype)
        return jnp.einsum('bhqk,bkhd->bqhd', p, vv)

    qb = q[:, M:].reshape(B, nb, BLOCK, H, dk).swapaxes(0, 1)
    posb = pos[M:].reshape(nb, BLOCK)
    if log_decay is not None:
        meta = attend(q[:, :M], pos[:M], k[:, :M], v[:, :M], pos[:M], log_decay[:, :M], log_decay[:, :M])
        decb = log_decay[:, M:].reshape(B, nb, BLOCK, H).swapaxes(0, 1)
        real = lax.map(lambda a: attend(a[0], a[1], k, v, pos, a[2], log_decay), (qb, posb, decb))
    else:
        meta = attend(q[:, :M], pos[:M], k[:, :M], v[:, :M], pos[:M])
        real = lax.map(lambda a: attend(a[0], a[1], k, v, pos), (qb, posb))
    real = real.swapaxes(0, 1).reshape(B, L - M, H, v.shape[-1])
    return jnp.concatenate([meta, real], axis=1)

def sliding_window_attention(q, k, v, sinks, slopes):
    B, L, Hq, d = q.shape
    Hkv = k.shape[2]
    G = Hq // Hkv
    M = N_META
    nb = (L - M) // BLOCK
    scale = d ** -0.5
    q = q.reshape(B, L, Hkv, G, d)
    sinks = sinks.astype(jnp.float32).reshape(Hkv, G)
    slopes = slopes.reshape(Hkv, G, 1, 1)

    def attend(qq, kk, vv, valid, dist):
        s = jnp.einsum('...qhgd,...khd->...hgqk', qq, kk, preferred_element_type=jnp.float32) * scale - slopes * dist
        s = jnp.where(valid, s, -jnp.inf)
        sink = jnp.broadcast_to(sinks[:, :, None, None], s.shape[:-1] + (1,))
        p = jax.nn.softmax(jnp.concatenate([s, sink], axis=-1), axis=-1)[..., :-1].astype(vv.dtype)
        return jnp.einsum('...hgqk,...khd->...qhgd', p, vv)

    mpos = jnp.arange(M)
    mdist = (mpos[:, None] - mpos[None, :]).astype(jnp.float32)
    meta = attend(q[:, :M], k[:, :M], v[:, :M], mdist >= 0, mdist)

    def band(t):
        tr = t[:, M:].reshape(B, nb, BLOCK, Hkv, d)
        prev = jnp.concatenate([jnp.zeros_like(tr[:, :1]), tr[:, :-1]], axis=1)
        meta_t = jnp.broadcast_to(t[:, None, :M], (B, nb, M, Hkv, d))
        return jnp.concatenate([meta_t, prev, tr], axis=2)

    blk = jnp.arange(nb)
    qpos = M + blk[:, None] * BLOCK + jnp.arange(BLOCK)[None, :]
    band_pos = M + (blk[:, None] - 1) * BLOCK + jnp.arange(2 * BLOCK)[None, :]
    band_dist = qpos[:, :, None] - band_pos[:, None, :]
    band_ok = (band_pos[:, None, :] >= M) & (band_dist >= 0) & (band_dist < WINDOW)
    meta_dist = qpos[:, :, None] - mpos[None, None, :]
    valid = jnp.concatenate([jnp.ones((nb, BLOCK, M), dtype=bool), band_ok], axis=-1)
    dist = jnp.concatenate([meta_dist, band_dist], axis=-1).astype(jnp.float32)
    qr = q[:, M:].reshape(B, nb, BLOCK, Hkv, G, d)
    real = attend(qr, band(k), band(v), valid[:, None, None], dist[:, None, None])
    return jnp.concatenate([meta.reshape(B, M, Hq, d), real.reshape(B, L - M, Hq, d)], axis=1)

def mixer_block(h, norm1_g, w_in, fox_forget_b, fox_q_g, fox_k_g, mla_q_a_g, mla_w_q_up, mla_kv_a_g,
                mla_w_kv_up, mla_q_g, mla_k_g, swa_q_g, swa_k_g, swa_sinks, w_branch, w_o):
    B, L, _ = h.shape
    pos = jnp.arange(L)
    xn = rms_norm(h, norm1_g)
    proj = xn @ w_in
    offsets = [int(o) for o in np.cumsum(IN_SPLITS)[:-1]]
    fq, fk, fv, ff, cq, ckv, krope, sq, sk, sv, gates = jnp.split(proj, offsets, axis=-1)

    fq = rms_norm(fq.reshape(B, L, FOX_HEADS, FOX_HEAD_DIM), fox_q_g)
    fk = rms_norm(fk.reshape(B, L, FOX_HEADS, FOX_HEAD_DIM), fox_k_g)
    fv = fv.reshape(B, L, FOX_HEADS, FOX_HEAD_DIM)
    log_decay = jnp.cumsum(jax.nn.log_sigmoid((ff + fox_forget_b).astype(jnp.float32)), axis=1)
    out_a = causal_block_attention(fq, fk, fv, log_decay)

    q = (rms_norm(cq, mla_q_a_g) @ mla_w_q_up).reshape(B, L, MLA_HEADS, MLA_NOPE_DIM + MLA_ROPE_DIM)
    q = rms_norm(q, mla_q_g)
    q = jnp.concatenate([q[..., :MLA_NOPE_DIM], rope(q[..., MLA_NOPE_DIM:], pos)], axis=-1)
    kv = (rms_norm(ckv, mla_kv_a_g) @ mla_w_kv_up).reshape(B, L, MLA_HEADS, MLA_NOPE_DIM + MLA_V_DIM)
    k_nope, v_mla = kv[..., :MLA_NOPE_DIM], kv[..., MLA_NOPE_DIM:]
    k = jnp.concatenate([k_nope, jnp.broadcast_to(krope[:, :, None, :], (B, L, MLA_HEADS, MLA_ROPE_DIM))], axis=-1)
    k = rms_norm(k, mla_k_g)
    k = jnp.concatenate([k[..., :MLA_NOPE_DIM], rope(k[..., MLA_NOPE_DIM:], pos)], axis=-1)
    out_b = causal_block_attention(q, k, v_mla)

    sq = rms_norm(sq.reshape(B, L, SWA_Q_HEADS, SWA_HEAD_DIM), swa_q_g)
    sk = rms_norm(sk.reshape(B, L, SWA_KV_HEADS, SWA_HEAD_DIM), swa_k_g)
    sv = sv.reshape(B, L, SWA_KV_HEADS, SWA_HEAD_DIM)
    out_c = sliding_window_attention(sq, sk, sv, swa_sinks, alibi_slopes(SWA_Q_HEADS))

    branches = jnp.stack([out_a.reshape(B, L, BRANCH_WIDTH), out_b.reshape(B, L, BRANCH_WIDTH),
                          out_c.reshape(B, L, BRANCH_WIDTH)], axis=2)
    g = jax.nn.sigmoid(gates.reshape(B, L, N_BRANCH, D_MODEL))
    y = jnp.einsum('blnc,ncd->blnd', branches, w_branch)
    merged = jnp.sum(g * y, axis=2)
    return h + merged @ w_o

def conv_ffn(h, norm2_g, w_up, conv_w, conv_b, w_down):
    L = h.shape[1]
    u = rms_norm(h, norm2_g) @ w_up
    up = jnp.pad(u, ((0, 0), (CONV_WIDTH - 1, 0), (0, 0)))
    c = conv_b
    for i in range(CONV_WIDTH):
        c = c + conv_w[i] * up[:, i:i + L]
    gate, val = jnp.split(c, 2, axis=-1)
    return h + (jax.nn.silu(gate) * val) @ w_down

def setup_inputs(seed: int = 0) -> dict:
    key = jax.random.key(seed)
    ks = jax.random.split(key, 23)
    f32 = jnp.float32
    nrm = lambda k, shape, s: jax.random.normal(k, shape, f32) * s
    gain = lambda k, shape: 1.0 + 0.1 * jax.random.normal(k, shape, f32)
    return {
        'x': nrm(ks[0], (BATCH, SEQ, D_MODEL), 1.0),
        'meta_tokens': nrm(ks[1], (N_META, D_MODEL), 1.0),
        'norm1_g': gain(ks[2], (DEPTH, D_MODEL)),
        'w_in': nrm(ks[3], (DEPTH, D_MODEL, IN_WIDTH), D_MODEL ** -0.5),
        'fox_forget_b': 3.0 + 0.1 * jax.random.normal(ks[4], (DEPTH, FOX_HEADS), f32),
        'fox_q_g': gain(ks[5], (DEPTH, FOX_HEAD_DIM)),
        'fox_k_g': gain(ks[6], (DEPTH, FOX_HEAD_DIM)),
        'mla_q_a_g': gain(ks[7], (DEPTH, MLA_Q_RANK)),
        'mla_w_q_up': nrm(ks[8], (DEPTH, MLA_Q_RANK, MLA_HEADS * (MLA_NOPE_DIM + MLA_ROPE_DIM)), MLA_Q_RANK ** -0.5),
        'mla_kv_a_g': gain(ks[9], (DEPTH, MLA_KV_RANK)),
        'mla_w_kv_up': nrm(ks[10], (DEPTH, MLA_KV_RANK, MLA_HEADS * (MLA_NOPE_DIM + MLA_V_DIM)), MLA_KV_RANK ** -0.5),
        'mla_q_g': gain(ks[11], (DEPTH, MLA_NOPE_DIM + MLA_ROPE_DIM)),
        'mla_k_g': gain(ks[12], (DEPTH, MLA_NOPE_DIM + MLA_ROPE_DIM)),
        'swa_q_g': gain(ks[13], (DEPTH, SWA_HEAD_DIM)),
        'swa_k_g': gain(ks[14], (DEPTH, SWA_HEAD_DIM)),
        'swa_sinks': nrm(ks[15], (DEPTH, SWA_Q_HEADS), 0.5),
        'w_branch': nrm(ks[16], (DEPTH, N_BRANCH, BRANCH_WIDTH, D_MODEL), BRANCH_WIDTH ** -0.5),
        'w_o': nrm(ks[17], (DEPTH, D_MODEL, D_MODEL), D_MODEL ** -0.5),
        'norm2_g': gain(ks[18], (DEPTH, D_MODEL)),
        'ffn_w_up': nrm(ks[19], (DEPTH, D_MODEL, 2 * D_FF), D_MODEL ** -0.5),
        'ffn_conv_w': nrm(ks[20], (DEPTH, CONV_WIDTH, 2 * D_FF), CONV_WIDTH ** -0.5),
        'ffn_conv_b': nrm(ks[21], (DEPTH, 2 * D_FF), 0.02),
        'ffn_w_down': nrm(ks[22], (DEPTH, D_FF, D_MODEL), D_FF ** -0.5),
    }

def reference(x, meta_tokens, norm1_g, w_in, fox_forget_b, fox_q_g, fox_k_g, mla_q_a_g, mla_w_q_up,
              mla_kv_a_g, mla_w_kv_up, mla_q_g, mla_k_g, swa_q_g, swa_k_g, swa_sinks, w_branch, w_o,
              norm2_g, ffn_w_up, ffn_conv_w, ffn_conv_b, ffn_w_down):
    B = x.shape[0]
    meta = jnp.broadcast_to(meta_tokens[None].astype(x.dtype), (B, N_META, x.shape[-1]))
    h = jnp.concatenate([meta, x], axis=1)
    for l in range(DEPTH):
        h = mixer_block(h, norm1_g[l], w_in[l], fox_forget_b[l], fox_q_g[l], fox_k_g[l], mla_q_a_g[l],
                        mla_w_q_up[l], mla_kv_a_g[l], mla_w_kv_up[l], mla_q_g[l], mla_k_g[l], swa_q_g[l],
                        swa_k_g[l], swa_sinks[l], w_branch[l], w_o[l])
        h = conv_ffn(h, norm2_g[l], ffn_w_up[l], ffn_conv_w[l], ffn_conv_b[l], ffn_w_down[l])
    return h[:, N_META:]


_drawn_inputs = setup_inputs


def setup_inputs(seed=0):
    import zlib

    import numpy as np

    out = dict(_drawn_inputs(seed))
    spreads = {}
    factors = {'fox_forget_b': 31.056,
     'mla_q_a_g': 4.684,
     'mla_kv_a_g': 2.97,
     'mla_q_g': 4.521,
     'mla_k_g': 4.714,
     'swa_q_g': 2.956,
     'swa_k_g': 2.999,
     'swa_sinks': 26.602,
     'ffn_conv_b': 2.684,
     'fox_k_g': 3.095}
    for name, (base, spread) in spreads.items():
        noise = np.random.default_rng([zlib.crc32(name.encode()), seed]).standard_normal(out[name].shape)
        drawn = base * np.exp(spread * noise) if base else spread * noise
        out[name] = jnp.asarray(drawn.astype(out[name].dtype))
    for name, factor in factors.items():
        out[name] = (out[name] * factor).astype(out[name].dtype)
    return out
```

```python
import concourse.bass as bass
import numpy as np
from concourse import mybir

F32 = mybir.dt.float32
F32R = mybir.dt.float32r
ALU = mybir.AluOpType
ACT = mybir.ActivationFunctionType
AX = mybir.AxisListType

P = 128
D = 1024
DEPTH = 2
SEQ = 512
META = 16
T = META + SEQ
TH = T // 2
KD = D // P
HEADS = 8
HD = 64
ROPE = 32
MQ = HD + ROPE
D_FF = 2816
FT = D_FF // P
EPS = 1e-6
NEG = -1.0e30
BRANCH_TILES = HEADS * HD // P
QTILES = 1 + SEQ // P
FOX, MLA, SWA = range(3)

BLK = 8
CW = BLK * P
RAW, SPLIT = 2, 4
STARTED_BEFORE = 2
AHEAD = 2

OFF = np.cumsum([0, 512, 512, 512, 8, 256, 128, 32, 512, 128, 128])
O_FQ, O_FK, O_FV, O_FF, O_CQ, O_CKV, O_KR, O_SQ, O_SK, O_SV, O_GATE = (int(v) for v in OFF)

PC_N1, PC_N2 = 0, 8
PC_FQ, PC_FK, PC_QA, PC_KVA, PC_MQ, PC_MK, PC_SQ, PC_SK, PC_FB = 16, 17, 18, 20, 21, 22, 23, 24, 25
PC_SINK = 26
PC_CW = 34
PC_CB = PC_CW + 3 * 2 * FT
PC_ALL = PC_CB + 2 * FT

CC_ID, CC_ONE, CC_PAIR, CC_MASK, CC_CS, CC_ALL = 0, 128, 256, 384, 512, 512 + T
DW = META + 2 * P
DIST_AT = [0, META]
for _b in range(2, QTILES + 1):
    DIST_AT.append(DIST_AT[-1] + (META + P if _b == 2 else DW))


SQUARED = {"fq": P, "fk": P, "sq": P, "sk": P, "cq": P, "ckv": P, "mq": MQ, "mk": HD}
MEAN_OF = {"fq": HD, "fk": HD, "sq": HD, "sk": HD, "cq": 2 * P, "ckv": P, "mq": MQ, "mk": MQ}
OT_DELAY = 2
TILE_BLOCKS = {"ff": 2 * BLK, "fv": 4 * KD, "fq": KD, "fk": KD, "cq": KD, "ckv": KD, "kr": KD, "mv": 4, "mq": 2,
               "mk": 1, "sv": KD, "sq": KD, "sk": KD, "g": KD, "y": BRANCH_TILES}
FILL_SPAN = 0.7
SP_CQ = KD
SP_MERGED = SP_CQ + 3
SP_NORM2 = SP_MERGED + KD
SP_FFN = SP_NORM2 + KD


def stream_plan():
    b = []

    def tile(what, rows, m):
        b.extend((what, k, m) for k in range(rows))

    pad = [("pad", 0, 0)]
    b += [("ff", k, 0) for k in range(4)] + pad * 4 + [("ff", k, 0) for k in range(4, 8)] + pad * 4
    b += [("fv", k, m) for k in range(KD) for m in range(4)]
    for m in range(4):
        tile("fq", KD, m)
    for m in range(4):
        tile("fk", KD, m)
    for m in range(2):
        tile("cq", KD, m)
    tile("ckv", KD, 0)
    tile("kr", KD, 0)
    b += [("mv", 0, m) for m in range(4)]
    for h in range(HEADS):
        tile("mq", 2, h)
    for h in range(HEADS):
        tile("mk", 1, h)
    b += pad * 4
    gb = {}
    for br in (FOX, MLA, SWA):
        gb[br] = []
        for d in range(KD):
            gb[br] += [(f"g{br}", k, d) for k in range(KD)] + [(f"y{br}", k, d) for k in range(BRANCH_TILES)]
    n_mla = len(b)
    b += gb[FOX]
    b += [("sv", k, 0) for k in range(KD)]
    for m in range(4):
        tile("sq", KD, m)
    tile("sk", KD, 0)
    b += gb[MLA] + gb[SWA]
    for m in range(KD):
        tile("wo", KD, m)
    for f in range(FT):
        tile("up", KD, f)
        tile("up", KD, FT + f)
    for m in range(KD):
        tile("dn", FT, m)
        b += pad * 2
    assert len(b) % (BLK * 4) == 0
    return b


PLAN = stream_plan()
CHUNKS = len(PLAN) // BLK


def alibi_tables():
    i = np.arange(P)[:, None]
    out = []
    for b in range(1, QTILES):
        qpos = META + (b - 1) * P + i
        meta = qpos - np.arange(META)[None, :]
        lo = META + (b - 2) * P
        kpos = lo + np.arange(2 * P)[None, :]
        dist = qpos - kpos
        ok = (dist >= 0) & (dist < P) & (kpos >= META)
        band = np.where(ok, dist, -NEG)
        if b == 1:
            band = band[:, P:]
        out.append(np.concatenate([meta, band], axis=1))
    m = np.arange(META)
    dm = np.zeros((P, META))
    dm[:META] = np.where(m[:, None] >= m[None, :], m[:, None] - m[None, :], -NEG)
    return np.concatenate([dm] + out, axis=1).astype(np.float32)


def constants():
    c = np.zeros((P, CC_ALL), np.float32)
    c[:, CC_ID:CC_ID + P] = np.eye(P)
    c[:, CC_ONE:CC_ONE + P] = 1.0
    c[:HD, CC_PAIR:CC_PAIR + HD] = 1.0
    c[HD:, CC_PAIR + HD:CC_PAIR + P] = 1.0
    c[:, CC_MASK:CC_MASK + P] = np.where(np.arange(P)[None, :] <= np.arange(P)[:, None], 0.0, NEG)
    half = ROPE // 2
    freqs = np.float32(10000.0) ** (-np.arange(half, dtype=np.float32) / np.float32(half))
    ang = (np.arange(T, dtype=np.float32)[:, None] * freqs[None, :]).T.astype(np.float32)
    cos, sin = np.cos(ang), np.sin(ang)
    c[:, CC_CS:CC_CS + T] = 1.0
    c[HD:MQ, CC_CS:CC_CS + T] = np.concatenate([cos, cos])
    c[MQ:P, CC_CS:CC_CS + T] = np.concatenate([-sin, sin])
    return c


class Signal:

    def __init__(self, nc, name, counts, before=0):
        self.sem = nc.alloc_semaphore(name)
        self.name, self.n = name, 0
        self.before = before
        self.per_layer = counts.get(name, 10 ** 5)

    def tick(self, by=1):
        self.n += by
        return by

    def skip(self, n):
        self.n += n

    def at(self, layer, n):
        return layer * self.per_layer + (n + self.before)


class Unit:

    def __init__(self, i, br, b, h):
        self.i, self.br, self.b, self.h = i, br, b, h
        self.nq = P
        self.q0 = 0 if b == 0 else META + (b - 1) * P
        self.end = META if b == 0 else self.q0 + P
        if br == SWA and b > 2:
            self.ranges = [(0, META, 0), (self.q0 - P, 2 * P, META)]
            self.nk = DW
            tiles = [(0, 0), (b - 1, META), (b, META + P)]
        else:
            self.nk = self.end
            self.ranges = [(0, self.nk, 0)] if self.nk <= 512 else [(0, TH, 0), (TH, TH, TH)]
            tiles = [(t, 0 if t == 0 else META + (t - 1) * P) for t in range(b + 1)]
        self.base = 512 - TH if self.nk > 512 else 0
        n = len(tiles)
        cut = n if n <= 4 else 3
        self.parts = [tiles[:cut]] + ([tiles[cut:]] if cut < n else [])
        self.part_ids = []


def schedule():
    steps = []
    tiles = {"n": 0, "blocks": 0}
    units = []
    parts = {"n": 0}
    stats = {"n": 1}
    squares = {"n": 0, "mine": {}}

    def gemm(kind, m=0, stat=False):
        t = dict(kind=kind, m=m, g=tiles["n"], slot=None, stat=None)
        tiles["blocks"] += TILE_BLOCKS[kind]
        t["chunk"] = (tiles["blocks"] - 1) // BLK
        if stat:
            t["stat"] = stats["n"]
            stats["n"] += 1
        tiles["n"] += 1
        if kind == "mk" and m == HEADS - 1:
            tiles["blocks"] += 4
        if kind in SQUARED:
            ring = "k" if kind == "mk" else "a"
            mine = squares["mine"].setdefault(ring, [])
            t["sqn"], t["par"] = squares["n"], len(mine) % 2
            squares["n"] += 1
            mine.append(t)
            t["prev"] = mine[-3] if len(mine) > 2 else None
        return t

    def attention(br, fillers):
        us = []
        for b in range(QTILES - 1, -1, -1):
            for h in range(HEADS):
                u = Unit(len(units), br, b, h)
                units.append(u)
                us.append(u)
        fill = list(fillers)
        pending = []
        weights = [0.0]
        for u in us:
            weights.append(weights[-1] + 0.5 + u.nk / 264)
        done = 0
        for u in us[:2]:
            steps.append(("S", u))
            steps.append(("E", u))
        behind = []

        def product(j):
            u, p = behind.pop(0)
            steps.append(("PV", u, p))
            if p == len(u.parts) - 1 and u.h == HEADS - 1:
                steps.append(("O", u))
                pending.append((u, j))

        for j, u in enumerate(us):
            if j + 2 < len(us):
                steps.append(("S", us[j + 2]))
            want = min(len(fill), int(len(fill) * weights[j + 1] / weights[-1] / FILL_SPAN + 1e-9))
            for p in range(len(u.parts)):
                u.part_ids.append(parts["n"])
                parts["n"] += 1
                steps.append(("T", u, p))
                if p == len(u.parts) - 1 and j + 2 < len(us):
                    steps.append(("E", us[j + 2]))
                if done < want:
                    steps.append(("gemm", gemm(*fill[done])))
                    done += 1
                if behind:
                    product(j)
                behind.append((u, p))
            while done < want:
                steps.append(("gemm", gemm(*fill[done])))
                done += 1
            while pending and done == len(fill) and j >= pending[0][1] + OT_DELAY:
                steps.append(("OT", pending.pop(0)[0]))
        product(len(us))
        for u, _ in pending:
            steps.append(("OT", u))
        steps.append(("end", br))

    def project(kinds):
        late = []
        for t in kinds:
            if t["kind"] == "mv":
                while late:
                    steps.append(("stat", late.pop(0)))
            steps.append(("gemm", t))
            if late:
                steps.append(("stat", late.pop(0)))
            if t["stat"] is not None:
                late.append(t)
        for t in late:
            steps.append(("stat", t))

    def gate_branch(br):
        out = []
        for d in range(KD):
            out += [("g", (br, d)), ("y", (br, d))]
        return out

    project([gemm("ff"), gemm("fv")] + [gemm("fq", m, True) for m in range(4)]
            + [gemm("fk", m, True) for m in range(4)])
    attention(FOX, [])
    a = [gemm("cq", 0), gemm("cq", 1, True), gemm("ckv", 0, True), gemm("kr")]
    a[1]["tiles"], a[2]["tiles"] = a[0:2], a[2:3]
    a += [gemm("mv")]
    a += [gemm("mq", h, True) for h in range(HEADS)] + [gemm("mk", h, True) for h in range(HEADS)]
    project(a)
    attention(MLA, gate_branch(FOX))
    project([gemm("sv")] + [gemm("sq", m, True) for m in range(4)] + [gemm("sk", 0, True)])
    attention(SWA, gate_branch(MLA))
    for t in gate_branch(SWA):
        steps.append(("gemm", gemm(*t)))
    steps.append(("merged", None))
    inside = False
    ring = 0
    for s in steps:
        if s[0] == "S":
            inside = True
        elif s[0] == "end":
            inside = False
            ring = 0
        elif s[0] == "gemm":
            t = s[1]
            if t["kind"] in ("fv", "mv", "sv"):
                t["slot"] = (0, 1, 2)
            elif inside:
                t["slot"] = (2,)
            else:
                t["slot"] = (ring % 3,)
                ring += 1
    last = {}
    for s in steps:
        if s[0] == "gemm":
            t = s[1]
            t["after"] = sorted({last[x] for x in t["slot"] if x in last})
            for x in t["slot"]:
                last[x] = t["g"]
    order = {"free": 0, "qkv": 0, "tmd": KD, "sgd": 0, "gmd": 0}
    freed = {}

    def frees(t, name, by=1):
        order[name] += by
        freed[t["g"]] = (name, order[name])

    for s in steps:
        if s[0] == "gemm":
            t = s[1]
            if t["kind"] in ("ff", "kr"):
                frees(t, "free")
            elif t["kind"] in ("fv", "mv", "sv"):
                frees(t, "qkv")
            elif t["kind"] == "g":
                frees(t, "sgd")
            elif t["kind"] == "y":
                frees(t, "gmd")
        elif s[0] == "stat":
            t = s[1]
            if t["kind"] == "mq":
                frees(t, "free")
                order["qkv"] += 1
            elif t["kind"] in ("cq", "ckv"):
                for x in t["tiles"]:
                    frees(x, "tmd")
            else:
                frees(t, "qkv")
    for s in steps:
        if s[0] == "gemm":
            latest = {}
            for name, count in (freed[g] for g in s[1]["after"]):
                latest[name] = max(count, latest.get(name, 0))
            s[1]["after"] = list(latest.items())
    n_free = order["free"]
    return steps, units, tiles["n"], stats["n"], n_free


def build(nc, W, H, PRM, CST, DIST, OUT, counts):
    steps, units, n_tiles, n_stats, n_free = schedule()

    at = [(nc.sbuf_base + 63) // 64 * 64]

    def sb(name, shape, dt=F32, offset=None):
        size = int(np.prod(shape[1:])) * 4
        if offset is None:
            offset = at[0]
            at[0] += (size + 31) // 32 * 32
        t = nc.alloc_sbuf_tensor_at(name, shape, dt, offset=offset)
        return t

    h = sb("h", [P, KD, T])
    xh = sb("xh", [P, KD, T], F32R)
    xl = sb("xl", [P, KD, T], F32R)
    raw = sb("raw", [P, RAW, CW])
    wh = [sb(f"wh{i}", [P, CW], F32R) for i in range(SPLIT)]
    wl = [sb(f"wl{i}", [P, CW], F32R) for i in range(SPLIT)]
    attn_at = at[0]
    qt = sb("qt", [P, HEADS, T])
    kt = sb("kt", [P, HEADS, T])
    v = sb("v", [P, QTILES, HEADS * HD])
    oth = sb("oth", [P, BRANCH_TILES, T], F32R)
    otl = sb("otl", [P, BRANCH_TILES, T], F32R)
    merged_at = at[0]
    merged = sb("merged", [P, KD, T])
    merged_end = at[0]
    at[0] = merged_at
    fz, fa, fe, fl, fm, fs, ld, nld = (sb(f"dec{i}", [P, T]) for i in range(8))
    at[0] = merged_at
    lath = sb("lath", [P, 3, T], F32R)
    latl = sb("latl", [P, 3, T], F32R)
    at[0] = merged_end
    probs = sb("probs", [P, 2, T])
    pts = sb("pts", [P, 2, 512])
    osb = sb("osb", [P, QTILES, 512])
    gq = sb("gq", [P, T])
    krr = sb("krr", [P, T])
    ksq = sb("ksq", [P, 2, T])
    end_attn = at[0]
    at[0] = attn_at
    ah = sb("ah", [P, FT, T], F32R)
    al = sb("al", [P, FT, T], F32R)
    at[0] = max(at[0], end_attn)
    tmp_at = at[0]
    sq = sb("sq", [P, 2, T])
    guess = sb("guess", [P, 2, T])
    guess2 = probs
    negmean = sb("negmean", [P, 2, T])
    rstd = sb("rstd", [P, T])
    tmp = sb("tmp", [P, 2, T])
    end_tmp = at[0]
    at[0] = tmp_at
    cg = sb("cg", [P, 2, T])
    cv = sb("cv", [P, 2, T])
    si = sb("si", [P, 2, T])
    am = sb("am", [P, 2, T])
    at[0] = max(at[0], end_tmp)
    ssum = sb("ssum", [P, T])
    hsq = sq
    gsb = sq
    dist = kt[:, 2:4, :].rearrange("p a t -> p (a t)")
    cst = sb("cst", [P, CC_ALL])
    prm = sb("prm", [P, PC_ALL])
    gts = sb("gts", [P, 4])
    nmax = sb("nmax", [P, 2, HEADS])
    nraw = sb("nraw", [P, 2, HEADS])
    rsum = sb("rsum", [P, 2, HEADS])
    skx = sb("skx", [P, 2, HEADS])
    ske = sb("ske", [P, 2, HEADS])
    rtot = sb("rtot", [P, 2, HEADS])
    rinv = sb("rinv", [P, 2, HEADS])
    nsink = sb("nsink", [P, HEADS])
    assert at[0] <= nc.sbuf_usable_end, at[0]

    ps = [nc.alloc_psum_tensor(f"ps{i}", [P, 1024], F32) for i in range(4)]

    ident = cst[:, CC_ID:CC_ID + P]
    ones = cst[:, CC_ONE:CC_ONE + P]
    pair = cst[:, CC_PAIR:CC_PAIR + P]
    mask = cst[:, CC_MASK:CC_MASK + P]
    cs = cst[:, CC_CS:CC_CS + T]
    CENTRE = 512 - TH

    def full(slot):
        return ps[slot][:, CENTRE:CENTRE + T]

    def half(slot, j):
        return ps[slot][:, CENTRE + j * TH:CENTRE + (j + 1) * TH]

    def heads_bank(gi):
        return ps[2][:, (gi % 2) * 512:(gi % 2) * 512 + 512]

    def value_bank(tt):
        return ps[tt // 2][:, (tt % 2) * 512:(tt % 2) * 512 + 512]

    def S(name, before=0):
        s = Signal(nc, name, counts, before)
        signals.append(s)
        return s

    signals = []
    s_cst = nc.alloc_semaphore("constants_loaded")
    s_hin = nc.alloc_semaphore("input_loaded")
    s_prm = nc.alloc_semaphore("params_loaded")
    s_out = nc.alloc_semaphore("output_stored")
    s_raw = [nc.alloc_semaphore(f"chunk_loaded{i}") for i in range(RAW)]
    s_hi = nc.alloc_semaphore("chunk_high_part")
    s_w = nc.alloc_semaphore("chunk_split")
    s_start = nc.alloc_semaphore("chunk_started")
    s_ini = nc.alloc_semaphore("eps_set")
    s_dist = nc.alloc_semaphore("distances_loaded")
    mm = S("tile_ready")
    st = S("stat_ready")
    free = S("tile_freed")
    sqd = S("square_ready")
    guessd = S("rsqrt_guess_ready")
    rsd = S("rsqrt_ready")
    ssd = S("sum_squares_ready", KD)
    hsd = S("residual_square", KD)
    hup = S("residual_updated", KD)
    tmd = S("fp32_ready")
    thd = S("high_part_ready")
    xld = S("low_part_ready")
    sS = S("scores_ready")
    mxd = S("max_ready")
    pd = S("probs_ready")
    td = S("probs_transposed")
    ptd = S("transposed_copied")
    pvd = S("pv_done")
    skd = S("sink_sum")
    sed = S("sink_exp")
    ond = S("heads_normalised")
    otd = S("heads_transposed")
    ohd = S("head_high_part")
    old = S("head_low_part")
    f1 = S("decay_logit")
    f2 = S("decay_log1p")
    f3 = S("decay_summed")
    f4 = S("decay_rows_placed")
    krd = S("rope_key_squared")
    qkv = S("qkv_written")
    sgd = S("gate_ready")
    gmd = S("gate_used")
    cvd = S("conv_scaled")
    sid = S("silu_ready")
    ca = S("act_chain")
    cd = S("dve_chain")
    WO_TILES = KD
    UP_TILES = 2 * FT
    c_out = max(s[1]["chunk"] for s in steps if s[0] == "gemm") + 1
    g_wo, g_up = n_tiles, n_tiles + WO_TILES
    g_dn = g_up + UP_TILES

    group_of = {}
    groups = []
    for u in units:
        if u.h == 0:
            groups.append((u.br, u.b))
        group_of[(u.br, u.b)] = len(groups) - 1
    per_branch = QTILES
    qkv_end = {}
    n = 0
    for s in steps:
        if s[0] == "gemm" and s[1]["kind"] in ("fq", "fk", "fv", "mq", "mk", "mv", "sq", "sk", "sv"):
            n += 1
        if s[0] == "end":
            qkv_end[s[1]] = n
    parts_end = {}
    for u in units:
        parts_end[u.br] = max(parts_end.get(u.br, 0), max(u.part_ids) + 1)
    stat_norm = (0, n_stats)
    split_norm = (0, SP_NORM2)
    last_y, stat_of = {}, {}
    for s in steps:
        if s[0] == "stat":
            for x in s[1].get("tiles", [s[1]]):
                stat_of[x["g"]] = s[1]["stat"]
    for s in steps:
        if s[0] == "gemm" and s[1]["kind"] == "y":
            last_y[s[1]["m"][0]] = s[1]["g"]
    by_name = {"free": free, "qkv": qkv, "tmd": tmd, "sgd": sgd, "gmd": gmd}

    def tile_of(t, i):
        if isinstance(i, int):
            return t[:, i, :]
        return t[:, bass.ds(i, 1), :].rearrange("p a t -> p (a t)")


    block = nc.Block()
    with block as blk:

        @blk.sync
        def _(sp):
            def load(n, s):
                sp.dma_start(raw[:, s, :], W[n, :, :]).then_inc(s_raw[s], 16)

            for k in range(0, KD, 4):
                sp.dma_start(h[:, k:k + 4, :], H[:, k:k + 4, :]).then_inc(s_hin, 16)
            sp.dma_start(cst[:, :], CST[:, :]).then_inc(s_cst, 16)
            for s in range(RAW):
                load(s, s)
            with sp.Fori(RAW, DEPTH * CHUNKS + AHEAD - RAW + 1, RAW) as n:
                for s in range(RAW):
                    sp.wait_ge(s_w, n + (s + 1 - RAW))
                    load(n + s, s)
            for k in range(KD):
                sp.wait_ge(hup.sem, hup.at(DEPTH - 1, WO_TILES + k + 1))
                sp.dma_start(OUT[:, k, :], h[:, k, META:T]).then_inc(s_out, 16)
            sp.wait_ge(s_out, 16 * KD)

        @blk.gpsimd
        def _(pool):
            with pool.Fori(0, DEPTH * CHUNKS - SPLIT + 1, SPLIT) as n:
                for s in range(SPLIT):
                    pool.wait_ge(s_hi, n + (s + 1))
                    nc.gpsimd.tensor_tensor(wl[s][:, :], raw[:, s % RAW, :], wh[s][:, :].bitcast(F32),
                                            ALU.subtract).then_inc(s_w, 1)

        @blk.scalar
        def _(act):
            def split_high(l, count, out, in_):
                act.wait_ge(tmd.sem, tmd.at(l, count))
                nc.scalar.activation(out, in_, ACT.Copy).then_inc(thd.sem, thd.tick())

            def rsqrt_guess(l, n, stat):
                act.wait_ge(st.sem, st.at(l, stat + 1))
                if stat > 1:
                    act.wait_ge(rsd.sem, rsd.at(l, stat - 1))
                s_ = stat % 2
                nc.scalar.activation(guess[:, s_, :], full(3), ACT.Abs_reciprocal_sqrt,
                                     scale=1.0 / n, bias=gts[:, 2:3]).then_inc(ca.sem, ca.tick())
                nc.scalar.activation(negmean[:, s_, :], full(3), ACT.Identity, scale=-1.0 / n, bias=gts[:, 3:4])
                act.wait_ge(ca.sem, ca.at(l, ca.n))
                nc.scalar.activation(guess2[:, s_, :], guess[:, s_, :], ACT.Square).then_inc(guessd.sem, guessd.tick())

            act.dma_start(prm[:, :], PRM[0, :, :]).then_inc(s_prm, 16)
            act.wait_ge(s_hin, 16 * (KD // 4))
            act.wait_ge(s_ini, 1)
            for k in range(KD):
                if k >= 2:
                    act.wait_ge(ssd.sem, k - 1)
                nc.scalar.activation(hsq[:, k % 2, :], h[:, k, :], ACT.Square).then_inc(hsd.sem, 1)
            with act.Fori(0, DEPTH) as l:

                def norm_input(which):
                    rsqrt_guess(l, D, stat_norm[which])
                    for k in range(KD):
                        split_high(l, split_norm[which] + k + 1, xh[:, k, :], tmp[:, k % 2, :])

                def attn(s):
                    kind, u = s[0], s[1]
                    if kind == "E":
                        act.wait_ge(mxd.sem, mxd.at(l, u.i + 1))
                        if u.i >= 2:
                            act.wait_ge(td.sem, td.at(l, units[u.i - 2].part_ids[-1] + 1))
                        nc.scalar.activation(
                            probs[0:u.nq, u.i % 2, 0:u.nk], ps[u.i % 2][0:u.nq, u.base:u.base + u.nk], ACT.Exp,
                            bias=nmax[0:u.nq, group_of[(u.br, u.b)] % 2, u.h:u.h + 1],
                            accum_out=rsum[0:u.nq, group_of[(u.br, u.b)] % 2, u.h:u.h + 1]).then_inc(pd.sem, pd.tick())
                    elif kind == "T":
                        i = u.part_ids[s[2]]
                        act.wait_ge(td.sem, td.at(l, i + 1))
                        if i >= 2:
                            act.wait_ge(pvd.sem, pvd.at(l, i - 1))
                        w = len(u.parts[s[2]]) * u.nq
                        nc.scalar.activation(pts[:, i % 2, 0:w], ps[3][:, 512:512 + w], ACT.Copy).then_inc(ptd.sem, ptd.tick())
                    elif kind == "O":
                        gi = group_of[(u.br, u.b)]
                        if u.br == SWA:
                            act.wait_ge(skd.sem, skd.at(l, sed.n + 1))
                            nc.scalar.activation(ske[:, gi % 2, :], skx[:, gi % 2, :], ACT.Exp).then_inc(sed.sem, sed.tick())
                    elif kind == "OT":
                        gi = group_of[(u.br, u.b)]
                        act.wait_ge(otd.sem, otd.at(l, gi + 1))
                        if u.b == QTILES - 1 and u.br != FOX:
                            act.wait_ge(mm.sem, mm.at(l, last_y[u.br - 1] + 1))
                        src = heads_bank(gi)[:, :].rearrange("p (c q) -> p c q", c=BRANCH_TILES)[:, :, 0:u.end - u.q0]
                        nc.scalar.activation(oth[:, :, u.q0:u.end], src, ACT.Copy).then_inc(ohd.sem, ohd.tick())

                norm_input(0)
                for s in steps:
                    if s[0] in ("E", "T", "O", "OT"):
                        attn(s)
                    elif s[0] == "end" and s[1] == MLA:
                        act.wait_ge(pvd.sem, pvd.at(l, parts_end[MLA]))
                        act.dma_start(dist[:, 0:DIST_AT[-1]], DIST[:, :]).then_inc(s_dist, 16)
                    elif s[0] == "merged":
                        for k in range(KD):
                            split_high(l, SP_MERGED + k + 1, xh[:, k, :], merged[:, k, :])
                    elif s[0] == "stat":
                        t = s[1]
                        rsqrt_guess(l, MEAN_OF[t["kind"]], t["stat"])
                        if t["kind"] == "cq":
                            for k in range(2):
                                split_high(l, SP_CQ + k + 1, lath[:, k, :], tmp[:, k, :])
                        if t["kind"] == "ckv":
                            split_high(l, SP_CQ + 3, lath[:, 2, :], tmp[:, 0, :])
                    elif s[0] == "gemm":
                        t = s[1]
                        k = t["kind"]
                        src = full(t["slot"][0])
                        if k in SQUARED:
                            rows = SQUARED[k]
                            if t["prev"] is not None:
                                act.wait_ge(st.sem, st.at(l, stat_of[t["prev"]["g"]] + 1))
                            act.wait_ge(mm.sem, mm.at(l, t["g"] + 1))
                            dst = ksq if k == "mk" else sq
                            nc.scalar.activation(dst[0:rows, t["par"], :], src[0:rows, :], ACT.Square).then_inc(sqd.sem, sqd.tick())
                        elif k == "ff":
                            act.wait_ge(f1.sem, f1.at(l, 1))
                            nc.scalar.activation(fa[0:8, :], fz[0:8, :], ACT.Abs).then_inc(ca.sem, ca.tick())
                            act.wait_ge(ca.sem, ca.at(l, ca.n))
                            nc.scalar.activation(fe[0:8, :], fa[0:8, :], ACT.Exp, scale=-1.0).then_inc(ca.sem, ca.tick())
                            act.wait_ge(ca.sem, ca.at(l, ca.n))
                            nc.scalar.activation(fl[0:8, :], fe[0:8, :], ACT.Ln, bias=1.0).then_inc(f2.sem, f2.tick())
                        elif k == "fv":
                            act.wait_ge(f3.sem, f3.at(l, 1))
                            for dst, row, src in ((qt, HD, ld), (kt, HD + 1, nld)):
                                act.dma_start(dst[row:row + 1, :, :], src[0:8, :]).then_inc(f4.sem, f4.tick(16))
                        elif k == "kr":
                            act.wait_ge(mm.sem, mm.at(l, t["g"] + 1))
                            for j in range(2):
                                nc.scalar.activation(ksq[HD:MQ, j, :], src[HD:MQ, :], ACT.Square).then_inc(krd.sem, krd.tick())
                        elif k == "g":
                            act.wait_ge(mm.sem, mm.at(l, t["g"] + 1))
                            i = sgd.n
                            if i >= 2:
                                act.wait_ge(gmd.sem, gmd.at(l, i - 1))
                            nc.scalar.activation(gsb[:, i % 2, :], src, ACT.Tanh, scale=0.5).then_inc(sgd.sem, sgd.tick())

                def square_residual(base, i, par):
                    act.wait_ge(hup.sem, hup.at(l, i + (base + 1)))
                    act.wait_ge(ssd.sem, ssd.at(l, i + (base - 1)))
                    nc.scalar.activation(hsq[:, par, :], tile_of(h, i), ACT.Square).then_inc(hsd.sem, hsd.tick())

                with act.Fori(0, WO_TILES - 3, 4) as m:
                    for j in range(4):
                        square_residual(0, m + j, j % 2)
                hsd.skip(WO_TILES - 4)
                norm_input(1)
                with act.Fori(0, FT - 1, 2) as f:
                    for j in range(2):
                        for side, dst in ((0, cg), (1, cv)):
                            act.wait_ge(mm.sem, mm.at(l, f * 2 + (g_up + 2 * j + side + 1)))
                            cw = f * 3 + (PC_CW + 3 * (side * FT + j))
                            nc.scalar.activation(
                                dst[:, j, :], full(2 * j + side), ACT.Identity,
                                scale=prm[:, bass.ds(cw + 2, 1)], bias=prm[:, bass.ds(f + (PC_CB + side * FT + j), 1)]).then_inc(cvd.sem, cvd.tick())
                        act.wait_ge(free.sem, free.at(l, f * 2 + (n_free + 2 * j + 1)))
                        nc.scalar.activation(si[:, j, :], cg[:, j, :], ACT.Silu).then_inc(sid.sem, sid.tick())
                        split_high(l, f + (SP_FFN + j + 1), tile_of(ah, f + j), am[:, j, :])
                for s_, n_ in ((cvd, 4), (sid, 2), (thd, 2)):
                    s_.skip(n_ * (FT // 2 - 1))
                act.wait_ge(xld.sem, xld.at(l, SP_FFN + FT))
                act.dma_start(prm[:, :], PRM[l + 1, :, :]).then_inc(s_prm, 16)
                with act.Fori(0, KD - 3, 4) as m:
                    for j in range(4):
                        square_residual(WO_TILES, m + j, j % 2)
                hsd.skip(KD - 4)
            act.wait_ge(s_prm, 16 * (DEPTH + 1))

        @blk.tensor
        def _(pe):
            pe.sem_inc(s_start, STARTED_BEFORE)
            pe.wait_ge(s_cst, 16)
            with pe.Fori(0, DEPTH) as l:
                cur = {"b": 0}

                def block_at(c, i, chunk_no):
                    if i == 0:
                        pe.wait_ge(s_w, chunk_no + 1)
                        cur["fresh"] = True
                    a = i * P
                    return wh[c][:, a:a + P], wl[c][:, a:a + P]

                def issued(ins):
                    if cur.get("fresh"):
                        ins.then_inc(s_start, 1)
                        cur["fresh"] = False

                def take():
                    b = cur["b"]
                    cur["b"] += 1
                    c = b // BLK
                    return block_at(c % SPLIT, b % BLK, l * CHUNKS + c)

                def take_padded():
                    if cur["b"] % BLK == BLK // 2:
                        cur["b"] += BLK // 2
                    return take()

                def rows_out(slot, blocks, xhi, xlo, nk):
                    ins = None
                    for k in range(nk):
                        a_hi, a_lo = blocks()
                        for j in range(2):
                            sl = slice(j * TH, (j + 1) * TH)
                            a = nc.tensor.matmul(half(slot, j), a_hi, xhi(k)[:, sl], start=(k == 0), stop=False)
                            issued(a)
                            nc.tensor.matmul(half(slot, j), a_hi, xlo(k)[:, sl], start=False, stop=False)
                        for j in range(2):
                            sl = slice(j * TH, (j + 1) * TH)
                            ins = nc.tensor.matmul(half(slot, j), a_lo, xhi(k)[:, sl], start=False, stop=(k == nk - 1))
                    return ins

                def tok(tt):
                    return slice(0, P) if tt == 0 else slice(META + (tt - 1) * P, META + tt * P)

                def tokens_out(xhi, xlo, nk, width):
                    ins = None
                    for k in range(nk):
                        nb_ = width // P
                        first = take()
                        b0 = cur["b"] - 1
                        for _ in range(nb_ - 1):
                            cur["b"] += 1
                        c = (b0 // BLK) % SPLIT
                        a = (b0 % BLK) * P
                        whi, wlo = wh[c][:, a:a + width], wl[c][:, a:a + width]
                        for tt in range(QTILES):
                            o = value_bank(tt)[:, 0:width]
                            i0 = nc.tensor.matmul(o, xhi(k)[:, tok(tt)], whi, start=(k == 0), stop=False)
                            issued(i0)
                            nc.tensor.matmul(o, xhi(k)[:, tok(tt)], wlo, start=False, stop=False)
                            ins = nc.tensor.matmul(o, xlo(k)[:, tok(tt)], whi, start=False, stop=(k == nk - 1))
                    return ins

                def xk(t):
                    return lambda k: t[:, k, :]

                def stat(rhs, lhs, rows, first=True, last=True):
                    for j in range(2):
                        ins = nc.tensor.matmul(half(3, j), lhs[0:rows, :], rhs[0:rows, j * TH:(j + 1) * TH],
                                               start=first, stop=last)
                    return ins

                def norm_stat(which):
                    pe.wait_ge(ssd.sem, ssd.at(l, KD * which))
                    stat(ssum, ones, P).then_inc(st.sem, st.tick())

                last_bank3 = {"v": None}

                def bank3_free():
                    if last_bank3["v"]:
                        pe.wait_ge(last_bank3["v"][0].sem, last_bank3["v"][0].at(l, last_bank3["v"][1]))

                norm_stat(0)

                def x_ready(base):
                    seen = set()

                    def get(t):
                        def f(k):
                            if k not in seen:
                                seen.add(k)
                                pe.wait_ge(xld.sem, xld.at(l, base + k + 1))
                            return t[:, k, :]
                        return f
                    return get

                norm_x = x_ready(split_norm[0])
                for s in steps:
                    if s[0] == "gemm":
                        t = s[1]
                        kind = t["kind"]
                        for name, count in t["after"]:
                            pe.wait_ge(by_name[name].sem, by_name[name].at(l, count))
                        slot = t["slot"][0]
                        if kind == "ff":
                            rows_out(slot, take_padded, norm_x(xh), norm_x(xl), KD).then_inc(mm.sem, mm.tick())
                            cur["b"] += BLK // 2
                        elif kind in ("fq", "fk", "cq", "ckv", "kr", "sq", "sk", "g"):
                            rows_out(slot, take, xk(xh), xk(xl), KD).then_inc(mm.sem, mm.tick())
                        elif kind == "mq":
                            if t["m"] == 0:
                                pe.wait_ge(xld.sem, xld.at(l, SP_CQ + 2))
                            rows_out(slot, take, xk(lath), xk(latl), 2).then_inc(mm.sem, mm.tick())
                        elif kind == "mk":
                            if t["m"] == 0:
                                pe.wait_ge(xld.sem, xld.at(l, SP_CQ + 3))
                            rows_out(slot, take, lambda k: lath[:, 2, :], lambda k: latl[:, 2, :], 1).then_inc(mm.sem, mm.tick())
                            if t["m"] == HEADS - 1:
                                cur["b"] += 4
                        elif kind in ("fv", "sv"):
                            tokens_out(xk(xh), xk(xl), KD, 512 if kind == "fv" else P).then_inc(mm.sem, mm.tick())
                        elif kind == "mv":
                            pe.wait_ge(xld.sem, xld.at(l, SP_CQ + 3))
                            tokens_out(lambda k: lath[:, 2, :], lambda k: latl[:, 2, :], 1, 512).then_inc(mm.sem, mm.tick())
                        elif kind == "y":
                            if t["m"][1] == 0:
                                pe.wait_ge(old.sem, old.at(l, QTILES * (t["m"][0] + 1)))
                            rows_out(slot, take, xk(oth), xk(otl), BRANCH_TILES).then_inc(mm.sem, mm.tick())
                    elif s[0] == "stat":
                        t = s[1]
                        kind = t["kind"]
                        i = t["stat"]
                        pe.wait_ge(guessd.sem, guessd.at(l, i))
                        pe.wait_ge(sqd.sem, sqd.at(l, t["sqn"] + 1))
                        if kind == "cq":
                            stat(sq[:, 1 - t["par"], :], ones, P, True, False)
                            stat(sq[:, t["par"], :], ones, P, False, True).then_inc(st.sem, st.tick())
                        elif kind == "mk":
                            stat(ksq[:, t["par"], :], ones, MQ).then_inc(st.sem, st.tick())
                        elif kind == "mq":
                            stat(sq[:, t["par"], :], ones, MQ).then_inc(st.sem, st.tick())
                        elif kind == "ckv":
                            stat(sq[:, t["par"], :], ones, P).then_inc(st.sem, st.tick())
                        else:
                            stat(sq[:, t["par"], :], pair, P).then_inc(st.sem, st.tick())
                    elif s[0] == "S":
                        u = s[1]
                        if u.h == 0 and u.b == QTILES - 1:
                            pe.wait_ge(qkv.sem, qkv.at(l, qkv_end[u.br]))
                            if u.br == FOX:
                                pe.wait_ge(f4.sem, f4.at(l, 32))
                        if u.i >= 2:
                            pe.wait_ge(pd.sem, pd.at(l, u.i - 1))
                        rows = {FOX: HD + 2, MLA: P, SWA: HD}[u.br]
                        kh = u.h // 4 if u.br == SWA else u.h
                        for k0, kn, col in u.ranges:
                            ins = nc.tensor.matmul(ps[u.i % 2][0:u.nq, u.base + col:u.base + col + kn],
                                                   qt[0:rows, u.h, u.q0:u.q0 + P], kt[0:rows, kh, k0:k0 + kn],
                                                   start=True, stop=True)
                        ins.then_inc(sS.sem, sS.tick())
                    elif s[0] == "T":
                        u, p = s[1], s[2]
                        i = u.part_ids[p]
                        pe.wait_ge(pd.sem, pd.at(l, u.i + 1))
                        bank3_free()
                        for j, (kt_i, col) in enumerate(u.parts[p]):
                            ins = nc.tensor.transpose(ps[3][:, 512 + j * P:512 + (j + 1) * P],
                                                      probs[:, u.i % 2, col:col + P],
                                                      ident[0:u.nq, 0:u.nq])
                        ins.then_inc(td.sem, td.tick())
                        last_bank3["v"] = (ptd, i + 1)
                    elif s[0] == "PV":
                        u, p = s[1], s[2]
                        i = u.part_ids[p]
                        pe.wait_ge(ptd.sem, ptd.at(l, i + 1))
                        gi = group_of[(u.br, u.b)]
                        if p == 0 and u.h == 0 and gi > 0:
                            pe.wait_ge(ond.sem, ond.at(l, gi))
                        vh = u.h // 4 if u.br == SWA else u.h
                        for j, (kt_i, col) in enumerate(u.parts[p]):
                            kn = META if kt_i == 0 else P
                            first = p == 0 and j == 0
                            final = p == len(u.parts) - 1 and j == len(u.parts[p]) - 1
                            ins = nc.tensor.matmul(ps[3][0:u.nq, u.h * HD:(u.h + 1) * HD],
                                                   pts[0:kn, i % 2, j * u.nq:(j + 1) * u.nq],
                                                   v[0:kn, kt_i, vh * HD:(vh + 1) * HD], start=first, stop=final)
                        ins.then_inc(pvd.sem, pvd.tick())
                    elif s[0] == "OT":
                        u = s[1]
                        gi = group_of[(u.br, u.b)]
                        pe.wait_ge(ond.sem, ond.at(l, gi + 1))
                        if u.b < QTILES - 2:
                            pe.wait_ge(old.sem, old.at(l, gi - 1))
                        elif u.b == QTILES - 1 and u.br != FOX:
                            pe.wait_ge(gmd.sem, gmd.at(l, KD * u.br))
                        for c in range(BRANCH_TILES):
                            ins = nc.tensor.transpose(heads_bank(gi)[:, c * P:c * P + u.nq],
                                                      osb[0:u.nq, u.b, c * P:(c + 1) * P], ident[0:u.nq, 0:u.nq])
                        ins.then_inc(otd.sem, otd.tick())
                    elif s[0] == "end":
                        pe.wait_ge(pd.sem, pd.at(l, max(u.i for u in units if u.br == s[1]) + 1))
                        pe.wait_ge(old.sem, old.at(l, QTILES * (s[1] + 1)))
                c0 = cur["b"] // BLK
                assert cur["b"] % BLK == 0

                def loop_tile(n, c, first_chunk, slot, x_hi, x_lo, nk, start_chunk):
                    pos = {"b": 0}

                    def blocks():
                        b = pos["b"]
                        pos["b"] += 1
                        cc = c + b // BLK
                        return block_at(cc % SPLIT, b % BLK, n + (start_chunk + cc))
                    return rows_out(slot, blocks, x_hi, x_lo, nk)

                assert c0 % SPLIT == 0, c0
                xw = {"done": False}
                with pe.Fori(0, WO_TILES - 3, 4) as m:
                    nbase = pe.snap(l * CHUNKS + m)
                    for j in range(4):
                        if j == 0:
                            pe.wait_ge(xld.sem, xld.at(l, SP_MERGED + KD))
                        pe.wait_ge(hup.sem, hup.at(l, m + (j - 3)))
                        loop_tile(nbase, j, 0, j, xk(xh), xk(xl), KD, c0).then_inc(mm.sem, mm.tick())
                mm.skip(WO_TILES - 4)
                norm_stat(1)
                c_up = c0 + KD
                with pe.Fori(0, FT - 1, 2) as f:
                    nbase = pe.snap(l * CHUNKS + f * 2)
                    pe.wait_ge(xld.sem, xld.at(l, split_norm[1] + KD))
                    for j in range(4):
                        pe.wait_ge(free.sem, free.at(l, f * 2 + (n_free + j - 3)))
                        loop_tile(nbase, j, 0, j, xk(xh), xk(xl), KD, c_up).then_inc(mm.sem, mm.tick())
                mm.skip(UP_TILES - 4)
                c_dn = c_up + 2 * FT
                with pe.Fori(0, KD - 3, 4) as m:
                    nbase = pe.snap(l * CHUNKS + m * 3)
                    pe.wait_ge(xld.sem, xld.at(l, SP_FFN + FT))
                    for j in range(4):
                        pe.wait_ge(hup.sem, hup.at(l, m + (WO_TILES + j - 3)))
                        loop_tile(nbase, 3 * j, 0, j, xk(ah), xk(al), FT, c_dn).then_inc(mm.sem, mm.tick())
                mm.skip(KD - 4)
                assert c_dn + 3 * KD == CHUNKS

        @blk.vector
        def _(dve):
            def high_part(base, c):
                dve.wait_ge(s_raw[c % RAW], base * (16 // RAW) + 16 * (c // RAW + 1))
                if c >= AHEAD:
                    dve.wait_ge(s_start, base + (c + 2 - SPLIT + STARTED_BEFORE))
                nc.vector.tensor_copy(wh[c % SPLIT][:, :], raw[:, c % RAW, :]).then_inc(s_hi, 1)

            nc.vector.memset(gts[:, 2:3], EPS)
            nc.vector.memset(gts[:, 3:4], -EPS).then_inc(s_ini, 1)
            for n in range(AHEAD):
                high_part(0, n)
            dve.wait_ge(s_hin, 16 * (KD // 4))
            dve.sem_inc(hup.sem, KD)
            for k in range(KD):
                dve.wait_ge(hsd.sem, k + 1)
                if k == 0:
                    nc.vector.tensor_copy(ssum[:, :], hsq[:, 0, :]).then_inc(ssd.sem, 1)
                else:
                    dve.wait_ge(ssd.sem, k)
                    nc.vector.tensor_tensor(ssum[:, :], ssum[:, :], hsq[:, k % 2, :], ALU.add).then_inc(ssd.sem, 1)
            dve.wait_ge(s_cst, 16)
            with dve.Fori(0, DEPTH) as l:

                rstd_used = []
                split = {"next": AHEAD}

                def split_to(c):
                    for n in range(split["next"], c + AHEAD + 1):
                        high_part(l * CHUNKS, n)
                    split["next"] = max(split["next"], c + AHEAD + 1)

                def newton(stat):
                    dve.wait_ge(guessd.sem, guessd.at(l, stat + 1))
                    s_ = stat % 2
                    nc.vector.scalar_tensor_tensor(
                        out=negmean[:, s_, :], in0=negmean[:, s_, :], scalar=0.5, in1=guess2[:, s_, :],
                        op0=ALU.mult, op1=ALU.mult).then_inc(cd.sem, cd.tick())
                    dve.wait_ge(cd.sem, cd.at(l, cd.n))
                    for used in rstd_used:
                        dve.wait_ge(used.sem, used.at(l, used.n))
                    rstd_used.clear()
                    nc.vector.scalar_tensor_tensor(
                        out=rstd[:, :], in0=negmean[:, s_, :], scalar=1.5, in1=guess[:, s_, :],
                        op0=ALU.add, op1=ALU.mult).then_inc(rsd.sem, rsd.tick())
                    dve.wait_ge(rsd.sem, rsd.at(l, rsd.n))

                def low(out, hi, tile):
                    dve.wait_ge(thd.sem, thd.at(l, xld.n + 1))
                    return nc.vector.tensor_tensor(out, tile, hi.bitcast(F32), ALU.subtract).then_inc(xld.sem, xld.tick())

                def norm_input(which):
                    dve.wait_ge(guessd.sem, guessd.at(l, stat_norm[which] + 1))
                    nc.vector.memset(ssum[:, :], 0.0)
                    newton(stat_norm[which])
                    rstd_used.append(tmd)
                    assert tmd.n == split_norm[which]
                    pc = PC_N1 if which == 0 else PC_N2

                    def scale(k):
                        if k >= 2:
                            dve.wait_ge(xld.sem, xld.at(l, split_norm[which] + k - 1))
                        nc.vector.scalar_tensor_tensor(
                            out=tmp[:, k % 2, :], in0=h[:, k, :], scalar=prm[:, pc + k:pc + k + 1],
                            in1=rstd[:, :], op0=ALU.mult, op1=ALU.mult).then_inc(tmd.sem, tmd.tick())
                    scale(0)
                    for k in range(KD):
                        if k + 1 < KD:
                            scale(k + 1)
                        low(xl[:, k, :], xh[:, k, :], tmp[:, k % 2, :])

                dve.wait_ge(s_prm, l * 16 + 16)
                dve.wait_ge(s_ini, 1)
                nc.vector.tensor_scalar(gts[:, 0:1], prm[:, PC_FQ:PC_FQ + 1], HD ** -0.5, None, ALU.mult)
                nc.vector.tensor_scalar(gts[:, 1:2], prm[:, PC_SQ:PC_SQ + 1], HD ** -0.5, None, ALU.mult)
                nc.vector.tensor_scalar(nsink[:, :], prm[:, PC_SINK:PC_SINK + HEADS], -1.0, None, ALU.mult).then_inc(cd.sem, cd.tick())
                dve.wait_ge(cd.sem, cd.at(l, cd.n))
                norm_input(0)
                for s in steps:
                    if s[0] == "stat":
                        t = s[1]
                        kind = t["kind"]
                        src = full(t["slot"][0])
                        newton(t["stat"])
                        rstd_used.append(tmd if kind in ("cq", "ckv") else qkv)
                        if kind in ("fq", "fk", "sq", "sk"):
                            dst = qt if kind in ("fq", "sq") else kt
                            g = {"fq": gts[:, 0:1], "sq": gts[:, 1:2], "fk": prm[:, PC_FK:PC_FK + 1],
                                 "sk": prm[:, PC_SK:PC_SK + 1]}[kind]
                            for e in range(2):
                                r = slice(e * HD, (e + 1) * HD)
                                ins = nc.vector.scalar_tensor_tensor(
                                    out=dst[0:HD, 2 * t["m"] + e, :], in0=src[r, :], scalar=g[r, :],
                                    in1=rstd[r, :], op0=ALU.mult, op1=ALU.mult)
                            ins.then_inc(qkv.sem, qkv.tick())
                        elif kind == "cq":
                            for k in range(2):
                                t_ = t["tiles"][k]
                                nc.vector.scalar_tensor_tensor(
                                    out=tmp[:, k, :], in0=full(t_["slot"][0]),
                                    scalar=prm[:, PC_QA + k:PC_QA + k + 1], in1=rstd[:, :],
                                    op0=ALU.mult, op1=ALU.mult).then_inc(tmd.sem, tmd.tick())
                            for k in range(2):
                                low(latl[:, k, :], lath[:, k, :], tmp[:, k, :])
                        elif kind == "ckv":
                            dve.wait_ge(xld.sem, xld.at(l, xld.n))
                            nc.vector.scalar_tensor_tensor(
                                out=tmp[:, 0, :], in0=src, scalar=prm[:, PC_KVA:PC_KVA + 1], in1=rstd[:, :],
                                op0=ALU.mult, op1=ALU.mult).then_inc(tmd.sem, tmd.tick())
                            low(latl[:, 2, :], lath[:, 2, :], tmp[:, 0, :])
                        elif kind == "mq":
                            nc.vector.tensor_tensor(tmp[:, t["m"] % 2, :], src, gq[:, :],
                                                                               ALU.mult).then_inc(free.sem, free.tick())
                            dve.wait_ge(free.sem, free.at(l, free.n))
                            nc.vector.tensor_tensor(qt[:, t["m"], :], tmp[:, t["m"] % 2, :], rstd[:, :],
                                                            ALU.mult).then_inc(qkv.sem, qkv.tick())
                        elif kind == "mk":
                            nc.vector.tensor_tensor(kt[HD:P, t["m"], :], krr[HD:P, :], rstd[HD:P, :], ALU.mult)
                            nc.vector.scalar_tensor_tensor(
                                out=kt[0:HD, t["m"], :], in0=src[0:HD, :], scalar=prm[0:HD, PC_MK:PC_MK + 1],
                                in1=rstd[0:HD, :], op0=ALU.mult, op1=ALU.mult).then_inc(qkv.sem, qkv.tick())
                    elif s[0] == "gemm":
                        t = s[1]
                        kind = t["kind"]
                        src = full(t["slot"][0])
                        split_to(t["chunk"])
                        if kind == "ff":
                            dve.wait_ge(mm.sem, mm.at(l, t["g"] + 1))
                            nc.vector.tensor_scalar(fz[0:8, :], src[0:8, :], prm[0:8, PC_FB:PC_FB + 1], None,
                                                             ALU.add).then_inc(free.sem, free.tick())
                            dve.wait_ge(free.sem, free.at(l, free.n))
                            nc.vector.tensor_scalar(fm[0:8, :], fz[0:8, :], 0.0, None, ALU.min).then_inc(f1.sem, f1.tick())
                            dve.wait_ge(f2.sem, f2.at(l, 1))
                            dve.wait_ge(f1.sem, f1.at(l, 1))
                            nc.vector.tensor_tensor(fs[0:8, :], fm[0:8, :], fl[0:8, :], ALU.subtract).then_inc(cd.sem, cd.tick())
                            dve.wait_ge(cd.sem, cd.at(l, cd.n))
                            nc.vector.tensor_tensor_scan(ld[0:8, :], cs[0:8, :], fs[0:8, :], 0.0,
                                                                 ALU.mult, ALU.add).then_inc(cd.sem, cd.tick())
                            dve.wait_ge(cd.sem, cd.at(l, cd.n))
                            nc.vector.tensor_scalar(nld[0:8, :], ld[0:8, :], -1.0, None, ALU.mult).then_inc(cd.sem, cd.tick())
                            dve.wait_ge(cd.sem, cd.at(l, cd.n))
                            nc.vector.memset(qt[HD:HD + 2, :, :], 1.0)
                            nc.vector.memset(kt[HD:HD + 2, :, :], 1.0).then_inc(f3.sem, f3.tick())
                        elif kind in ("fv", "mv", "sv"):
                            width = P if kind == "sv" else HEADS * HD
                            dve.wait_ge(mm.sem, mm.at(l, t["g"] + 1))
                            for tt in range(QTILES):
                                rows = META if tt == 0 else P
                                ins = nc.vector.tensor_copy(v[0:rows, tt, 0:width], value_bank(tt)[0:rows, 0:width])
                            ins.then_inc(qkv.sem, qkv.tick())
                        elif kind == "kr":
                            dve.wait_ge(mm.sem, mm.at(l, t["g"] + 1))
                            gk = tmp[:, 1, :]
                            dve.wait_ge(xld.sem, xld.at(l, xld.n))
                            nc.vector.tensor_scalar(gq[:, :], cs, prm[:, PC_MQ:PC_MQ + 1], MQ ** -0.5,
                                                    ALU.mult, ALU.mult)
                            nc.vector.tensor_scalar(gk, cs, prm[:, PC_MK:PC_MK + 1], None, ALU.mult).then_inc(cd.sem, cd.tick())
                            dve.wait_ge(cd.sem, cd.at(l, cd.n))
                            t1, t2 = merged[:, 6, :], rstd
                            dve.wait_ge(krd.sem, krd.at(l, 2))
                            nc.vector.tensor_tensor(t1[HD:MQ, :], src[HD:MQ, :], gk[HD:MQ, :], ALU.mult)
                            nc.vector.tensor_tensor(t2[HD:MQ, :], src[MQ:P, :], gk[MQ:P, :], ALU.mult).then_inc(cd.sem, cd.tick())
                            dve.wait_ge(cd.sem, cd.at(l, cd.n))
                            nc.vector.tensor_tensor(krr[HD:MQ, :], t1[HD:MQ, :], t2[HD:MQ, :], ALU.add)
                            nc.vector.tensor_tensor(krr[MQ:P, :], t1[HD:MQ, :],
                                                                               t2[HD:MQ, :], ALU.add).then_inc(free.sem, free.tick())
                            dve.wait_ge(free.sem, free.at(l, free.n))
                        elif kind == "y":
                            br, d = t["m"]
                            dve.wait_ge(mm.sem, mm.at(l, t["g"] + 1))
                            dve.wait_ge(sgd.sem, sgd.at(l, gmd.n + 1))
                            gate = gsb[:, gmd.n % 2, :]
                            dst = merged[:, d, :] if br == FOX else tmp[:, d % 2, :]
                            nc.vector.scalar_tensor_tensor(out=dst, in0=gate, scalar=1.0, in1=src,
                                                                   op0=ALU.add, op1=ALU.mult).then_inc(gmd.sem, gmd.tick())
                            if br != FOX:
                                dve.wait_ge(gmd.sem, gmd.at(l, gmd.n))
                                ins = nc.vector.tensor_tensor(merged[:, d, :], merged[:, d, :], tmp[:, d % 2, :],
                                                              ALU.add)
                                if br == MLA:
                                    ins.then_inc(cd.sem, cd.tick())
                                    dve.wait_ge(cd.sem, cd.at(l, cd.n))
                                else:
                                    ins.then_inc(tmd.sem, tmd.tick())
                    elif s[0] == "end":
                        dve.wait_ge(pvd.sem, pvd.at(l, parts_end[s[1]]))
                    elif s[0] == "merged":
                        for k in range(KD):
                            low(xl[:, k, :], xh[:, k, :], merged[:, k, :])
                    elif s[0] == "S":
                        u = s[1]
                        gi = group_of[(u.br, u.b)]
                        dve.wait_ge(sS.sem, sS.at(l, u.i + 1))
                        sc = ps[u.i % 2][0:u.nq, u.base:u.base + u.nk]
                        if u.h == 0 and gi >= 2:
                            dve.wait_ge(ond.sem, ond.at(l, gi - 1))
                        if u.br == SWA:
                            if u.b == QTILES - 1 and u.h == 0:
                                dve.wait_ge(s_dist, l * 16 + 16)
                            nc.vector.scalar_tensor_tensor(
                                out=sc, in0=dist[0:u.nq, DIST_AT[u.b]:DIST_AT[u.b + 1]], scalar=-(2.0 ** -(u.h + 1)), in1=sc, op0=ALU.mult, op1=ALU.add).then_inc(cd.sem, cd.tick())
                            dve.wait_ge(cd.sem, cd.at(l, cd.n))
                            nc.vector.tensor_reduce(nraw[0:u.nq, gi % 2, u.h:u.h + 1], sc, AX.X, ALU.max,
                                                            negate=True).then_inc(cd.sem, cd.tick())
                            dve.wait_ge(cd.sem, cd.at(l, cd.n))
                            nc.vector.tensor_tensor(nmax[0:u.nq, gi % 2, u.h:u.h + 1],
                                                            nraw[0:u.nq, gi % 2, u.h:u.h + 1],
                                                            nsink[0:u.nq, u.h:u.h + 1], ALU.min).then_inc(mxd.sem, mxd.tick())
                        else:
                            w = u.end - u.q0
                            dg = sc[:, u.nk - w:u.nk]
                            nc.vector.tensor_tensor(dg, dg, mask[:, 0:w], ALU.add).then_inc(cd.sem, cd.tick())
                            dve.wait_ge(cd.sem, cd.at(l, cd.n))
                            nc.vector.tensor_reduce(nmax[0:u.nq, gi % 2, u.h:u.h + 1], sc, AX.X, ALU.max,
                                                            negate=True).then_inc(mxd.sem, mxd.tick())
                    elif s[0] == "O":
                        u = s[1]
                        gi = group_of[(u.br, u.b)]
                        r = slice(0, u.nq)
                        dve.wait_ge(pd.sem, pd.at(l, u.i + 1))
                        total = rsum
                        if u.br == SWA:
                            nc.vector.tensor_tensor(skx[r, gi % 2, :], nmax[r, gi % 2, :],
                                                            nsink[r, :], ALU.subtract).then_inc(skd.sem, skd.tick())
                            dve.wait_ge(sed.sem, sed.at(l, skd.n))
                            nc.vector.tensor_tensor(rtot[r, gi % 2, :], ske[r, gi % 2, :],
                                                            rsum[r, gi % 2, :], ALU.add).then_inc(cd.sem, cd.tick())
                            dve.wait_ge(cd.sem, cd.at(l, cd.n))
                            total = rtot
                        nc.vector.reciprocal(rinv[r, gi % 2, :], total[r, gi % 2, :]).then_inc(cd.sem, cd.tick())
                        dve.wait_ge(cd.sem, cd.at(l, cd.n))
                        dve.wait_ge(pvd.sem, pvd.at(l, u.part_ids[-1] + 1))
                        nc.vector.tensor_tensor(
                            osb[r, u.b, :].rearrange("p (h d) -> p h d", h=HEADS),
                            ps[3][r, 0:512].rearrange("p (h d) -> p h d", h=HEADS),
                            rinv[r, gi % 2, :].rearrange("p (h a) -> p h a", a=1).broadcast_to([u.nq, HEADS, HD]),
                            ALU.mult).then_inc(ond.sem, ond.tick())
                    elif s[0] == "OT":
                        u = s[1]
                        gi = group_of[(u.br, u.b)]
                        dve.wait_ge(ohd.sem, ohd.at(l, gi + 1))
                        src = heads_bank(gi)[:, :].rearrange("p (c q) -> p c q", c=BRANCH_TILES)[:, :, 0:u.end - u.q0]
                        nc.vector.tensor_tensor(otl[:, :, u.q0:u.end], src,
                                                        oth[:, :, u.q0:u.end].bitcast(F32), ALU.subtract).then_inc(old.sem, old.tick())

                def residual(base_g, base, i, slot, scale):
                    dve.wait_ge(mm.sem, mm.at(l, i + (base_g + 1)))
                    nc.vector.scalar_tensor_tensor(out=tile_of(h, i), in0=full(slot), scalar=scale,
                                                           in1=tile_of(h, i), op0=ALU.mult, op1=ALU.add).then_inc(hup.sem, hup.tick())
                    dve.wait_ge(hsd.sem, hsd.at(l, i + (base + 1)))
                    dve.wait_ge(ssd.sem, ssd.at(l, i + base))
                    nc.vector.tensor_tensor(ssum[:, :], ssum[:, :], hsq[:, slot % 2, :], ALU.add).then_inc(ssd.sem, ssd.tick())

                c_wo = split["next"]
                assert c_wo == c_out + AHEAD
                with dve.Fori(0, WO_TILES - 3, 4) as m:
                    for j in range(4):
                        high_part(l * CHUNKS + m, c_wo + j)
                        residual(g_wo, 0, m + j, j, 0.5)
                for s_ in (hup, ssd):
                    s_.skip(WO_TILES - 4)
                norm_input(1)
                tm0, x0 = tmd.n, xld.n
                assert tm0 == SP_FFN and x0 == SP_FFN, (tm0, x0)
                with dve.Fori(0, FT - 1, 2) as f:
                    for j in range(2):
                        for side, dst in ((0, cg), (1, cv)):
                            slot = 2 * j + side
                            high_part(l * CHUNKS + f * 2, c_wo + WO_TILES + slot)
                            src = full(slot)
                            cw = f * 3 + (PC_CW + 3 * (side * FT + j))
                            dve.wait_ge(cvd.sem, cvd.at(l, f * 2 + (2 * j + side + 1)))
                            nc.vector.scalar_tensor_tensor(
                                out=dst[:, j, 1:T], in0=src[:, 0:T - 1], scalar=prm[:, bass.ds(cw + 1, 1)],
                                in1=dst[:, j, 1:T], op0=ALU.mult, op1=ALU.add).then_inc(cd.sem, cd.tick())
                            dve.wait_ge(cd.sem, cd.at(l, f * 2 + cd.n))
                            ins = nc.vector.scalar_tensor_tensor(
                                out=dst[:, j, 2:T], in0=src[:, 0:T - 2], scalar=prm[:, bass.ds(cw, 1)],
                                in1=dst[:, j, 2:T], op0=ALU.mult, op1=ALU.add)
                            ins.then_inc(free.sem, free.tick())
                        dve.wait_ge(free.sem, free.at(l, f * 2 + (n_free + 2 * j + 2)))
                        dve.wait_ge(sid.sem, sid.at(l, f + (j + 1)))
                        nc.vector.tensor_tensor(am[:, j, :], si[:, j, :], cv[:, j, :], ALU.mult).then_inc(tmd.sem, tmd.tick())
                        dve.wait_ge(tmd.sem, tmd.at(l, f + (tm0 + j + 1)))
                        dve.wait_ge(thd.sem, thd.at(l, f + (x0 + j + 1)))
                        nc.vector.tensor_tensor(tile_of(al, f + j), am[:, j, :],
                                                        tile_of(ah, f + j).bitcast(F32), ALU.subtract).then_inc(xld.sem, xld.tick())
                for s_, n_ in ((cd, 4), (free, 4), (tmd, 2), (xld, 2)):
                    s_.skip(n_ * (FT // 2 - 1))
                with dve.Fori(0, KD - 3, 4) as m:
                    for j in range(4):
                        for i in range(3):
                            high_part(l * CHUNKS + m * 3, c_wo + WO_TILES + UP_TILES + 3 * j + i)
                        residual(g_dn, WO_TILES, m + j, j, 1.0)
                for s_ in (hup, ssd):
                    s_.skip(KD - 4)

    return {s.name: s.n for s in signals}


def pack_weights(inp):
    zero = np.zeros((P, P), np.float32)
    half = ROPE // 2

    def block(l, what, k, m):
        w_in = inp["w_in"][l]
        r = slice(k * P, (k + 1) * P)
        at = {"fq": O_FQ, "fk": O_FK, "fv": O_FV, "cq": O_CQ, "ckv": O_CKV, "sq": O_SQ, "sk": O_SK, "sv": O_SV}
        if what == "pad":
            return zero
        if what in at:
            return w_in[r, at[what] + m * P:at[what] + (m + 1) * P]
        out = zero.copy()
        if what == "ff":
            out[:, 0:HEADS] = w_in[r, O_FF:O_FF + HEADS]
        elif what == "kr":
            out[:, HD:MQ] = w_in[r, O_KR:O_KR + ROPE]
            out[:, MQ:MQ + half] = w_in[r, O_KR + half:O_KR + ROPE]
            out[:, MQ + half:P] = w_in[r, O_KR:O_KR + half]
        elif what == "mq":
            w = inp["mla_w_q_up"][l][r, m * MQ:(m + 1) * MQ]
            out[:, 0:MQ] = w
            out[:, MQ:MQ + half] = w[:, HD + half:MQ]
            out[:, MQ + half:P] = w[:, HD:HD + half]
        elif what == "mk":
            out[:, 0:HD] = inp["mla_w_kv_up"][l][:, m * 2 * HD:m * 2 * HD + HD]
        elif what == "mv":
            for e in range(2):
                c = (2 * m + e) * 2 * HD + HD
                out[:, e * HD:(e + 1) * HD] = inp["mla_w_kv_up"][l][:, c:c + HD]
        elif what[0] == "g":
            c = O_GATE + int(what[1]) * D + m * P
            out = w_in[r, c:c + P]
        elif what[0] == "y":
            out = inp["w_branch"][l][int(what[1])][r, m * P:(m + 1) * P]
        elif what == "wo":
            out = inp["w_o"][l][r, m * P:(m + 1) * P]
        elif what == "up":
            out = inp["ffn_w_up"][l][r, m * P:(m + 1) * P]
        elif what == "dn":
            out = inp["ffn_w_down"][l][r, m * P:(m + 1) * P]
        return out

    W = np.zeros((DEPTH * CHUNKS + AHEAD, P, CW), np.float32)
    for l in range(DEPTH):
        for i, (what, k, m) in enumerate(PLAN):
            W[l * CHUNKS + i // BLK, :, (i % BLK) * P:(i % BLK + 1) * P] = block(l, what, k, m)
    return W


def pack_params(inp):
    p = np.zeros((DEPTH + 1, P, PC_ALL), np.float32)
    half = ROPE // 2

    def cols(x, n):
        return x.reshape(n, P).T

    for l in range(DEPTH):
        p[l, :, PC_N1:PC_N1 + KD] = cols(inp["norm1_g"][l], KD)
        p[l, :, PC_N2:PC_N2 + KD] = cols(inp["norm2_g"][l], KD)
        for c, name in ((PC_FQ, "fox_q_g"), (PC_FK, "fox_k_g"), (PC_SQ, "swa_q_g"), (PC_SK, "swa_k_g")):
            p[l, :HD, c] = inp[name][l]
            p[l, HD:, c] = inp[name][l]
        p[l, :, PC_QA:PC_QA + 2] = cols(inp["mla_q_a_g"][l], 2)
        p[l, :, PC_KVA] = inp["mla_kv_a_g"][l]
        for c, name in ((PC_MQ, "mla_q_g"), (PC_MK, "mla_k_g")):
            g = inp[name][l]
            p[l, :MQ, c] = g
            p[l, MQ:MQ + half, c] = g[HD + half:]
            p[l, MQ + half:, c] = g[HD:HD + half]
        p[l, :HEADS, PC_FB] = inp["fox_forget_b"][l]
        p[l, :, PC_SINK:PC_SINK + HEADS] = inp["swa_sinks"][l][None, :]
        for i in range(3):
            p[l, :, PC_CW + i:PC_CB:3] = cols(inp["ffn_conv_w"][l][i], 2 * FT)
        p[l, :, PC_CB:PC_ALL] = cols(inp["ffn_conv_b"][l], 2 * FT)
    return p


def kernel(**inputs):
    import concourse.bacc as bacc
    from concourse.bass_utils import run_bass_kernel_spmd

    inp = {k: np.asarray(v) for k, v in inputs.items()}
    tokens = np.concatenate([inp["meta_tokens"], inp["x"][0]], axis=0)
    arrays = {
        "weights": pack_weights(inp),
        "tokens": np.ascontiguousarray(tokens.T.reshape(KD, P, T).transpose(1, 0, 2)),
        "params": pack_params(inp),
        "constants": constants(),
        "distances": alibi_tables(),
    }

    def program(counts):
        nc = bacc.Bacc("TRN2", target_bir_lowering=False, num_devices=1, dynamic_dma_scratch_size=2048)
        args = [nc.dram_tensor(n, a.shape, F32, kind="ExternalInput").ap() for n, a in arrays.items()]
        args.append(nc.dram_tensor("out", (P, KD, SEQ), F32, kind="ExternalOutput").ap())
        return nc, build(nc, *args, counts)

    _, counts = program({})
    nc, again = program(counts)
    assert again == counts
    r = run_bass_kernel_spmd(nc, [arrays], core_ids=[0])
    out = r.results[0]["out"]
    return np.ascontiguousarray(out.transpose(2, 1, 0)).reshape(1, SEQ, D)
```

```python
import concourse.bass as bass
import numpy as np
from concourse import mybir

F32 = mybir.dt.float32
F32R = mybir.dt.float32r
ALU = mybir.AluOpType
ACT = mybir.ActivationFunctionType
AX = mybir.AxisListType

P = 128
D = 1024
DEPTH = 2
SEQ = 512
META = 16
T = META + SEQ
TH = T // 2
KD = D // P
HEADS = 8
HD = 64
ROPE = 32
MQ = HD + ROPE
D_FF = 2816
FT = D_FF // P
EPS = 1e-6
NEG = -1.0e30
BRANCH_TILES = HEADS * HD // P
QTILES = 1 + SEQ // P
FOX, MLA, SWA = range(3)

BLK = 8
CW = BLK * P
RAW, SPLIT = 2, 4
STARTED_BEFORE = 2
AHEAD = 2

OFF = np.cumsum([0, 512, 512, 512, 8, 256, 128, 32, 512, 128, 128])
O_FQ, O_FK, O_FV, O_FF, O_CQ, O_CKV, O_KR, O_SQ, O_SK, O_SV, O_GATE = (int(v) for v in OFF)

PC_N1, PC_N2 = 0, 8
PC_FQ, PC_FK, PC_QA, PC_KVA, PC_MQ, PC_MK, PC_SQ, PC_SK, PC_FB = 16, 17, 18, 20, 21, 22, 23, 24, 25
PC_SINK = 26
PC_MKN = 34
PC_CW = 35
PC_CB = PC_CW + 3 * 2 * FT
PC_ALL = PC_CB + 2 * FT

CC_ID, CC_ONE, CC_PAIR, CC_MASK, CC_CS, CC_ALL = 0, 128, 256, 384, 512, 512 + T
DW = META + 2 * P
DIST_AT = [0, META]
for _b in range(2, QTILES + 1):
    DIST_AT.append(DIST_AT[-1] + (META + P if _b == 2 else DW))


SQUARED = {"fq": P, "fk": P, "sq": P, "sk": P, "cq": P, "ckv": P, "mq": MQ, "mk": P}
MEAN_OF = {"fq": HD, "fk": HD, "sq": HD, "sk": HD, "cq": 2 * P, "ckv": P, "mq": MQ, "mk": MQ}
LATE_SPAN = 0.93
OT_DELAY = 1
EARLY = 4
PADDED = (FOX, EARLY - 1)
TILE_BLOCKS = {"ff": 2 * BLK, "fv": 4 * KD, "fq": KD, "fk": KD, "cq": KD, "ckv": KD, "kr": KD, "mv": BLK, "mq": 2,
               "mk": 1, "sv": KD, "svt": 0, "sq": KD, "sk": KD, "g": KD, "y": BRANCH_TILES}
FILL_SPAN = 0.75
SP_CQ = KD
SP_MERGED = SP_CQ + 3
SP_NORM2 = SP_MERGED + KD
SP_FFN = SP_NORM2 + KD


def alibi_tables():
    i = np.arange(P)[:, None]
    out = []
    for b in range(1, QTILES):
        qpos = META + (b - 1) * P + i
        meta = qpos - np.arange(META)[None, :]
        lo = META + (b - 2) * P
        kpos = lo + np.arange(2 * P)[None, :]
        dist = qpos - kpos
        ok = (dist >= 0) & (dist < P) & (kpos >= META)
        band = np.where(ok, dist, -NEG)
        if b == 1:
            band = band[:, P:]
        out.append(np.concatenate([meta, band], axis=1))
    m = np.arange(META)
    dm = np.zeros((P, META))
    dm[:META] = np.where(m[:, None] >= m[None, :], m[:, None] - m[None, :], -NEG)
    return np.concatenate([dm] + out, axis=1).astype(np.float32)


def constants():
    c = np.zeros((P, CC_ALL), np.float32)
    c[:, CC_ID:CC_ID + P] = np.eye(P)
    c[:, CC_ONE:CC_ONE + P] = 1.0
    c[:HD, CC_PAIR:CC_PAIR + HD] = 1.0
    c[HD:, CC_PAIR + HD:CC_PAIR + P] = 1.0
    c[:, CC_MASK:CC_MASK + P] = np.where(np.arange(P)[None, :] <= np.arange(P)[:, None], 0.0, NEG)
    half = ROPE // 2
    freqs = np.float32(10000.0) ** (-np.arange(half, dtype=np.float32) / np.float32(half))
    ang = (np.arange(T, dtype=np.float32)[:, None] * freqs[None, :]).T.astype(np.float32)
    cos, sin = np.cos(ang), np.sin(ang)
    c[:, CC_CS:CC_CS + T] = 1.0
    c[HD:MQ, CC_CS:CC_CS + T] = np.concatenate([cos, cos])
    c[MQ:P, CC_CS:CC_CS + T] = np.concatenate([-sin, sin])
    return c


class Signal:

    def __init__(self, nc, name, counts, before=0):
        self.sem = nc.alloc_semaphore(name)
        self.name, self.n = name, 0
        self.before = before
        self.per_layer = counts.get(name, 10 ** 5)

    def tick(self, by=1):
        self.n += by
        return by

    def skip(self, n):
        self.n += n

    def at(self, layer, n):
        return layer * self.per_layer + (n + self.before)


class Unit:

    def __init__(self, i, br, b, h):
        self.i, self.br, self.b, self.h = i, br, b, h
        self.nq = P
        self.q0 = 0 if b == 0 else META + (b - 1) * P
        self.end = META if b == 0 else self.q0 + P
        if br == SWA and b > 2:
            self.ranges = [(0, META, 0), (self.q0 - P, 2 * P, META)]
            self.nk = DW
            tiles = [(0, 0), (b - 1, META), (b, META + P)]
        else:
            self.nk = self.end
            self.ranges = [(0, self.nk, 0)] if self.nk <= 512 else [(0, TH, 0), (TH, TH, TH)]
            tiles = [(t, 0 if t == 0 else META + (t - 1) * P) for t in range(b + 1)]
        self.base = 512 - TH if self.nk > 512 else 0
        n = len(tiles)
        cut = n if n <= 4 else 3
        self.parts = [tiles[:cut]] + ([tiles[cut:]] if cut < n else [])
        self.part_ids = []


def schedule():
    steps = []
    tiles = {"n": 0, "blocks": 0}
    units = []
    parts = {"n": 0}
    stats = {"n": 1}
    squares = {"n": 0, "mine": {}}

    def gemm(kind, m=0, stat=False):
        t = dict(kind=kind, m=m, g=tiles["n"], slot=None, stat=None)
        tiles["blocks"] += TILE_BLOCKS[kind]
        t["chunk"] = (tiles["blocks"] - 1) // BLK
        if stat:
            t["stat"] = stats["n"]
            stats["n"] += 1
        tiles["n"] += 1
        if kind == "y" and m == PADDED:
            tiles["blocks"] += 4
        if kind in SQUARED:
            ring = "k" if kind in ("mk", "ckv") else "a"
            mine = squares["mine"].setdefault(ring, [])
            t["sqn"], t["par"] = squares["n"], len(mine) % 2
            squares["n"] += 1
            mine.append(t)
            t["prev"] = mine[-3] if len(mine) > 2 else None
        return t

    def attention(br, fillers, late=()):
        us = []
        for b in range(QTILES - 1, -1, -1):
            for h in range(HEADS):
                u = Unit(len(units), br, b, h)
                units.append(u)
                us.append(u)
        fill = list(fillers) + list(late)
        pending = []
        weights = [0.0]
        for u in us:
            weights.append(weights[-1] + 0.5 + u.nk / 264)
        done = 0
        for u in us[:2]:
            steps.append(("S", u))
            steps.append(("E", u))
        behind = []
        filled = []
        if late and not fillers or br == MLA:
            filled.append(gemm(*fill[0]))
            steps.append(("gemm", filled[-1]))
            done = 1

        def product(j):
            u, p = behind.pop(0)
            steps.append(("PV", u, p))
            if p == len(u.parts) - 1 and u.h == HEADS - 1:
                steps.append(("O", u))
                pending.append((u, j))

        for j, u in enumerate(us):
            if j + 2 < len(us):
                steps.append(("S", us[j + 2]))
            part = weights[j + 1] / weights[-1]
            want = min(len(fillers), int(len(fillers) * part / FILL_SPAN + 1e-9))
            if want == len(fillers) and late:
                begin = FILL_SPAN if fillers else 0.0
                want += min(len(late), max(0, int(len(late) * (part - begin) / (LATE_SPAN - begin) + 1e-9)))
            for p in range(len(u.parts)):
                u.part_ids.append(parts["n"])
                parts["n"] += 1
                steps.append(("T", u, p))
                if p == len(u.parts) - 1 and j + 2 < len(us):
                    steps.append(("E", us[j + 2]))
                if done < want:
                    filled.append(gemm(*fill[done]))
                    steps.append(("gemm", filled[-1]))
                    done += 1
                if behind:
                    product(j)
                behind.append((u, p))
            while done < want:
                filled.append(gemm(*fill[done]))
                steps.append(("gemm", filled[-1]))
                done += 1
            while pending and done >= len(fillers) and j >= pending[0][1] + OT_DELAY:
                steps.append(("OT", pending.pop(0)[0]))
        product(len(us))
        for u, _ in pending:
            steps.append(("OT", u))
        steps.append(("end", br))
        return filled

    def project(kinds, more=()):
        late = []
        for t in kinds:
            if t["kind"] == "mv":
                while late:
                    steps.append(("stat", late.pop(0)))
            steps.append(("gemm", t))
            if late:
                steps.append(("stat", late.pop(0)))
            if t["stat"] is not None:
                late.append(t)
        for t in more:
            steps.append(("gemm", t))
            while late:
                steps.append(("stat", late.pop(0)))
        for t in late:
            steps.append(("stat", t))

    def gate_branch(br, first=0):
        out = []
        for d in range(first, KD):
            out += [("g", (br, d)), ("y", (br, d))]
        return out

    front = ([gemm("ff"), gemm("fv")] + [gemm("fq", m, True) for m in range(4)]
             + [gemm("fk", m, True) for m in range(4)] + [gemm("cq", 0), gemm("cq", 1)])
    latents = front[-2:]
    latents[1]["stat"] = stats["n"]
    stats["n"] += 1
    project(front[:-2], latents)
    latents += attention(FOX, (), [("ckv", 0, True), ("kr",)] + [("g", (FOX, d)) for d in range(EARLY)])
    steps.append(("stat", latents[1]))
    steps.append(("gemm", gemm("y", (FOX, 0))))
    steps.append(("stat", latents[2]))
    steps.append(("gemm", gemm("y", (FOX, 1))))
    steps.append(("rope", latents[3]))
    a = [gemm("mv")]
    for h in range(HEADS):
        a.append(gemm("mq", h, True))
        if h == 3:
            a.append(gemm("y", (FOX, 2)))
    a += [gemm("mk", m, True) for m in range(HEADS // 2)]
    project(a, [gemm("y", (FOX, EARLY - 1)), gemm("g", (FOX, EARLY))])
    attention(MLA, gate_branch(FOX, EARLY)[1:], [("sv",)])
    project([gemm("sq", 0, True), gemm("svt")] + [gemm("sq", m, True) for m in range(1, 4)]
            + [gemm("sk", 0, True)], [gemm("g", (MLA, 0))])
    attention(SWA, gate_branch(MLA)[1:], [("g", (SWA, 0)), ("g", (SWA, 1))])
    last = gate_branch(SWA)
    for kind, m in [last[1]] + [t for d in range(2, KD) for t in (last[2 * d], last[2 * d - 1])] + [last[-1]]:
        steps.append(("gemm", gemm(kind, m)))
        if kind == "y" and m[1] > 0:
            steps.append(("merged", m[1] - 1))
    steps.append(("merged", KD - 1))
    inside = False
    ring = 0
    for s in steps:
        if s[0] == "S":
            inside = True
        elif s[0] == "end":
            inside = False
            ring = 0
        elif s[0] == "gemm":
            t = s[1]
            if t["kind"] in ("fv", "mv"):
                t["slot"] = (0, 1, 2)
            elif inside:
                t["slot"] = (2,)
            else:
                t["slot"] = (ring % 3,)
                ring += 1
    last = {}
    for s in steps:
        if s[0] == "gemm":
            t = s[1]
            t["after"] = sorted({last[x] for x in t["slot"] if x in last})
            for x in t["slot"]:
                last[x] = t["g"]
    order = {"free": 0, "rawd": 0, "svd": 0, "qkv": 0, "tmd": KD, "sgd": 0, "gmd": 0}
    freed = {}

    def frees(t, name, by=1):
        order[name] += by
        freed[t["g"]] = (name, order[name])

    for s in steps:
        if s[0] == "gemm":
            t = s[1]
            if t["kind"] == "ff":
                frees(t, "free")
            elif t["kind"] in ("cq", "ckv", "kr"):
                frees(t, "rawd")
            elif t["kind"] == "sv":
                frees(t, "svd")
            elif t["kind"] in ("fv", "mv", "svt"):
                frees(t, "qkv")
            elif t["kind"] == "g":
                frees(t, "sgd")
            elif t["kind"] == "y":
                frees(t, "gmd")
        elif s[0] == "stat":
            t = s[1]
            if t["kind"] == "mq":
                frees(t, "free")
                order["qkv"] += 1
            elif t["kind"] not in ("cq", "ckv"):
                frees(t, "qkv")
    filler, transposed, before = None, 0, []
    for s in steps:
        if s[0] == "gemm":
            before.append(s[1])
            if filler is None and 2 in s[1]["slot"] and transposed:
                s[1]["behind_ot"] = transposed
            if 2 in s[1]["slot"]:
                filler = s[1]
        elif s[0] == "S" and s[1].i % (QTILES * HEADS) < 2:
            s[1].slot_free = freed[[x for x in before if s[1].i % 2 in x["slot"]][-1]["g"]]
        elif s[0] == "OT":
            s[1].slot_free = freed[filler["g"]] if filler else None
            filler = None
            transposed += 1
    for s in steps:
        if s[0] == "gemm":
            latest = {}
            for name, count in (freed[g] for g in s[1]["after"]):
                latest[name] = max(count, latest.get(name, 0))
            if "behind_ot" in s[1]:
                latest["old"] = s[1]["behind_ot"]
            s[1]["after"] = list(latest.items())
    n_free = order["free"]
    return steps, units, tiles["n"], stats["n"], n_free


def stream_plan(steps):
    b = []
    pad = [("pad", 0, 0)]

    def tile(what, rows, m):
        b.extend((what, k, m) for k in range(rows))

    for s in steps:
        if s[0] != "gemm":
            continue
        kind, m = s[1]["kind"], s[1]["m"]
        if kind == "ff":
            tile("ff", 4, 0)
            b.extend(pad * 4 + [("ff", k, 0) for k in range(4, KD)] + pad * 4)
        elif kind == "fv":
            b.extend(("fv", k, c) for k in range(KD) for c in range(4))
        elif kind == "mv":
            b.extend([("mv", 0, c) for c in range(4)] + pad * 4)
        elif kind in ("g", "y"):
            tile(f"{kind}{m[0]}", TILE_BLOCKS[kind], m[1])
            if kind == "y" and m == PADDED:
                b.extend(pad * 4)
        elif kind != "svt":
            tile(kind, TILE_BLOCKS[kind], m)
    for m in range(KD):
        tile("wo", KD, m)
    for f in range(FT):
        tile("up", KD, f)
        tile("up", KD, FT + f)
    for m in range(KD):
        tile("dn", FT, m)
        b.extend(pad * 2)
    assert len(b) % (BLK * 4) == 0
    return b


PLAN = stream_plan(schedule()[0])
CHUNKS = len(PLAN) // BLK


def build(nc, W, H, PRM, CST, DIST, OUT, counts):
    steps, units, n_tiles, n_stats, n_free = schedule()

    at = [(nc.sbuf_base + 63) // 64 * 64]

    def sb(name, shape, dt=F32, offset=None):
        size = int(np.prod(shape[1:])) * 4
        if offset is None:
            offset = at[0]
            at[0] += (size + 31) // 32 * 32
        t = nc.alloc_sbuf_tensor_at(name, shape, dt, offset=offset)
        return t

    h = sb("h", [P, KD, T])
    xh = sb("xh", [P, KD, T], F32R)
    xl = sb("xl", [P, KD, T], F32R)
    raw = sb("raw", [P, RAW, CW])
    wh = [sb(f"wh{i}", [P, CW], F32R) for i in range(SPLIT)]
    wl = [sb(f"wl{i}", [P, CW], F32R) for i in range(SPLIT)]
    attn_at = at[0]
    qt = sb("qt", [P, HEADS, T])
    kt = sb("kt", [P, HEADS, T])
    mh = sb("mh", [P, KD, T], F32R, offset=attn_at)
    ml = sb("ml", [P, KD, T], F32R, offset=attn_at + KD * T * 4)
    v = sb("v", [P, QTILES, HEADS * HD])
    oth = sb("oth", [P, BRANCH_TILES, T], F32R)
    otl = sb("otl", [P, BRANCH_TILES, T], F32R)
    merged_at = at[0]
    merged = sb("merged", [P, KD, T])
    merged_end = at[0]
    at[0] = merged_at
    fz, fa, fe, fl, fm, fs, ld, nld = (sb(f"dec{i}", [P, T]) for i in range(8))
    at[0] = merged_end
    latent = merged[:, EARLY:, :]
    rope_square = latent[:, 2, :]
    probs = sb("probs", [P, 2, T])
    pts_at = at[0]
    pts = sb("pts", [P, 2, 512])
    osb = sb("osb", [P, QTILES, 512])
    lath = sb("lath", [P, 3, T], F32R, offset=pts_at)
    latl = sb("latl", [P, 3, T], F32R, offset=pts_at + 3 * T * 4)
    assert pts_at + 6 * T * 4 <= at[0]
    gq = sb("gq", [P, T])
    krr = sb("krr", [P, T])
    ksq = sb("ksq", [P, 2, T])
    end_attn = at[0]
    at[0] = attn_at
    ah = sb("ah", [P, FT, T], F32R)
    al = sb("al", [P, FT, T], F32R)
    at[0] = max(at[0], end_attn)
    tmp_at = at[0]
    sq = sb("sq", [P, 2, T])
    guess = sb("guess", [P, 2, T])
    guess2 = probs
    negmean = sb("negmean", [P, 2, T])
    tmp = sb("tmp", [P, 2, T])
    end_tmp = at[0]
    at[0] = tmp_at
    cg = sb("cg", [P, 2, T])
    cv = sb("cv", [P, 2, T])
    si = sb("si", [P, 2, T])
    am = sb("am", [P, 2, T])
    at[0] = max(at[0], end_tmp)
    rstd = sb("rstd", [P, T])
    ssum = sb("ssum", [P, T])
    hsq = sq
    gsb = tmp
    dist = kt[:, 2:4, :].rearrange("p a t -> p (a t)")
    cst = sb("cst", [P, CC_ALL])
    prm = sb("prm", [P, PC_ALL])
    gts = sb("gts", [P, 4])
    nmax = sb("nmax", [P, 2, HEADS])
    nraw = sb("nraw", [P, 2, HEADS])
    rsum = sb("rsum", [P, 2, HEADS])
    skx = sb("skx", [P, 2, HEADS])
    ske = sb("ske", [P, 2, HEADS])
    rtot = sb("rtot", [P, 2, HEADS])
    rinv = sb("rinv", [P, 2, HEADS])
    nsink = sb("nsink", [P, HEADS])
    assert at[0] <= nc.sbuf_usable_end, at[0]

    ps = [nc.alloc_psum_tensor(f"ps{i}", [P, 1024], F32) for i in range(4)]

    ident = cst[:, CC_ID:CC_ID + P]
    ones = cst[:, CC_ONE:CC_ONE + P]
    pair = cst[:, CC_PAIR:CC_PAIR + P]
    mask = cst[:, CC_MASK:CC_MASK + P]
    cs = cst[:, CC_CS:CC_CS + T]
    CENTRE = 512 - TH

    def full(slot):
        return ps[slot][:, CENTRE:CENTRE + T]

    def half(slot, j):
        return ps[slot][:, CENTRE + j * TH:CENTRE + (j + 1) * TH]

    def heads_bank(gi):
        return ps[2][:, (gi % 2) * 512:(gi % 2) * 512 + 512]

    def probs_bank(u, part):
        return ps[0 if u.base == 0 and part % 2 else 3][:, 512:1024]

    def value_bank(tt):
        return ps[tt // 2][:, (tt % 2) * 512:(tt % 2) * 512 + 512]

    def S(name, before=0):
        s = Signal(nc, name, counts, before)
        signals.append(s)
        return s

    signals = []
    s_cst = nc.alloc_semaphore("constants_loaded")
    s_hin = [nc.alloc_semaphore(f"input_loaded{i}") for i in range(KD // 2)]
    s_prm = nc.alloc_semaphore("params_loaded")
    s_out = nc.alloc_semaphore("output_stored")
    s_raw = [nc.alloc_semaphore(f"chunk_loaded{i}") for i in range(RAW)]
    s_hi = nc.alloc_semaphore("chunk_high_part")
    s_w = nc.alloc_semaphore("chunk_split")
    s_start = nc.alloc_semaphore("chunk_started")
    s_ini = nc.alloc_semaphore("eps_set")
    s_dist = nc.alloc_semaphore("distances_loaded")
    mm = S("tile_ready")
    st = S("stat_ready")
    free = S("tile_freed")
    sqd = S("square_ready")
    statd = S("statistic_read")
    guessd = S("rsqrt_guess_ready")
    rsd = S("rsqrt_ready")
    ssd = S("sum_squares_ready", KD)
    hsd = S("residual_square", KD)
    hup = S("residual_updated", KD)
    tmd = S("fp32_ready")
    thd = S("high_part_ready")
    xld = S("low_part_ready")
    sS = S("scores_ready")
    mxd = S("max_ready")
    pd = S("probs_ready")
    td = S("probs_transposed")
    ptd = S("transposed_copied")
    pvd = S("pv_done")
    skd = S("sink_sum")
    sed = S("sink_exp")
    ond = S("heads_normalised")
    otd = S("heads_transposed")
    ohd = S("head_high_part")
    old = S("head_low_part")
    f1 = S("decay_logit")
    f2 = S("decay_log1p")
    f3 = S("decay_summed")
    f4 = S("decay_rows_placed")
    krd = S("rope_key_squared")
    qkv = S("qkv_written")
    rawd = S("latent_copied")
    svd = S("window_values_copied")
    sgd = S("gate_ready")
    addd = S("gated_tile_added")
    gmd = S("gate_used")
    scd = S("up_tile_scaled")
    cvd = S("conv_scaled")
    sid = S("silu_ready")
    ca = S("act_chain")
    cd = S("dve_chain")
    WO_TILES = KD
    UP_TILES = 2 * FT
    c_out = max(s[1]["chunk"] for s in steps if s[0] == "gemm") + 1
    g_wo, g_up = n_tiles, n_tiles + WO_TILES
    g_dn = g_up + UP_TILES

    group_of = {}
    groups = []
    for u in units:
        if u.h == 0:
            groups.append((u.br, u.b))
        group_of[(u.br, u.b)] = len(groups) - 1
    per_branch = QTILES
    qkv_end = {}
    n = 0
    for s in steps:
        if s[0] == "gemm" and s[1]["kind"] in ("fq", "fk", "fv", "mq", "mk", "mv", "sq", "sk", "svt"):
            n += 1
        if s[0] == "end":
            qkv_end[s[1]] = n
    parts_end = {}
    for u in units:
        parts_end[u.br] = max(parts_end.get(u.br, 0), max(u.part_ids) + 1)
    last_y, stat_of = {}, {}
    for s in steps:
        if s[0] == "stat":
            stat_of[s[1]["g"]] = s[1]["stat"]
            if s[1]["kind"] == "cq":
                stat_of[s[1]["g"] - 1] = s[1]["stat"]
    for s in steps:
        if s[0] == "gemm" and s[1]["kind"] == "y":
            last_y[s[1]["m"][0]] = s[1]["g"]
    by_name = {"free": free, "old": old, "rawd": rawd, "svd": svd, "qkv": qkv, "tmd": tmd, "sgd": sgd, "gmd": gmd}

    def tile_of(t, i):
        if isinstance(i, int):
            return t[:, i, :]
        return t[:, bass.ds(i, 1), :].rearrange("p a t -> p (a t)")


    block = nc.Block()
    with block as blk:

        @blk.sync
        def _(sp):
            def load(n, s):
                sp.dma_start(raw[:, s, :], W[n, :, :]).then_inc(s_raw[s], 16)

            for k in range(0, KD, 2):
                sp.dma_start(h[:, k:k + 2, :], H[:, k:k + 2, :]).then_inc(s_hin[k // 2], 16)
            sp.dma_start(cst[:, :], CST[:, :]).then_inc(s_cst, 16)
            for s in range(RAW):
                load(s, s)
            with sp.Fori(RAW, DEPTH * CHUNKS + AHEAD - RAW + 1, RAW) as n:
                for s in range(RAW):
                    sp.wait_ge(s_w, n + (s + 1 - RAW))
                    load(n + s, s)
            for k in range(KD):
                sp.wait_ge(hup.sem, hup.at(DEPTH - 1, WO_TILES + k + 1))
                sp.dma_start(OUT[:, k, :], h[:, k, META:T]).then_inc(s_out, 16)
            sp.wait_ge(s_out, 16 * KD)

        @blk.gpsimd
        def _(pool):
            with pool.Fori(0, DEPTH * CHUNKS - SPLIT + 1, SPLIT) as n:
                for s in range(SPLIT):
                    pool.wait_ge(s_hi, n + (s + 1))
                    nc.gpsimd.tensor_tensor(wl[s][:, :], raw[:, s % RAW, :], wh[s][:, :].bitcast(F32),
                                            ALU.subtract).then_inc(s_w, 1)

        @blk.scalar
        def _(act):
            def split_high(l, count, out, in_):
                act.wait_ge(tmd.sem, tmd.at(l, count))
                nc.scalar.activation(out, in_, ACT.Copy).then_inc(thd.sem, thd.tick())

            def rsqrt_guess(l, n, stat):
                act.wait_ge(st.sem, st.at(l, stat + 1))
                if stat > 1:
                    act.wait_ge(rsd.sem, rsd.at(l, stat - 1))
                s_ = stat % 2
                nc.scalar.activation(guess[:, s_, :], full(3), ACT.Abs_reciprocal_sqrt,
                                     scale=1.0 / n, bias=gts[:, 2:3]).then_inc(ca.sem, ca.tick())
                nc.scalar.activation(negmean[:, s_, :], full(3), ACT.Identity, scale=-1.0 / n,
                                     bias=gts[:, 3:4]).then_inc(statd.sem, statd.tick())
                act.wait_ge(ca.sem, ca.at(l, ca.n))
                nc.scalar.activation(guess2[:, s_, :], guess[:, s_, :], ACT.Square).then_inc(guessd.sem, guessd.tick())

            act.dma_start(prm[:, :], PRM[0, :, :]).then_inc(s_prm, 16)
            act.wait_ge(s_ini, 1)
            for k in range(KD):
                if k % 2 == 0:
                    act.wait_ge(s_hin[k // 2], 16)
                if k >= 2:
                    act.wait_ge(ssd.sem, k - 1)
                nc.scalar.activation(hsq[:, k % 2, :], h[:, k, :], ACT.Square).then_inc(hsd.sem, 1)
            with act.Fori(0, DEPTH) as l:

                def norm_input():
                    rsqrt_guess(l, D, 0)
                    for k in range(KD):
                        split_high(l, k + 1, xh[:, k, :], tmp[:, k % 2, :])

                def attn(s):
                    kind, u = s[0], s[1]
                    if kind == "E":
                        act.wait_ge(mxd.sem, mxd.at(l, u.i + 1))
                        if u.i >= 2:
                            act.wait_ge(td.sem, td.at(l, units[u.i - 2].part_ids[-1] + 1))
                        nc.scalar.activation(
                            probs[0:u.nq, u.i % 2, 0:u.nk], ps[u.i % 2][0:u.nq, u.base:u.base + u.nk], ACT.Exp,
                            bias=nmax[0:u.nq, group_of[(u.br, u.b)] % 2, u.h:u.h + 1],
                            accum_out=rsum[0:u.nq, group_of[(u.br, u.b)] % 2, u.h:u.h + 1]).then_inc(pd.sem, pd.tick())
                    elif kind == "T":
                        i = u.part_ids[s[2]]
                        act.wait_ge(td.sem, td.at(l, i + 1))
                        if i >= 2:
                            act.wait_ge(pvd.sem, pvd.at(l, i - 1))
                        w = len(u.parts[s[2]]) * u.nq
                        nc.scalar.activation(pts[:, i % 2, 0:w], probs_bank(u, i)[:, 0:w], ACT.Copy).then_inc(ptd.sem, ptd.tick())
                    elif kind == "O":
                        gi = group_of[(u.br, u.b)]
                        if u.br == SWA:
                            act.wait_ge(skd.sem, skd.at(l, sed.n + 1))
                            nc.scalar.activation(ske[:, gi % 2, :], skx[:, gi % 2, :], ACT.Exp).then_inc(sed.sem, sed.tick())
                    elif kind == "OT":
                        gi = group_of[(u.br, u.b)]
                        act.wait_ge(otd.sem, otd.at(l, gi + 1))
                        if u.b == QTILES - 1 and u.br != FOX:
                            act.wait_ge(mm.sem, mm.at(l, last_y[u.br - 1] + 1))
                        src = heads_bank(gi)[:, :].rearrange("p (c q) -> p c q", c=BRANCH_TILES)[:, :, 0:u.end - u.q0]
                        nc.scalar.activation(oth[:, :, u.q0:u.end], src, ACT.Copy).then_inc(ohd.sem, ohd.tick())

                norm_input()
                for s in steps:
                    if s[0] in ("E", "T", "O", "OT"):
                        attn(s)
                    elif s[0] == "end" and s[1] == MLA:
                        act.wait_ge(pvd.sem, pvd.at(l, parts_end[MLA]))
                        act.dma_start(dist[:, 0:DIST_AT[-1]], DIST[:, :]).then_inc(s_dist, 16)
                    elif s[0] == "merged":
                        split_high(l, SP_MERGED + s[1] + 1, mh[:, s[1], :], merged[:, s[1], :])
                    elif s[0] == "rope":
                        act.wait_ge(tmd.sem, tmd.at(l, SP_CQ + 3))
                        act.wait_ge(rawd.sem, rawd.at(l, 4))
                        nc.scalar.activation(rope_square[HD:MQ, :], latent[HD:MQ, 3, :], ACT.Square).then_inc(krd.sem, krd.tick())
                    elif s[0] == "stat":
                        t = s[1]
                        rsqrt_guess(l, MEAN_OF[t["kind"]], t["stat"])
                        if t["kind"] == "cq":
                            for k in range(2):
                                split_high(l, SP_CQ + k + 1, lath[:, k, :], tmp[:, k, :])
                        if t["kind"] == "ckv":
                            split_high(l, SP_CQ + 3, lath[:, 2, :], tmp[:, 0, :])
                    elif s[0] == "gemm":
                        t = s[1]
                        k = t["kind"]
                        src = full(t["slot"][0])
                        if k in SQUARED:
                            rows = SQUARED[k]
                            if t["prev"] is not None:
                                act.wait_ge(st.sem, st.at(l, stat_of[t["prev"]["g"]] + 1))
                            act.wait_ge(mm.sem, mm.at(l, t["g"] + 1))
                            dst = ksq if k in ("mk", "ckv") else sq
                            nc.scalar.activation(dst[0:rows, t["par"], :], src[0:rows, :], ACT.Square).then_inc(sqd.sem, sqd.tick())
                        elif k == "ff":
                            act.wait_ge(f1.sem, f1.at(l, 1))
                            nc.scalar.activation(fa[0:8, :], fz[0:8, :], ACT.Abs).then_inc(ca.sem, ca.tick())
                            act.wait_ge(ca.sem, ca.at(l, ca.n))
                            nc.scalar.activation(fe[0:8, :], fa[0:8, :], ACT.Exp, scale=-1.0).then_inc(ca.sem, ca.tick())
                            act.wait_ge(ca.sem, ca.at(l, ca.n))
                            nc.scalar.activation(fl[0:8, :], fe[0:8, :], ACT.Ln, bias=1.0).then_inc(f2.sem, f2.tick())
                        elif k == "fv":
                            act.wait_ge(f3.sem, f3.at(l, 1))
                            for dst, row, src in ((qt, HD, ld), (kt, HD + 1, nld)):
                                act.dma_start(dst[row:row + 1, :, :], src[0:8, :]).then_inc(f4.sem, f4.tick(16))
                        elif k == "g":
                            act.wait_ge(mm.sem, mm.at(l, t["g"] + 1))
                            i = sgd.n
                            before = i - 2 - KD
                            if before >= KD:
                                act.wait_ge(tmd.sem, tmd.at(l, SP_MERGED + before - KD + 1))
                            elif before >= 0:
                                act.wait_ge(addd.sem, addd.at(l, before + 1))
                            elif i == 0:
                                act.wait_ge(f4.sem, f4.at(l, 32))
                            dst = merged[:, i, :] if t["m"][0] == FOX else gsb[:, i % 2, :]
                            nc.scalar.activation(dst, src, ACT.Tanh, scale=0.5).then_inc(sgd.sem, sgd.tick())

                def square_residual(base, i, par):
                    act.wait_ge(hup.sem, hup.at(l, i + (base + 1)))
                    act.wait_ge(ssd.sem, ssd.at(l, i + (base - 1)))
                    nc.scalar.activation(hsq[:, par, :], tile_of(h, i), ACT.Square).then_inc(hsd.sem, hsd.tick())

                with act.Fori(0, WO_TILES - 3, 4) as m:
                    for j in range(4):
                        square_residual(0, m + j, j % 2)
                        split_high(l, m + (SP_NORM2 + j + 1), tile_of(xh, m + j), tmp[:, j % 2, :])
                for s_ in (hsd, thd):
                    s_.skip(WO_TILES - 4)
                rsqrt_guess(l, D, n_stats)
                with act.Fori(0, FT - 1, 2) as f:
                    for j in range(2):
                        for side, dst in ((0, cg), (1, cv)):
                            act.wait_ge(scd.sem, scd.at(l, f * 2 + (2 * j + side + 1)))
                            cw = f * 3 + (PC_CW + 3 * (side * FT + j))
                            nc.scalar.activation(
                                dst[:, j, :], full(2 * j + side), ACT.Identity,
                                scale=prm[:, bass.ds(cw + 2, 1)], bias=prm[:, bass.ds(f + (PC_CB + side * FT + j), 1)]).then_inc(cvd.sem, cvd.tick())
                        act.wait_ge(free.sem, free.at(l, f * 2 + (n_free + 2 * j + 1)))
                        nc.scalar.activation(si[:, j, :], cg[:, j, :], ACT.Silu).then_inc(sid.sem, sid.tick())
                        split_high(l, f + (SP_FFN + j + 1), tile_of(ah, f + j), am[:, j, :])
                for s_, n_ in ((cvd, 4), (sid, 2), (thd, 2)):
                    s_.skip(n_ * (FT // 2 - 1))
                act.wait_ge(xld.sem, xld.at(l, SP_FFN + FT))
                act.dma_start(prm[:, :], PRM[l + 1, :, :]).then_inc(s_prm, 16)
                with act.Fori(0, KD - 3, 4) as m:
                    for j in range(4):
                        square_residual(WO_TILES, m + j, j % 2)
                hsd.skip(KD - 4)
            act.wait_ge(s_prm, 16 * (DEPTH + 1))

        @blk.tensor
        def _(pe):
            pe.sem_inc(s_start, STARTED_BEFORE)
            pe.wait_ge(s_cst, 16)
            with pe.Fori(0, DEPTH) as l:
                cur = {"b": 0}

                def block_at(c, i, chunk_no):
                    if i == 0:
                        pe.wait_ge(s_w, chunk_no + 1)
                        cur["fresh"] = True
                    a = i * P
                    return wh[c][:, a:a + P], wl[c][:, a:a + P]

                def issued(ins):
                    if cur.get("fresh"):
                        ins.then_inc(s_start, 1)
                        cur["fresh"] = False

                def take():
                    b = cur["b"]
                    cur["b"] += 1
                    c = b // BLK
                    return block_at(c % SPLIT, b % BLK, l * CHUNKS + c)

                def take_padded():
                    if cur["b"] % BLK == BLK // 2:
                        cur["b"] += BLK // 2
                    return take()

                def rows_out(slot, blocks, xhi, xlo, nk):
                    ins = None
                    for k in range(nk):
                        a_hi, a_lo = blocks()
                        x_hi = xhi(k)
                        for j in range(2):
                            sl = slice(j * TH, (j + 1) * TH)
                            a = nc.tensor.matmul(half(slot, j), a_hi, x_hi[:, sl], start=(k == 0), stop=False)
                            issued(a)
                            nc.tensor.matmul(half(slot, j), a_hi, xlo(k)[:, sl], start=False, stop=False)
                        for j in range(2):
                            sl = slice(j * TH, (j + 1) * TH)
                            ins = nc.tensor.matmul(half(slot, j), a_lo, x_hi[:, sl], start=False, stop=(k == nk - 1))
                    return ins

                def tok(tt):
                    return slice(0, P) if tt == 0 else slice(META + (tt - 1) * P, META + tt * P)

                def tokens_out(xhi, xlo, nk, width):
                    ins = None
                    for k in range(nk):
                        nb_ = width // P
                        first = take()
                        b0 = cur["b"] - 1
                        for _ in range(nb_ - 1):
                            cur["b"] += 1
                        c = (b0 // BLK) % SPLIT
                        a = (b0 % BLK) * P
                        whi, wlo = wh[c][:, a:a + width], wl[c][:, a:a + width]
                        for tt in range(QTILES):
                            o = value_bank(tt)[:, 0:width]
                            i0 = nc.tensor.matmul(o, xhi(k)[:, tok(tt)], whi, start=(k == 0), stop=False)
                            issued(i0)
                            nc.tensor.matmul(o, xhi(k)[:, tok(tt)], wlo, start=False, stop=False)
                            ins = nc.tensor.matmul(o, xlo(k)[:, tok(tt)], whi, start=False, stop=(k == nk - 1))
                    return ins

                def xk(t):
                    return lambda k: t[:, k, :]

                def stat(rhs, lhs, rows, first=True, last=True):
                    for j in range(2):
                        ins = nc.tensor.matmul(half(3, j), lhs[0:rows, :], rhs[0:rows, j * TH:(j + 1) * TH],
                                               start=first, stop=last)
                    return ins

                def norm_stat(which):
                    pe.wait_ge(ssd.sem, ssd.at(l, KD * which))
                    stat(ssum, ones, P).then_inc(st.sem, st.tick())

                copied = {}

                norm_stat(0)

                def x_ready(t, base):
                    def f(k):
                        pe.wait_ge(xld.sem, xld.at(l, base + k + 1))
                        return t[:, k, :]
                    return f

                for s in steps:
                    if s[0] == "gemm":
                        t = s[1]
                        kind = t["kind"]
                        for name, count in t["after"]:
                            pe.wait_ge(by_name[name].sem, by_name[name].at(l, count))
                        slot = t["slot"][0]
                        if kind == "ff":
                            rows_out(slot, take_padded, x_ready(xh, 0), xk(xl), KD).then_inc(mm.sem, mm.tick())
                            cur["b"] += BLK // 2
                        elif kind in ("fq", "fk", "cq", "ckv", "kr", "sq", "sk", "sv", "g"):
                            rows_out(slot, take, xk(xh), xk(xl), KD).then_inc(mm.sem, mm.tick())
                        elif kind == "mq":
                            if t["m"] == 0:
                                pe.wait_ge(xld.sem, xld.at(l, SP_CQ + 2))
                            rows_out(slot, take, xk(lath), xk(latl), 2).then_inc(mm.sem, mm.tick())
                        elif kind == "mk":
                            if t["m"] == 0:
                                pe.wait_ge(xld.sem, xld.at(l, SP_CQ + 3))
                            rows_out(slot, take, lambda k: lath[:, 2, :], lambda k: latl[:, 2, :], 1).then_inc(mm.sem, mm.tick())
                        elif kind == "fv":
                            tokens_out(xk(xh), xk(xl), KD, 512).then_inc(mm.sem, mm.tick())
                        elif kind == "svt":
                            pe.wait_ge(svd.sem, svd.at(l, 1))
                            for tt in range(QTILES):
                                ins = nc.tensor.transpose(ps[slot][:, tt * P:(tt + 1) * P], tmp[:, 0, tok(tt)], ident)
                            ins.then_inc(mm.sem, mm.tick())
                        elif kind == "mv":
                            pe.wait_ge(xld.sem, xld.at(l, SP_CQ + 3))
                            tokens_out(lambda k: lath[:, 2, :], lambda k: latl[:, 2, :], 1, 512).then_inc(mm.sem, mm.tick())
                            cur["b"] += 4
                        elif kind == "y":
                            if t["m"][1] == 0:
                                pe.wait_ge(old.sem, old.at(l, QTILES * (t["m"][0] + 1)))
                            rows_out(slot, take, xk(oth), xk(otl), BRANCH_TILES).then_inc(mm.sem, mm.tick())
                            if t["m"] == PADDED:
                                cur["b"] += 4
                    elif s[0] == "stat":
                        t = s[1]
                        kind = t["kind"]
                        i = t["stat"]
                        pe.wait_ge(statd.sem, statd.at(l, i))
                        pe.wait_ge(sqd.sem, sqd.at(l, t["sqn"] + 1))
                        if kind == "cq":
                            stat(sq[:, 1 - t["par"], :], ones, P, True, False)
                            stat(sq[:, t["par"], :], ones, P, False, True).then_inc(st.sem, st.tick())
                        elif kind == "mk":
                            if t["m"] == 0:
                                pe.wait_ge(krd.sem, krd.at(l, 1))
                            stat(ksq[:, t["par"], :], pair, P, True, False)
                            for j in range(2):
                                ins = nc.tensor.matmul(half(3, j), ones[HD:MQ, :], rope_square[HD:MQ, j * TH:(j + 1) * TH],
                                                       start=False, stop=True)
                            ins.then_inc(st.sem, st.tick())
                        elif kind == "mq":
                            stat(sq[:, t["par"], :], ones, MQ).then_inc(st.sem, st.tick())
                        elif kind == "ckv":
                            stat(ksq[:, t["par"], :], ones, P).then_inc(st.sem, st.tick())
                        else:
                            stat(sq[:, t["par"], :], pair, P).then_inc(st.sem, st.tick())
                    elif s[0] == "S":
                        u = s[1]
                        if u.h == 0 and u.b == QTILES - 1:
                            pe.wait_ge(qkv.sem, qkv.at(l, qkv_end[u.br]))
                            if u.br == FOX:
                                pe.wait_ge(f4.sem, f4.at(l, 32))
                        if u.i % (QTILES * HEADS) < 2:
                            name, count = u.slot_free
                            pe.wait_ge(by_name[name].sem, by_name[name].at(l, count))
                        if u.i >= 2:
                            pe.wait_ge(pd.sem, pd.at(l, u.i - 1))
                        rows = {FOX: HD + 2, MLA: P, SWA: HD}[u.br]
                        kh = u.h // 4 if u.br == SWA else u.h
                        for k0, kn, col in u.ranges:
                            ins = nc.tensor.matmul(ps[u.i % 2][0:u.nq, u.base + col:u.base + col + kn],
                                                   qt[0:rows, u.h, u.q0:u.q0 + P], kt[0:rows, kh, k0:k0 + kn],
                                                   start=True, stop=True)
                        ins.then_inc(sS.sem, sS.tick())
                    elif s[0] == "T":
                        u, p = s[1], s[2]
                        i = u.part_ids[p]
                        pe.wait_ge(pd.sem, pd.at(l, u.i + 1))
                        bank = 0 if u.base == 0 and i % 2 else 3
                        if bank in copied:
                            pe.wait_ge(ptd.sem, ptd.at(l, copied[bank]))
                        copied[bank] = i + 1
                        for j, (kt_i, col) in enumerate(u.parts[p]):
                            ins = nc.tensor.transpose(probs_bank(u, i)[:, j * P:(j + 1) * P],
                                                      probs[:, u.i % 2, col:col + P],
                                                      ident[0:u.nq, 0:u.nq])
                        ins.then_inc(td.sem, td.tick())
                    elif s[0] == "PV":
                        u, p = s[1], s[2]
                        i = u.part_ids[p]
                        pe.wait_ge(ptd.sem, ptd.at(l, i + 1))
                        gi = group_of[(u.br, u.b)]
                        if p == 0 and u.h == 0 and gi > 0:
                            pe.wait_ge(ond.sem, ond.at(l, gi))
                        vh = u.h // 4 if u.br == SWA else u.h
                        for j, (kt_i, col) in enumerate(u.parts[p]):
                            kn = META if kt_i == 0 else P
                            first = p == 0 and j == 0
                            final = p == len(u.parts) - 1 and j == len(u.parts[p]) - 1
                            ins = nc.tensor.matmul(ps[3][0:u.nq, u.h * HD:(u.h + 1) * HD],
                                                   pts[0:kn, i % 2, j * u.nq:(j + 1) * u.nq],
                                                   v[0:kn, kt_i, vh * HD:(vh + 1) * HD], start=first, stop=final)
                        ins.then_inc(pvd.sem, pvd.tick())
                    elif s[0] == "OT":
                        u = s[1]
                        gi = group_of[(u.br, u.b)]
                        pe.wait_ge(ond.sem, ond.at(l, gi + 1))
                        if u.b < QTILES - 2:
                            pe.wait_ge(old.sem, old.at(l, gi - 1))
                        if u.slot_free:
                            name, count = u.slot_free
                            pe.wait_ge(by_name[name].sem, by_name[name].at(l, count))
                        for c in range(BRANCH_TILES):
                            ins = nc.tensor.transpose(heads_bank(gi)[:, c * P:c * P + u.nq],
                                                      osb[0:u.nq, u.b, c * P:(c + 1) * P], ident[0:u.nq, 0:u.nq])
                        ins.then_inc(otd.sem, otd.tick())
                    elif s[0] == "end":
                        pe.wait_ge(pd.sem, pd.at(l, max(u.i for u in units if u.br == s[1]) + 1))
                        pe.wait_ge(old.sem, old.at(l, QTILES * (s[1] + 1)))
                c0 = cur["b"] // BLK
                assert cur["b"] % BLK == 0

                def loop_tile(n, c, first_chunk, slot, x_hi, x_lo, nk, start_chunk):
                    pos = {"b": 0}

                    def blocks():
                        b = pos["b"]
                        pos["b"] += 1
                        cc = c + b // BLK
                        return block_at(cc % SPLIT, b % BLK, n + (start_chunk + cc))
                    return rows_out(slot, blocks, x_hi, x_lo, nk)

                assert c0 % SPLIT == 0, c0
                with pe.Fori(0, WO_TILES - 3, 4) as m:
                    nbase = pe.snap(l * CHUNKS + m)
                    for j in range(4):
                        if j == 1:
                            pe.wait_ge(tmd.sem, tmd.at(l, SP_MERGED + KD))
                        pe.wait_ge(hup.sem, hup.at(l, m + (j - 3)))
                        loop_tile(nbase, j, 0, 3 - j, x_ready(mh, SP_MERGED) if j == 0 else xk(mh), xk(ml), KD, c0).then_inc(mm.sem, mm.tick())
                mm.skip(WO_TILES - 4)
                norm_stat(1)
                c_up = c0 + KD
                with pe.Fori(0, FT - 1, 2) as f:
                    nbase = pe.snap(l * CHUNKS + f * 2)
                    for j in range(4):
                        pe.wait_ge(free.sem, free.at(l, f * 2 + (n_free + j - 3)))
                        if j == 3:
                            pe.wait_ge(statd.sem, statd.at(l, n_stats + 1))
                        loop_tile(nbase, j, 0, j, x_ready(xh, SP_NORM2) if j == 0 else xk(xh), xk(xl), KD,
                                  c_up).then_inc(mm.sem, mm.tick())
                mm.skip(UP_TILES - 4)
                c_dn = c_up + 2 * FT

                def last_ready(k):
                    if k == FT - 1:
                        pe.wait_ge(xld.sem, xld.at(l, SP_FFN + FT))
                    return ah[:, k, :]

                with pe.Fori(0, KD - 3, 4) as m:
                    nbase = pe.snap(l * CHUNKS + m * 3)
                    pe.wait_ge(xld.sem, xld.at(l, SP_FFN + FT - 1))
                    for j in range(4):
                        pe.wait_ge(hup.sem, hup.at(l, m + (WO_TILES + j - 3)))
                        loop_tile(nbase, 3 * j, 0, j, last_ready if j == 0 else xk(ah), xk(al), FT, c_dn).then_inc(mm.sem, mm.tick())
                mm.skip(KD - 4)
                assert c_dn + 3 * KD == CHUNKS

        @blk.vector
        def _(dve):
            def high_part(base, c):
                dve.wait_ge(s_raw[c % RAW], base * (16 // RAW) + 16 * (c // RAW + 1))
                if c >= AHEAD:
                    dve.wait_ge(s_start, base + (c + 2 - SPLIT + STARTED_BEFORE))
                nc.vector.tensor_copy(wh[c % SPLIT][:, :], raw[:, c % RAW, :]).then_inc(s_hi, 1)

            nc.vector.memset(gts[:, 2:3], EPS)
            nc.vector.memset(gts[:, 3:4], -EPS).then_inc(s_ini, 1)
            for k in range(KD):
                dve.wait_ge(hsd.sem, k + 1)
                if k == 0:
                    nc.vector.tensor_copy(ssum[:, :], hsq[:, 0, :]).then_inc(ssd.sem, 1)
                else:
                    dve.wait_ge(ssd.sem, k)
                    nc.vector.tensor_tensor(ssum[:, :], ssum[:, :], hsq[:, k % 2, :], ALU.add).then_inc(ssd.sem, 1)
            for i in range(KD // 2):
                dve.wait_ge(s_hin[i], 16)
            dve.sem_inc(hup.sem, KD)
            dve.wait_ge(s_cst, 16)
            for n in range(AHEAD):
                high_part(0, n)
            with dve.Fori(0, DEPTH) as l:

                rstd_used = []
                split = {"next": AHEAD}

                def split_to(c):
                    for n in range(split["next"], c + AHEAD + 1):
                        high_part(l * CHUNKS, n)
                    split["next"] = max(split["next"], c + AHEAD + 1)

                def newton(stat):
                    dve.wait_ge(guessd.sem, guessd.at(l, stat + 1))
                    s_ = stat % 2
                    nc.vector.scalar_tensor_tensor(
                        out=negmean[:, s_, :], in0=negmean[:, s_, :], scalar=0.5, in1=guess2[:, s_, :],
                        op0=ALU.mult, op1=ALU.mult).then_inc(cd.sem, cd.tick())
                    dve.wait_ge(cd.sem, cd.at(l, cd.n))
                    for used in rstd_used:
                        dve.wait_ge(used.sem, used.at(l, used.n))
                    rstd_used.clear()
                    nc.vector.scalar_tensor_tensor(
                        out=rstd[:, :], in0=negmean[:, s_, :], scalar=1.5, in1=guess[:, s_, :],
                        op0=ALU.add, op1=ALU.mult).then_inc(rsd.sem, rsd.tick())
                    dve.wait_ge(rsd.sem, rsd.at(l, rsd.n))

                def low(out, hi, tile):
                    dve.wait_ge(thd.sem, thd.at(l, xld.n + 1))
                    return nc.vector.tensor_tensor(out, tile, hi.bitcast(F32), ALU.subtract).then_inc(xld.sem, xld.tick())

                def sum_again(stat):
                    dve.wait_ge(guessd.sem, guessd.at(l, stat + 1))
                    nc.vector.memset(ssum[:, :], 0.0)

                def norm_input():
                    newton(0)
                    sum_again(0)
                    rstd_used.append(tmd)

                    def scale(k):
                        if k >= 2:
                            dve.wait_ge(xld.sem, xld.at(l, k - 1))
                        nc.vector.scalar_tensor_tensor(
                            out=tmp[:, k % 2, :], in0=h[:, k, :], scalar=prm[:, PC_N1 + k:PC_N1 + k + 1],
                            in1=rstd[:, :], op0=ALU.mult, op1=ALU.mult).then_inc(tmd.sem, tmd.tick())
                    scale(0)
                    for k in range(KD):
                        if k + 1 < KD:
                            scale(k + 1)
                        low(xl[:, k, :], xh[:, k, :], tmp[:, k % 2, :])

                dve.wait_ge(s_prm, l * 16 + 16)
                dve.wait_ge(s_ini, 1)
                nc.vector.tensor_scalar(gts[:, 0:1], prm[:, PC_FQ:PC_FQ + 1], HD ** -0.5, None, ALU.mult)
                nc.vector.tensor_scalar(gts[:, 1:2], prm[:, PC_SQ:PC_SQ + 1], HD ** -0.5, None, ALU.mult)
                nc.vector.tensor_scalar(nsink[:, :], prm[:, PC_SINK:PC_SINK + HEADS], -1.0, None, ALU.mult).then_inc(cd.sem, cd.tick())
                dve.wait_ge(cd.sem, cd.at(l, cd.n))
                norm_input()
                for s in steps:
                    if s[0] == "stat":
                        t = s[1]
                        kind = t["kind"]
                        src = full(t["slot"][0])
                        newton(t["stat"])
                        rstd_used.append(tmd if kind in ("cq", "ckv") else qkv)
                        if kind in ("fq", "fk", "sq", "sk"):
                            dst = qt if kind in ("fq", "sq") else kt
                            g = {"fq": gts[:, 0:1], "sq": gts[:, 1:2], "fk": prm[:, PC_FK:PC_FK + 1],
                                 "sk": prm[:, PC_SK:PC_SK + 1]}[kind]
                            for e in range(2):
                                r = slice(e * HD, (e + 1) * HD)
                                ins = nc.vector.scalar_tensor_tensor(
                                    out=dst[0:HD, 2 * t["m"] + e, :], in0=src[r, :], scalar=g[r, :],
                                    in1=rstd[r, :], op0=ALU.mult, op1=ALU.mult)
                            ins.then_inc(qkv.sem, qkv.tick())
                        elif kind == "cq":
                            for k in range(2):
                                nc.vector.scalar_tensor_tensor(
                                    out=tmp[:, k, :], in0=latent[:, k, :],
                                    scalar=prm[:, PC_QA + k:PC_QA + k + 1], in1=rstd[:, :],
                                    op0=ALU.mult, op1=ALU.mult).then_inc(tmd.sem, tmd.tick())
                            for k in range(2):
                                low(latl[:, k, :], lath[:, k, :], tmp[:, k, :])
                        elif kind == "ckv":
                            dve.wait_ge(xld.sem, xld.at(l, xld.n))
                            nc.vector.scalar_tensor_tensor(
                                out=tmp[:, 0, :], in0=latent[:, 2, :], scalar=prm[:, PC_KVA:PC_KVA + 1], in1=rstd[:, :],
                                op0=ALU.mult, op1=ALU.mult).then_inc(tmd.sem, tmd.tick())
                            low(latl[:, 2, :], lath[:, 2, :], tmp[:, 0, :])
                        elif kind == "mq":
                            nc.vector.tensor_tensor(tmp[:, t["m"] % 2, :], src, gq[:, :],
                                                                               ALU.mult).then_inc(free.sem, free.tick())
                            dve.wait_ge(free.sem, free.at(l, free.n))
                            nc.vector.tensor_tensor(qt[:, t["m"], :], tmp[:, t["m"] % 2, :], rstd[:, :],
                                                            ALU.mult).then_inc(qkv.sem, qkv.tick())
                        elif kind == "mk":
                            for e in range(2):
                                r = slice(e * HD, (e + 1) * HD)
                                nc.vector.tensor_tensor(kt[HD:P, 2 * t["m"] + e, :], krr[r, :], rstd[r, :], ALU.mult)
                                ins = nc.vector.scalar_tensor_tensor(
                                    out=kt[0:HD, 2 * t["m"] + e, :], in0=src[r, :],
                                    scalar=prm[r, PC_MKN:PC_MKN + 1], in1=rstd[r, :], op0=ALU.mult, op1=ALU.mult)
                            ins.then_inc(qkv.sem, qkv.tick())
                    elif s[0] == "gemm":
                        t = s[1]
                        kind = t["kind"]
                        src = full(t["slot"][0])
                        split_to(t["chunk"])
                        if kind == "ff":
                            dve.wait_ge(mm.sem, mm.at(l, t["g"] + 1))
                            nc.vector.tensor_scalar(fz[0:8, :], src[0:8, :], prm[0:8, PC_FB:PC_FB + 1], None,
                                                             ALU.add).then_inc(free.sem, free.tick())
                            dve.wait_ge(free.sem, free.at(l, free.n))
                            nc.vector.tensor_scalar(fm[0:8, :], fz[0:8, :], 0.0, None, ALU.min).then_inc(f1.sem, f1.tick())
                            dve.wait_ge(f2.sem, f2.at(l, 1))
                            dve.wait_ge(f1.sem, f1.at(l, 1))
                            nc.vector.tensor_tensor(fs[0:8, :], fm[0:8, :], fl[0:8, :], ALU.subtract).then_inc(cd.sem, cd.tick())
                            dve.wait_ge(cd.sem, cd.at(l, cd.n))
                            nc.vector.tensor_tensor_scan(ld[0:8, :], cs[0:8, :], fs[0:8, :], 0.0,
                                                                 ALU.mult, ALU.add).then_inc(cd.sem, cd.tick())
                            dve.wait_ge(cd.sem, cd.at(l, cd.n))
                            nc.vector.tensor_scalar(nld[0:8, :], ld[0:8, :], -1.0, None, ALU.mult).then_inc(cd.sem, cd.tick())
                            dve.wait_ge(cd.sem, cd.at(l, cd.n))
                            nc.vector.memset(qt[HD:HD + 2, :, :], 1.0)
                            nc.vector.memset(kt[HD:HD + 2, :, :], 1.0).then_inc(f3.sem, f3.tick())
                        elif kind == "sv":
                            dve.wait_ge(mm.sem, mm.at(l, t["g"] + 1))
                            nc.vector.tensor_copy(tmp[:, 0, :], src).then_inc(svd.sem, svd.tick())
                        elif kind == "svt":
                            dve.wait_ge(mm.sem, mm.at(l, t["g"] + 1))
                            bank = ps[t["slot"][0]]
                            nc.vector.tensor_copy(v[0:META, 0, 0:P], bank[0:META, 0:P])
                            nc.vector.tensor_copy(
                                v[:, 1:4, 0:P], bank[:, P:4 * P].rearrange("p (a f) -> p a f", a=3))
                            nc.vector.tensor_copy(v[:, 4, 0:P], bank[:, 4 * P:5 * P]).then_inc(qkv.sem, qkv.tick())
                        elif kind in ("fv", "mv"):
                            width = HEADS * HD
                            dve.wait_ge(mm.sem, mm.at(l, t["g"] + 1))
                            for tt in range(QTILES):
                                rows = META if tt == 0 else P
                                ins = nc.vector.tensor_copy(v[0:rows, tt, 0:width], value_bank(tt)[0:rows, 0:width])
                            ins.then_inc(qkv.sem, qkv.tick())
                        elif kind in ("cq", "ckv", "kr"):
                            if rawd.n == 0:
                                dve.wait_ge(f4.sem, f4.at(l, 32))
                            if kind == "kr":
                                dve.wait_ge(mm.sem, mm.at(l, t["g"] + 1))
                            else:
                                dve.wait_ge(sqd.sem, sqd.at(l, t["sqn"] + 1))
                            nc.vector.tensor_copy(latent[:, rawd.n, :], src).then_inc(rawd.sem, rawd.tick())
                        elif kind == "y":
                            br, d = t["m"]
                            dve.wait_ge(mm.sem, mm.at(l, t["g"] + 1))
                            dve.wait_ge(sgd.sem, sgd.at(l, gmd.n + 1))
                            gate = merged[:, d, :] if br == FOX else gsb[:, gmd.n % 2, :]
                            nc.vector.scalar_tensor_tensor(out=gate, in0=gate, scalar=1.0, in1=src,
                                                                   op0=ALU.add, op1=ALU.mult).then_inc(gmd.sem, gmd.tick())
                            if br != FOX:
                                dve.wait_ge(gmd.sem, gmd.at(l, gmd.n))
                                ins = nc.vector.tensor_tensor(merged[:, d, :], merged[:, d, :], gate,
                                                              ALU.add)
                                if br == MLA:
                                    ins.then_inc(addd.sem, addd.tick())
                                    dve.wait_ge(addd.sem, addd.at(l, addd.n))
                                else:
                                    ins.then_inc(tmd.sem, tmd.tick())
                    elif s[0] == "rope":
                        gk = tmp[:, 1, :]
                        dve.wait_ge(xld.sem, xld.at(l, xld.n))
                        nc.vector.tensor_scalar(gq[:, :], cs, prm[:, PC_MQ:PC_MQ + 1], MQ ** -0.5,
                                                ALU.mult, ALU.mult)
                        nc.vector.tensor_scalar(gk, cs, prm[:, PC_MK:PC_MK + 1], None, ALU.mult).then_inc(cd.sem, cd.tick())
                        dve.wait_ge(cd.sem, cd.at(l, cd.n))
                        t1, t2, key = latent[:, 0, :], rstd, latent[:, 3, :]
                        nc.vector.tensor_tensor(t1[HD:MQ, :], key[HD:MQ, :], gk[HD:MQ, :], ALU.mult)
                        nc.vector.tensor_tensor(t2[HD:MQ, :], key[MQ:P, :], gk[MQ:P, :], ALU.mult).then_inc(cd.sem, cd.tick())
                        dve.wait_ge(cd.sem, cd.at(l, cd.n))
                        for r in range(0, P, ROPE):
                            ins = nc.vector.tensor_tensor(krr[r:r + ROPE, :], t1[HD:MQ, :], t2[HD:MQ, :], ALU.add)
                        ins.then_inc(cd.sem, cd.tick())
                        dve.wait_ge(cd.sem, cd.at(l, cd.n))
                    elif s[0] == "end":
                        dve.wait_ge(pvd.sem, pvd.at(l, parts_end[s[1]]))
                    elif s[0] == "merged":
                        low(ml[:, s[1], :], mh[:, s[1], :], merged[:, s[1], :])
                    elif s[0] == "S":
                        u = s[1]
                        gi = group_of[(u.br, u.b)]
                        dve.wait_ge(sS.sem, sS.at(l, u.i + 1))
                        sc = ps[u.i % 2][0:u.nq, u.base:u.base + u.nk]
                        if u.h == 0 and gi >= 2:
                            dve.wait_ge(ond.sem, ond.at(l, gi - 1))
                        if u.br == SWA:
                            if u.b == QTILES - 1 and u.h == 0:
                                dve.wait_ge(s_dist, l * 16 + 16)
                            nc.vector.scalar_tensor_tensor(
                                out=sc, in0=dist[0:u.nq, DIST_AT[u.b]:DIST_AT[u.b + 1]], scalar=-(2.0 ** -(u.h + 1)), in1=sc, op0=ALU.mult, op1=ALU.add).then_inc(cd.sem, cd.tick())
                            dve.wait_ge(cd.sem, cd.at(l, cd.n))
                            nc.vector.tensor_reduce(nraw[0:u.nq, gi % 2, u.h:u.h + 1], sc, AX.X, ALU.max,
                                                            negate=True).then_inc(cd.sem, cd.tick())
                            dve.wait_ge(cd.sem, cd.at(l, cd.n))
                            nc.vector.tensor_tensor(nmax[0:u.nq, gi % 2, u.h:u.h + 1],
                                                            nraw[0:u.nq, gi % 2, u.h:u.h + 1],
                                                            nsink[0:u.nq, u.h:u.h + 1], ALU.min).then_inc(mxd.sem, mxd.tick())
                        else:
                            w = u.end - u.q0
                            dg = sc[:, u.nk - w:u.nk]
                            nc.vector.tensor_tensor(dg, dg, mask[:, 0:w], ALU.add).then_inc(cd.sem, cd.tick())
                            dve.wait_ge(cd.sem, cd.at(l, cd.n))
                            nc.vector.tensor_reduce(nmax[0:u.nq, gi % 2, u.h:u.h + 1], sc, AX.X, ALU.max,
                                                            negate=True).then_inc(mxd.sem, mxd.tick())
                    elif s[0] == "O":
                        u = s[1]
                        gi = group_of[(u.br, u.b)]
                        r = slice(0, u.nq)
                        dve.wait_ge(pd.sem, pd.at(l, u.i + 1))
                        total = rsum
                        if u.br == SWA:
                            nc.vector.tensor_tensor(skx[r, gi % 2, :], nmax[r, gi % 2, :],
                                                            nsink[r, :], ALU.subtract).then_inc(skd.sem, skd.tick())
                            dve.wait_ge(sed.sem, sed.at(l, skd.n))
                            nc.vector.tensor_tensor(rtot[r, gi % 2, :], ske[r, gi % 2, :],
                                                            rsum[r, gi % 2, :], ALU.add).then_inc(cd.sem, cd.tick())
                            dve.wait_ge(cd.sem, cd.at(l, cd.n))
                            total = rtot
                        nc.vector.reciprocal(rinv[r, gi % 2, :], total[r, gi % 2, :]).then_inc(cd.sem, cd.tick())
                        dve.wait_ge(cd.sem, cd.at(l, cd.n))
                        dve.wait_ge(pvd.sem, pvd.at(l, u.part_ids[-1] + 1))
                        nc.vector.tensor_tensor(
                            osb[r, u.b, :].rearrange("p (h d) -> p h d", h=HEADS),
                            ps[3][r, 0:512].rearrange("p (h d) -> p h d", h=HEADS),
                            rinv[r, gi % 2, :].rearrange("p (h a) -> p h a", a=1).broadcast_to([u.nq, HEADS, HD]),
                            ALU.mult).then_inc(ond.sem, ond.tick())
                    elif s[0] == "OT":
                        u = s[1]
                        gi = group_of[(u.br, u.b)]
                        dve.wait_ge(ohd.sem, ohd.at(l, gi + 1))
                        src = heads_bank(gi)[:, :].rearrange("p (c q) -> p c q", c=BRANCH_TILES)[:, :, 0:u.end - u.q0]
                        nc.vector.tensor_tensor(otl[:, :, u.q0:u.end], src,
                                                        oth[:, :, u.q0:u.end].bitcast(F32), ALU.subtract).then_inc(old.sem, old.tick())

                def residual(base_g, base, i, slot, scale):
                    dve.wait_ge(mm.sem, mm.at(l, i + (base_g + 1)))
                    nc.vector.scalar_tensor_tensor(out=tile_of(h, i), in0=full(slot), scalar=scale,
                                                   in1=tile_of(h, i), op0=ALU.mult, op1=ALU.add).then_inc(hup.sem, hup.tick())

                def sum_square(base, i, par):
                    dve.wait_ge(hsd.sem, hsd.at(l, i + (base + 1)))
                    dve.wait_ge(ssd.sem, ssd.at(l, i + base))
                    nc.vector.tensor_tensor(ssum[:, :], ssum[:, :], hsq[:, par, :], ALU.add).then_inc(ssd.sem, ssd.tick())

                c_wo = split["next"]
                assert c_wo == c_out + AHEAD
                assert tmd.n == SP_NORM2 and xld.n == SP_NORM2
                with dve.Fori(0, WO_TILES - 3, 4) as m:
                    for j in range(4):
                        high_part(l * CHUNKS + m, c_wo + j)
                        residual(g_wo, 0, m + j, 3 - j, 0.5)
                        dve.wait_ge(hup.sem, hup.at(l, m + (j + 1)))
                        nc.vector.tensor_scalar(tmp[:, j % 2, :], tile_of(h, m + j), prm[:, bass.ds(m + (PC_N2 + j), 1)],
                                                None, ALU.mult).then_inc(tmd.sem, tmd.tick())
                        sum_square(0, m + j, j % 2)
                        dve.wait_ge(thd.sem, thd.at(l, m + (SP_NORM2 + j + 1)))
                        nc.vector.tensor_tensor(tile_of(xl, m + j), tmp[:, j % 2, :], tile_of(xh, m + j).bitcast(F32),
                                                ALU.subtract).then_inc(xld.sem, xld.tick())
                for s_ in (tmd, xld):
                    s_.skip(WO_TILES - 4)
                for s_ in (hup, ssd):
                    s_.skip(WO_TILES - 4)
                newton(n_stats)
                sum_again(n_stats)
                tm0, x0 = tmd.n, xld.n
                assert tm0 == SP_FFN and x0 == SP_FFN, (tm0, x0)
                with dve.Fori(0, FT - 1, 2) as f:
                    for j in range(2):
                        for side, dst in ((0, cg), (1, cv)):
                            slot = 2 * j + side
                            high_part(l * CHUNKS + f * 2, c_wo + WO_TILES + slot)
                            src = full(slot)
                            cw = f * 3 + (PC_CW + 3 * (side * FT + j))
                            dve.wait_ge(mm.sem, mm.at(l, f * 2 + (g_up + slot + 1)))
                            nc.vector.tensor_tensor(src, src, rstd[:, :], ALU.mult).then_inc(scd.sem, scd.tick())
                            dve.wait_ge(cvd.sem, cvd.at(l, f * 2 + (2 * j + side + 1)))
                            nc.vector.scalar_tensor_tensor(
                                out=dst[:, j, 1:T], in0=src[:, 0:T - 1], scalar=prm[:, bass.ds(cw + 1, 1)],
                                in1=dst[:, j, 1:T], op0=ALU.mult, op1=ALU.add).then_inc(cd.sem, cd.tick())
                            dve.wait_ge(cd.sem, cd.at(l, f * 2 + cd.n))
                            ins = nc.vector.scalar_tensor_tensor(
                                out=dst[:, j, 2:T], in0=src[:, 0:T - 2], scalar=prm[:, bass.ds(cw, 1)],
                                in1=dst[:, j, 2:T], op0=ALU.mult, op1=ALU.add)
                            ins.then_inc(free.sem, free.tick())
                        dve.wait_ge(free.sem, free.at(l, f * 2 + (n_free + 2 * j + 2)))
                        dve.wait_ge(sid.sem, sid.at(l, f + (j + 1)))
                        nc.vector.tensor_tensor(am[:, j, :], si[:, j, :], cv[:, j, :], ALU.mult).then_inc(tmd.sem, tmd.tick())
                        dve.wait_ge(tmd.sem, tmd.at(l, f + (tm0 + j + 1)))
                        dve.wait_ge(thd.sem, thd.at(l, f + (x0 + j + 1)))
                        nc.vector.tensor_tensor(tile_of(al, f + j), am[:, j, :],
                                                        tile_of(ah, f + j).bitcast(F32), ALU.subtract).then_inc(xld.sem, xld.tick())
                for s_, n_ in ((scd, 4), (cd, 4), (free, 4), (tmd, 2), (xld, 2)):
                    s_.skip(n_ * (FT // 2 - 1))
                with dve.Fori(0, KD - 3, 4) as m:
                    for j in range(4):
                        for i in range(3):
                            high_part(l * CHUNKS + m * 3, c_wo + WO_TILES + UP_TILES + 3 * j + i)
                        residual(g_dn, WO_TILES, m + j, j, 1.0)
                        sum_square(WO_TILES, m + j, j % 2)
                for s_ in (hup, ssd):
                    s_.skip(KD - 4)

    return {s.name: s.n for s in signals}


def pack_weights(inp):
    zero = np.zeros((P, P), np.float32)
    half = ROPE // 2

    def block(l, what, k, m):
        w_in = inp["w_in"][l]
        r = slice(k * P, (k + 1) * P)
        at = {"fq": O_FQ, "fk": O_FK, "fv": O_FV, "cq": O_CQ, "ckv": O_CKV, "sq": O_SQ, "sk": O_SK, "sv": O_SV}
        if what == "pad":
            return zero
        if what in at:
            return w_in[r, at[what] + m * P:at[what] + (m + 1) * P]
        out = zero.copy()
        if what == "ff":
            out[:, 0:HEADS] = w_in[r, O_FF:O_FF + HEADS]
        elif what == "kr":
            out[:, HD:MQ] = w_in[r, O_KR:O_KR + ROPE]
            out[:, MQ:MQ + half] = w_in[r, O_KR + half:O_KR + ROPE]
            out[:, MQ + half:P] = w_in[r, O_KR:O_KR + half]
        elif what == "mq":
            w = inp["mla_w_q_up"][l][r, m * MQ:(m + 1) * MQ]
            out[:, 0:MQ] = w
            out[:, MQ:MQ + half] = w[:, HD + half:MQ]
            out[:, MQ + half:P] = w[:, HD:HD + half]
        elif what == "mk":
            for e in range(2):
                c = (2 * m + e) * 2 * HD
                out[:, e * HD:(e + 1) * HD] = inp["mla_w_kv_up"][l][:, c:c + HD]
        elif what == "mv":
            for e in range(2):
                c = (2 * m + e) * 2 * HD + HD
                out[:, e * HD:(e + 1) * HD] = inp["mla_w_kv_up"][l][:, c:c + HD]
        elif what[0] == "g":
            c = O_GATE + int(what[1]) * D + m * P
            out = w_in[r, c:c + P]
        elif what[0] == "y":
            out = inp["w_branch"][l][int(what[1])][r, m * P:(m + 1) * P]
        elif what == "wo":
            out = inp["w_o"][l][r, m * P:(m + 1) * P]
        elif what == "up":
            out = inp["ffn_w_up"][l][r, m * P:(m + 1) * P]
        elif what == "dn":
            out = inp["ffn_w_down"][l][r, m * P:(m + 1) * P]
        return out

    W = np.zeros((DEPTH * CHUNKS + AHEAD, P, CW), np.float32)
    for l in range(DEPTH):
        for i, (what, k, m) in enumerate(PLAN):
            W[l * CHUNKS + i // BLK, :, (i % BLK) * P:(i % BLK + 1) * P] = block(l, what, k, m)
    return W


def pack_params(inp):
    p = np.zeros((DEPTH + 1, P, PC_ALL), np.float32)
    half = ROPE // 2

    def cols(x, n):
        return x.reshape(n, P).T

    for l in range(DEPTH):
        p[l, :, PC_N1:PC_N1 + KD] = cols(inp["norm1_g"][l], KD)
        p[l, :, PC_N2:PC_N2 + KD] = cols(inp["norm2_g"][l], KD)
        for c, name in ((PC_FQ, "fox_q_g"), (PC_FK, "fox_k_g"), (PC_SQ, "swa_q_g"), (PC_SK, "swa_k_g")):
            p[l, :HD, c] = inp[name][l]
            p[l, HD:, c] = inp[name][l]
        p[l, :, PC_QA:PC_QA + 2] = cols(inp["mla_q_a_g"][l], 2)
        p[l, :, PC_KVA] = inp["mla_kv_a_g"][l]
        for c, name in ((PC_MQ, "mla_q_g"), (PC_MK, "mla_k_g")):
            g = inp[name][l]
            p[l, :MQ, c] = g
            p[l, MQ:MQ + half, c] = g[HD + half:]
            p[l, MQ + half:, c] = g[HD:HD + half]
        for e in range(2):
            p[l, e * HD:(e + 1) * HD, PC_MKN] = inp["mla_k_g"][l][:HD]
        p[l, :HEADS, PC_FB] = inp["fox_forget_b"][l]
        p[l, :, PC_SINK:PC_SINK + HEADS] = inp["swa_sinks"][l][None, :]
        for i in range(3):
            p[l, :, PC_CW + i:PC_CB:3] = cols(inp["ffn_conv_w"][l][i], 2 * FT)
        p[l, :, PC_CB:PC_ALL] = cols(inp["ffn_conv_b"][l], 2 * FT)
    return p


def kernel(**inputs):
    import concourse.bacc as bacc
    from concourse.bass_utils import run_bass_kernel_spmd

    inp = {k: np.asarray(v) for k, v in inputs.items()}
    tokens = np.concatenate([inp["meta_tokens"], inp["x"][0]], axis=0)
    arrays = {
        "weights": pack_weights(inp),
        "tokens": np.ascontiguousarray(tokens.T.reshape(KD, P, T).transpose(1, 0, 2)),
        "params": pack_params(inp),
        "constants": constants(),
        "distances": alibi_tables(),
    }

    def program(counts):
        nc = bacc.Bacc("TRN2", target_bir_lowering=False, num_devices=1, dynamic_dma_scratch_size=2048)
        args = [nc.dram_tensor(n, a.shape, F32, kind="ExternalInput").ap() for n, a in arrays.items()]
        args.append(nc.dram_tensor("out", (P, KD, SEQ), F32, kind="ExternalOutput").ap())
        return nc, build(nc, *args, counts)

    _, counts = program({})
    nc, again = program(counts)
    assert again == counts
    r = run_bass_kernel_spmd(nc, [arrays], core_ids=[0])
    out = r.results[0]["out"]
    return np.ascontiguousarray(out.transpose(2, 1, 0)).reshape(1, SEQ, D)
```

```python
import concourse.bass as bass
import numpy as np
from concourse import mybir

F32 = mybir.dt.float32
F32R = mybir.dt.float32r
ALU = mybir.AluOpType
ACT = mybir.ActivationFunctionType
AX = mybir.AxisListType

P = 128
D = 1024
DEPTH = 2
SEQ = 512
META = 16
T = META + SEQ
TH = T // 2
KD = D // P
HEADS = 8
HD = 64
ROPE = 32
MQ = HD + ROPE
D_FF = 2816
FT = D_FF // P
EPS = 1e-6
NEG = -1.0e30
BRANCH_TILES = HEADS * HD // P
QTILES = 1 + SEQ // P
FOX, MLA, SWA = range(3)

BLK = 8
CW = BLK * P
RAW, SPLIT = 2, 4
STARTED_BEFORE = 2
AHEAD = 2

OFF = np.cumsum([0, 512, 512, 512, 8, 256, 128, 32, 512, 128, 128])
O_FQ, O_FK, O_FV, O_FF, O_CQ, O_CKV, O_KR, O_SQ, O_SK, O_SV, O_GATE = (int(v) for v in OFF)

PC_N1, PC_N2 = 0, 8
PC_FQ, PC_FK, PC_QA, PC_KVA, PC_MQ, PC_MK, PC_SQ, PC_SK, PC_FB = 16, 17, 18, 20, 21, 22, 23, 24, 25
PC_SINK = 26
PC_MKN = 34
PC_CW = 35
PC_CB = PC_CW + 3 * 2 * FT
PC_ALL = PC_CB + 2 * FT

CC_ID, CC_ONE, CC_PAIR, CC_MASK, CC_CS, CC_ALL = 0, 128, 256, 384, 512, 512 + T
DW = META + 2 * P
DIST_AT = [0, META]
for _b in range(2, QTILES + 1):
    DIST_AT.append(DIST_AT[-1] + (META + P if _b == 2 else DW))


SQUARED = {"fq": P, "fk": P, "sq": P, "sk": P, "cq": P, "ckv": P, "mq": MQ, "mk": P}
MEAN_OF = {"fq": HD, "fk": HD, "sq": HD, "sk": HD, "cq": 2 * P, "ckv": P, "mq": MQ, "mk": MQ}
LATE_SPAN = 0.93
OT_DELAY = 2
EARLY = 4
PADDED = (FOX, EARLY - 1)
TILE_BLOCKS = {"ff": 2 * BLK, "fv": 4 * KD, "fq": KD, "fk": KD, "cq": KD, "ckv": KD, "kr": KD, "mv": BLK, "mq": 2,
               "mk": 1, "sv": KD, "svt": 0, "sq": KD, "sk": KD, "g": KD, "y": BRANCH_TILES}
FILL_SPAN = 0.75
SP_CQ = KD
SP_MERGED = SP_CQ + 3
SP_NORM2 = SP_MERGED + KD
SP_FFN = SP_NORM2 + KD


def alibi_tables():
    i = np.arange(P)[:, None]
    out = []
    for b in range(1, QTILES):
        qpos = META + (b - 1) * P + i
        meta = qpos - np.arange(META)[None, :]
        lo = META + (b - 2) * P
        kpos = lo + np.arange(2 * P)[None, :]
        dist = qpos - kpos
        ok = (dist >= 0) & (dist < P) & (kpos >= META)
        band = np.where(ok, dist, -NEG)
        if b == 1:
            band = band[:, P:]
        out.append(np.concatenate([meta, band], axis=1))
    m = np.arange(META)
    dm = np.zeros((P, META))
    dm[:META] = np.where(m[:, None] >= m[None, :], m[:, None] - m[None, :], -NEG)
    return np.concatenate([dm] + out, axis=1).astype(np.float32)


def constants():
    c = np.zeros((P, CC_ALL), np.float32)
    c[:, CC_ID:CC_ID + P] = np.eye(P)
    c[:, CC_ONE:CC_ONE + P] = 1.0
    c[:HD, CC_PAIR:CC_PAIR + HD] = 1.0
    c[HD:, CC_PAIR + HD:CC_PAIR + P] = 1.0
    c[:, CC_MASK:CC_MASK + P] = np.where(np.arange(P)[None, :] <= np.arange(P)[:, None], 0.0, NEG)
    half = ROPE // 2
    freqs = np.float32(10000.0) ** (-np.arange(half, dtype=np.float32) / np.float32(half))
    ang = (np.arange(T, dtype=np.float32)[:, None] * freqs[None, :]).T.astype(np.float32)
    cos, sin = np.cos(ang), np.sin(ang)
    c[:, CC_CS:CC_CS + T] = 1.0
    c[HD:MQ, CC_CS:CC_CS + T] = np.concatenate([cos, cos])
    c[MQ:P, CC_CS:CC_CS + T] = np.concatenate([-sin, sin])
    return c


class Signal:

    def __init__(self, nc, name, counts, before=0):
        self.sem = nc.alloc_semaphore(name)
        self.name, self.n = name, 0
        self.before = before
        self.per_layer = counts.get(name, 10 ** 5)

    def tick(self, by=1):
        self.n += by
        return by

    def skip(self, n):
        self.n += n

    def at(self, layer, n):
        return layer * self.per_layer + (n + self.before)


class Unit:

    def __init__(self, i, br, b, h):
        self.i, self.br, self.b, self.h = i, br, b, h
        self.nq = P
        self.q0 = 0 if b == 0 else META + (b - 1) * P
        self.end = META if b == 0 else self.q0 + P
        if br == SWA and b > 2:
            self.ranges = [(0, META, 0), (self.q0 - P, 2 * P, META)]
            self.nk = DW
            tiles = [(0, 0), (b - 1, META), (b, META + P)]
        else:
            self.nk = self.end
            self.ranges = [(0, self.nk, 0)] if self.nk <= 512 else [(0, TH, 0), (TH, TH, TH)]
            tiles = [(t, 0 if t == 0 else META + (t - 1) * P) for t in range(b + 1)]
        self.base = 512 - TH if self.nk > 512 else 0
        n = len(tiles)
        cut = n if n <= 4 else 3
        self.parts = [tiles[:cut]] + ([tiles[cut:]] if cut < n else [])
        self.part_ids = []


def schedule():
    steps = []
    tiles = {"n": 0, "blocks": 0}
    units = []
    parts = {"n": 0}
    stats = {"n": 1}
    squares = {"n": 0, "mine": {}}

    def gemm(kind, m=0, stat=False):
        t = dict(kind=kind, m=m, g=tiles["n"], slot=None, stat=None)
        tiles["blocks"] += TILE_BLOCKS[kind]
        t["chunk"] = (tiles["blocks"] - 1) // BLK
        if stat:
            t["stat"] = stats["n"]
            stats["n"] += 1
        tiles["n"] += 1
        if kind == "y" and m == PADDED:
            tiles["blocks"] += 4
        if kind in SQUARED:
            ring = "k" if kind in ("mk", "ckv") else "a"
            mine = squares["mine"].setdefault(ring, [])
            t["sqn"], t["par"] = squares["n"], len(mine) % 2
            squares["n"] += 1
            mine.append(t)
            t["prev"] = mine[-3] if len(mine) > 2 else None
        return t

    def attention(br, fillers, late=()):
        us = []
        for b in range(QTILES - 1, -1, -1):
            for h in range(HEADS):
                u = Unit(len(units), br, b, h)
                units.append(u)
                us.append(u)
        fill = list(fillers) + list(late)
        pending = []
        weights = [0.0]
        for u in us:
            weights.append(weights[-1] + 0.5 + u.nk / 264)
        done = 0
        for u in us[:2]:
            steps.append(("S", u))
            steps.append(("E", u))
        behind = []
        filled = []
        if late and not fillers or br == MLA:
            filled.append(gemm(*fill[0]))
            steps.append(("gemm", filled[-1]))
            done = 1

        def product(j):
            u, p = behind.pop(0)
            steps.append(("PV", u, p))
            if p == len(u.parts) - 1 and u.h == HEADS - 1:
                steps.append(("O", u))
                pending.append((u, j))

        for j, u in enumerate(us):
            if j + 2 < len(us):
                steps.append(("S", us[j + 2]))
            part = weights[j + 1] / weights[-1]
            want = min(len(fillers), int(len(fillers) * part / FILL_SPAN + 1e-9))
            if want == len(fillers) and late:
                begin = FILL_SPAN if fillers else 0.0
                want += min(len(late), max(0, int(len(late) * (part - begin) / (LATE_SPAN - begin) + 1e-9)))
            for p in range(len(u.parts)):
                u.part_ids.append(parts["n"])
                parts["n"] += 1
                steps.append(("T", u, p))
                if p == len(u.parts) - 1 and j + 2 < len(us):
                    steps.append(("E", us[j + 2]))
                if done < want:
                    filled.append(gemm(*fill[done]))
                    steps.append(("gemm", filled[-1]))
                    done += 1
                if behind:
                    product(j)
                behind.append((u, p))
            while done < want:
                filled.append(gemm(*fill[done]))
                steps.append(("gemm", filled[-1]))
                done += 1
            while pending and done >= len(fillers) and j >= pending[0][1] + OT_DELAY:
                steps.append(("OT", pending.pop(0)[0]))
        product(len(us))
        for u, _ in pending:
            steps.append(("OT", u))
        steps.append(("end", br))
        return filled

    def project(kinds, more=()):
        late = []
        for t in kinds:
            if t["kind"] == "mv":
                while late:
                    steps.append(("stat", late.pop(0)))
            steps.append(("gemm", t))
            if late:
                steps.append(("stat", late.pop(0)))
            if t["stat"] is not None:
                late.append(t)
        for t in more:
            steps.append(("gemm", t))
            while late:
                steps.append(("stat", late.pop(0)))
        for t in late:
            steps.append(("stat", t))

    def gate_branch(br, first=0):
        out = []
        for d in range(first, KD):
            out += [("g", (br, d)), ("y", (br, d))]
        return out

    front = ([gemm("ff"), gemm("fv")] + [gemm("fq", m, True) for m in range(4)]
             + [gemm("fk", m, True) for m in range(4)] + [gemm("cq", 0), gemm("cq", 1)])
    latents = front[-2:]
    latents[1]["stat"] = stats["n"]
    stats["n"] += 1
    project(front[:-2], latents)
    latents += attention(FOX, (), [("ckv", 0, True), ("kr",)] + [("g", (FOX, d)) for d in range(EARLY)])
    steps.append(("stat", latents[1]))
    steps.append(("gemm", gemm("y", (FOX, 0))))
    steps.append(("stat", latents[2]))
    steps.append(("gemm", gemm("y", (FOX, 1))))
    steps.append(("rope", latents[3]))
    a = [gemm("mv")]
    for h in range(HEADS):
        a.append(gemm("mq", h, True))
        if h == 3:
            a.append(gemm("y", (FOX, 2)))
    a += [gemm("mk", m, True) for m in range(HEADS // 2)]
    project(a, [gemm("y", (FOX, EARLY - 1)), gemm("g", (FOX, EARLY))])
    attention(MLA, gate_branch(FOX, EARLY)[1:], [("sv",)])
    project([gemm("sq", 0, True), gemm("svt")] + [gemm("sq", m, True) for m in range(1, 4)]
            + [gemm("sk", 0, True)], [gemm("g", (MLA, 0))])
    attention(SWA, gate_branch(MLA)[1:], [("g", (SWA, 0)), ("g", (SWA, 1))])
    last = gate_branch(SWA)
    for kind, m in [last[1]] + [t for d in range(2, KD) for t in (last[2 * d], last[2 * d - 1])] + [last[-1]]:
        steps.append(("gemm", gemm(kind, m)))
        if kind == "y" and m[1] > 0:
            steps.append(("merged", m[1] - 1))
    steps.append(("merged", KD - 1))
    inside = False
    ring = 0
    for s in steps:
        if s[0] == "S":
            inside = True
        elif s[0] == "end":
            inside = False
            ring = 0
        elif s[0] == "gemm":
            t = s[1]
            if t["kind"] in ("fv", "mv"):
                t["slot"] = (0, 1, 2)
            elif inside:
                t["slot"] = (2,)
            else:
                t["slot"] = (ring % 3,)
                ring += 1
    last = {}
    for s in steps:
        if s[0] == "gemm":
            t = s[1]
            t["after"] = sorted({last[x] for x in t["slot"] if x in last})
            for x in t["slot"]:
                last[x] = t["g"]
    order = {"tile_freed": 0, "latent_copied": 0, "window_values_copied": 0,
             "qkv_written": 0, "fp32_ready": KD, "gate_ready": 0, "gate_used": 0}
    freed = {}

    def frees(t, name, by=1):
        order[name] += by
        freed[t["g"]] = (name, order[name])

    for s in steps:
        if s[0] == "gemm":
            t = s[1]
            if t["kind"] == "ff":
                frees(t, "tile_freed")
            elif t["kind"] in ("cq", "ckv", "kr"):
                frees(t, "latent_copied")
            elif t["kind"] == "sv":
                frees(t, "window_values_copied")
            elif t["kind"] in ("fv", "mv", "svt"):
                frees(t, "qkv_written")
            elif t["kind"] == "g":
                frees(t, "gate_ready")
            elif t["kind"] == "y":
                frees(t, "gate_used")
        elif s[0] == "stat":
            t = s[1]
            if t["kind"] == "mq":
                frees(t, "tile_freed")
                order["qkv_written"] += 1
            elif t["kind"] not in ("cq", "ckv"):
                frees(t, "qkv_written")
    filler, transposed, before = None, 0, []
    for s in steps:
        if s[0] == "gemm":
            before.append(s[1])
            if filler is None and 2 in s[1]["slot"] and transposed:
                s[1]["behind_ot"] = transposed
            if 2 in s[1]["slot"]:
                filler = s[1]
        elif s[0] == "S" and s[1].i % (QTILES * HEADS) < 2:
            s[1].slot_free = freed[[x for x in before if s[1].i % 2 in x["slot"]][-1]["g"]]
        elif s[0] == "OT":
            s[1].slot_free = freed[filler["g"]] if filler else None
            filler = None
            transposed += 1
    for s in steps:
        if s[0] == "gemm":
            latest = {}
            for name, count in (freed[g] for g in s[1]["after"]):
                latest[name] = max(count, latest.get(name, 0))
            if "behind_ot" in s[1]:
                latest["heads_low"] = s[1]["behind_ot"]
            s[1]["after"] = list(latest.items())
    n_free = order["tile_freed"]
    return steps, units, tiles["n"], stats["n"], n_free


def stream_plan(steps):
    b = []
    pad = [("pad", 0, 0)]

    def tile(what, rows, m):
        b.extend((what, k, m) for k in range(rows))

    for s in steps:
        if s[0] != "gemm":
            continue
        kind, m = s[1]["kind"], s[1]["m"]
        if kind == "ff":
            tile("ff", 4, 0)
            b.extend(pad * 4 + [("ff", k, 0) for k in range(4, KD)] + pad * 4)
        elif kind == "fv":
            b.extend(("fv", k, c) for k in range(KD) for c in range(4))
        elif kind == "mv":
            b.extend([("mv", 0, c) for c in range(4)] + pad * 4)
        elif kind in ("g", "y"):
            tile(f"{kind}{m[0]}", TILE_BLOCKS[kind], m[1])
            if kind == "y" and m == PADDED:
                b.extend(pad * 4)
        elif kind != "svt":
            tile(kind, TILE_BLOCKS[kind], m)
    for m in range(KD):
        tile("wo", KD, m)
    for f in range(FT):
        tile("up", KD, f)
        tile("up", KD, FT + f)
    for m in range(KD):
        tile("dn", FT, m)
        b.extend(pad * 2)
    assert len(b) % (BLK * 4) == 0
    return b


PLAN = stream_plan(schedule()[0])
CHUNKS = len(PLAN) // BLK


def build(nc, W, H, PRM, CST, DIST, OUT, counts):
    steps, units, n_tiles, n_stats, n_free = schedule()

    at = [(nc.sbuf_base + 63) // 64 * 64]

    def sb(name, shape, dt=F32, offset=None):
        size = int(np.prod(shape[1:])) * 4
        if offset is None:
            offset = at[0]
            at[0] += (size + 31) // 32 * 32
        t = nc.alloc_sbuf_tensor_at(name, shape, dt, offset=offset)
        return t

    h = sb("h", [P, KD, T])
    xh = sb("xh", [P, KD, T], F32R)
    xl = sb("xl", [P, KD, T], F32R)
    raw = sb("raw", [P, RAW, CW])
    wh = [sb(f"wh{i}", [P, CW], F32R) for i in range(SPLIT)]
    wl = [sb(f"wl{i}", [P, CW], F32R) for i in range(SPLIT)]
    attn_at = at[0]
    qt = sb("qt", [P, HEADS, T])
    kt = sb("kt", [P, HEADS, T])
    mh = sb("mh", [P, KD, T], F32R, offset=attn_at)
    ml = sb("ml", [P, KD, T], F32R, offset=attn_at + KD * T * 4)
    v = sb("v", [P, QTILES, HEADS * HD])
    oth = sb("oth", [P, BRANCH_TILES, T], F32R)
    otl = sb("otl", [P, BRANCH_TILES, T], F32R)
    merged_at = at[0]
    merged = sb("merged", [P, KD, T])
    merged_end = at[0]
    at[0] = merged_at
    fz, fa, fe, fl, fm, fs, ld, nld = (sb(f"dec{i}", [P, T]) for i in range(8))
    at[0] = merged_end
    latent = merged[:, EARLY:, :]
    rope_square = latent[:, 2, :]
    probs = sb("probs", [P, 2, T])
    pts_at = at[0]
    pts = sb("pts", [P, 2, 512])
    osb = sb("osb", [P, QTILES, 512])
    lath = sb("lath", [P, 3, T], F32R, offset=pts_at)
    latl = sb("latl", [P, 3, T], F32R, offset=pts_at + 3 * T * 4)
    assert pts_at + 6 * T * 4 <= at[0]
    gq = sb("gq", [P, T])
    krr = sb("krr", [P, T])
    ksq = sb("ksq", [P, 2, T])
    end_attn = at[0]
    at[0] = attn_at
    ah = sb("ah", [P, FT, T], F32R)
    al = sb("al", [P, FT, T], F32R)
    at[0] = max(at[0], end_attn)
    tmp_at = at[0]
    sq = sb("sq", [P, 2, T])
    guess = sb("guess", [P, 2, T])
    guess2 = probs
    negmean = sb("negmean", [P, 2, T])
    tmp = sb("tmp", [P, 2, T])
    end_tmp = at[0]
    at[0] = tmp_at
    cg = sb("cg", [P, 2, T])
    cv = sb("cv", [P, 2, T])
    si = sb("si", [P, 2, T])
    am = sb("am", [P, 2, T])
    at[0] = max(at[0], end_tmp)
    rstd = sb("rstd", [P, T])
    ssum = sb("ssum", [P, T])
    hsq = sq
    gsb = tmp
    dist = kt[:, 2:4, :].rearrange("p a t -> p (a t)")
    cst = sb("cst", [P, CC_ALL])
    prm = sb("prm", [P, PC_ALL])
    gts = sb("gts", [P, 4])
    nmax = sb("nmax", [P, 2, HEADS])
    nraw = sb("nraw", [P, 2, HEADS])
    rsum = sb("rsum", [P, 2, HEADS])
    skx = sb("skx", [P, 2, HEADS])
    ske = sb("ske", [P, 2, HEADS])
    rtot = sb("rtot", [P, 2, HEADS])
    rinv = sb("rinv", [P, 2, HEADS])
    nsink = sb("nsink", [P, HEADS])
    assert at[0] <= nc.sbuf_usable_end, at[0]

    ps = [nc.alloc_psum_tensor(f"ps{i}", [P, 1024], F32) for i in range(4)]

    ident = cst[:, CC_ID:CC_ID + P]
    ones = cst[:, CC_ONE:CC_ONE + P]
    pair = cst[:, CC_PAIR:CC_PAIR + P]
    mask = cst[:, CC_MASK:CC_MASK + P]
    cs = cst[:, CC_CS:CC_CS + T]
    CENTRE = 512 - TH

    def full(slot):
        return ps[slot][:, CENTRE:CENTRE + T]

    def half(slot, j):
        return ps[slot][:, CENTRE + j * TH:CENTRE + (j + 1) * TH]

    def heads_bank(gi):
        return ps[2][:, (gi % 2) * 512:(gi % 2) * 512 + 512]

    def probs_bank(u, part):
        return ps[0 if u.base == 0 and part % 2 else 3][:, 512:1024]

    def value_bank(tt):
        return ps[tt // 2][:, (tt % 2) * 512:(tt % 2) * 512 + 512]

    def S(name, before=0):
        s = Signal(nc, name, counts, before)
        signals.append(s)
        return s

    signals = []
    s_cst = nc.alloc_semaphore("constants_loaded")
    s_hin = [nc.alloc_semaphore(f"input_loaded{i}") for i in range(KD // 2)]
    s_prm = nc.alloc_semaphore("params_loaded")
    s_out = nc.alloc_semaphore("output_stored")
    s_raw = [nc.alloc_semaphore(f"chunk_loaded{i}") for i in range(RAW)]
    s_hi = nc.alloc_semaphore("chunk_high_part")
    s_w = nc.alloc_semaphore("chunk_split")
    s_start = nc.alloc_semaphore("chunk_started")
    s_ini = nc.alloc_semaphore("eps_set")
    s_dist = nc.alloc_semaphore("distances_loaded")
    tile_ready = S("tile_ready")
    stat_ready = S("stat_ready")
    tile_freed = S("tile_freed")
    square_ready = S("square_ready")
    statistic_read = S("statistic_read")
    guess_ready = S("rsqrt_guess_ready")
    rsqrt_ready = S("rsqrt_ready")
    sum_ready = S("sum_squares_ready", KD)
    residual_squared = S("residual_square", KD)
    residual_updated = S("residual_updated", KD)
    fp32_ready = S("fp32_ready")
    high_ready = S("high_part_ready")
    low_ready = S("low_part_ready")
    scores_ready = S("scores_ready")
    max_ready = S("max_ready")
    probs_ready = S("probs_ready")
    probs_transposed = S("probs_transposed")
    transposed_copied = S("transposed_copied")
    pv_done = S("pv_done")
    sink_shifted = S("sink_sum")
    sink_exp_ready = S("sink_exp")
    heads_normalised = S("heads_normalised")
    heads_transposed = S("heads_transposed")
    heads_high = S("head_high_part")
    heads_low = S("head_low_part")
    decay_logit = S("decay_logit")
    decay_log1p = S("decay_log1p")
    decay_summed = S("decay_summed")
    decay_placed = S("decay_rows_placed")
    rope_key_squared = S("rope_key_squared")
    qkv_written = S("qkv_written")
    latent_copied = S("latent_copied")
    window_values_copied = S("window_values_copied")
    gate_ready = S("gate_ready")
    gate_added = S("gated_tile_added")
    gate_used = S("gate_used")
    up_tile_scaled = S("up_tile_scaled")
    conv_scaled = S("conv_scaled")
    silu_ready = S("silu_ready")
    act_chain = S("act_chain")
    dve_chain = S("dve_chain")
    WO_TILES = KD
    UP_TILES = 2 * FT
    c_out = max(s[1]["chunk"] for s in steps if s[0] == "gemm") + 1
    g_wo, g_up = n_tiles, n_tiles + WO_TILES
    g_dn = g_up + UP_TILES

    group_of = {}
    groups = []
    for u in units:
        if u.h == 0:
            groups.append((u.br, u.b))
        group_of[(u.br, u.b)] = len(groups) - 1
    per_branch = QTILES
    qkv_end = {}
    n = 0
    for s in steps:
        if s[0] == "gemm" and s[1]["kind"] in ("fq", "fk", "fv", "mq", "mk", "mv", "sq", "sk", "svt"):
            n += 1
        if s[0] == "end":
            qkv_end[s[1]] = n
    parts_end = {}
    for u in units:
        parts_end[u.br] = max(parts_end.get(u.br, 0), max(u.part_ids) + 1)
    last_y, stat_of = {}, {}
    for s in steps:
        if s[0] == "stat":
            stat_of[s[1]["g"]] = s[1]["stat"]
            if s[1]["kind"] == "cq":
                stat_of[s[1]["g"] - 1] = s[1]["stat"]
    for s in steps:
        if s[0] == "gemm" and s[1]["kind"] == "y":
            last_y[s[1]["m"][0]] = s[1]["g"]
    by_name = {"tile_freed": tile_freed, "heads_low": heads_low, "latent_copied": latent_copied,
               "window_values_copied": window_values_copied, "qkv_written": qkv_written,
               "fp32_ready": fp32_ready, "gate_ready": gate_ready, "gate_used": gate_used}

    def tile_of(t, i):
        if isinstance(i, int):
            return t[:, i, :]
        return t[:, bass.ds(i, 1), :].rearrange("p a t -> p (a t)")


    block = nc.Block()
    with block as blk:

        @blk.sync
        def _(sp):
            def load(n, s):
                sp.dma_start(raw[:, s, :], W[n, :, :]).then_inc(s_raw[s], 16)

            for k in range(0, KD, 2):
                sp.dma_start(h[:, k:k + 2, :], H[:, k:k + 2, :]).then_inc(s_hin[k // 2], 16)
            sp.dma_start(cst[:, :], CST[:, :]).then_inc(s_cst, 16)
            for s in range(RAW):
                load(s, s)
            with sp.Fori(RAW, DEPTH * CHUNKS + AHEAD - RAW + 1, RAW) as n:
                for s in range(RAW):
                    sp.wait_ge(s_w, n + (s + 1 - RAW))
                    load(n + s, s)
            for k in range(KD):
                sp.wait_ge(residual_updated.sem, residual_updated.at(DEPTH - 1, WO_TILES + k + 1))
                sp.dma_start(OUT[:, k, :], h[:, k, META:T]).then_inc(s_out, 16)
            sp.wait_ge(s_out, 16 * KD)

        @blk.gpsimd
        def _(pool):
            with pool.Fori(0, DEPTH * CHUNKS - SPLIT + 1, SPLIT) as n:
                for s in range(SPLIT):
                    pool.wait_ge(s_hi, n + (s + 1))
                    nc.gpsimd.tensor_tensor(wl[s][:, :], raw[:, s % RAW, :], wh[s][:, :].bitcast(F32),
                                            ALU.subtract).then_inc(s_w, 1)

        @blk.scalar
        def _(act):
            def split_high(l, count, out, in_):
                act.wait_ge(fp32_ready.sem, fp32_ready.at(l, count))
                nc.scalar.activation(out, in_, ACT.Copy).then_inc(high_ready.sem, high_ready.tick())

            def rsqrt_guess(l, n, stat):
                act.wait_ge(stat_ready.sem, stat_ready.at(l, stat + 1))
                if stat > 1:
                    act.wait_ge(rsqrt_ready.sem, rsqrt_ready.at(l, stat - 1))
                s_ = stat % 2
                nc.scalar.activation(guess[:, s_, :], full(3), ACT.Abs_reciprocal_sqrt,
                                     scale=1.0 / n, bias=gts[:, 2:3]).then_inc(act_chain.sem, act_chain.tick())
                nc.scalar.activation(negmean[:, s_, :], full(3), ACT.Identity, scale=-1.0 / n,
                                     bias=gts[:, 3:4]).then_inc(statistic_read.sem, statistic_read.tick())
                act.wait_ge(act_chain.sem, act_chain.at(l, act_chain.n))
                nc.scalar.activation(guess2[:, s_, :], guess[:, s_, :], ACT.Square).then_inc(
                        guess_ready.sem, guess_ready.tick())

            act.dma_start(prm[:, :], PRM[0, :, :]).then_inc(s_prm, 16)
            act.wait_ge(s_ini, 1)
            for k in range(KD):
                if k % 2 == 0:
                    act.wait_ge(s_hin[k // 2], 16)
                if k >= 2:
                    act.wait_ge(sum_ready.sem, k - 1)
                nc.scalar.activation(hsq[:, k % 2, :], h[:, k, :], ACT.Square).then_inc(residual_squared.sem, 1)
            with act.Fori(0, DEPTH) as l:

                def norm_input():
                    rsqrt_guess(l, D, 0)
                    for k in range(KD):
                        split_high(l, k + 1, xh[:, k, :], tmp[:, k % 2, :])

                def attn(s):
                    kind, u = s[0], s[1]
                    if kind == "E":
                        act.wait_ge(max_ready.sem, max_ready.at(l, u.i + 1))
                        if u.i >= 2:
                            act.wait_ge(probs_transposed.sem, probs_transposed.at(l, units[u.i - 2].part_ids[-1] + 1))
                        nc.scalar.activation(
                            probs[0:u.nq, u.i % 2, 0:u.nk], ps[u.i % 2][0:u.nq, u.base:u.base + u.nk], ACT.Exp,
                            bias=nmax[0:u.nq, group_of[(u.br, u.b)] % 2, u.h:u.h + 1],
                            accum_out=rsum[0:u.nq, group_of[(u.br, u.b)] % 2, u.h:u.h + 1]).then_inc(
                                    probs_ready.sem, probs_ready.tick())
                    elif kind == "T":
                        i = u.part_ids[s[2]]
                        act.wait_ge(probs_transposed.sem, probs_transposed.at(l, i + 1))
                        if i >= 2:
                            act.wait_ge(pv_done.sem, pv_done.at(l, i - 1))
                        w = len(u.parts[s[2]]) * u.nq
                        nc.scalar.activation(pts[:, i % 2, 0:w], probs_bank(u, i)[:, 0:w], ACT.Copy).then_inc(
                                transposed_copied.sem, transposed_copied.tick())
                    elif kind == "O":
                        gi = group_of[(u.br, u.b)]
                        if u.br == SWA:
                            act.wait_ge(sink_shifted.sem, sink_shifted.at(l, sink_exp_ready.n + 1))
                            nc.scalar.activation(ske[:, gi % 2, :], skx[:, gi % 2, :], ACT.Exp).then_inc(
                                    sink_exp_ready.sem, sink_exp_ready.tick())
                    elif kind == "OT":
                        gi = group_of[(u.br, u.b)]
                        act.wait_ge(heads_transposed.sem, heads_transposed.at(l, gi + 1))
                        if u.b == QTILES - 1 and u.br != FOX:
                            act.wait_ge(tile_ready.sem, tile_ready.at(l, last_y[u.br - 1] + 1))
                        src = heads_bank(gi)[:, :].rearrange("p (c q) -> p c q", c=BRANCH_TILES)[:, :, 0:u.end - u.q0]
                        nc.scalar.activation(oth[:, :, u.q0:u.end], src, ACT.Copy).then_inc(
                                heads_high.sem, heads_high.tick())

                norm_input()
                for s in steps:
                    if s[0] in ("E", "T", "O", "OT"):
                        attn(s)
                    elif s[0] == "end" and s[1] == MLA:
                        act.wait_ge(pv_done.sem, pv_done.at(l, parts_end[MLA]))
                        act.dma_start(dist[:, 0:DIST_AT[-1]], DIST[:, :]).then_inc(s_dist, 16)
                    elif s[0] == "merged":
                        split_high(l, SP_MERGED + s[1] + 1, mh[:, s[1], :], merged[:, s[1], :])
                    elif s[0] == "rope":
                        act.wait_ge(fp32_ready.sem, fp32_ready.at(l, SP_CQ + 3))
                        act.wait_ge(latent_copied.sem, latent_copied.at(l, 4))
                        nc.scalar.activation(rope_square[HD:MQ, :], latent[HD:MQ, 3, :], ACT.Square).then_inc(
                                rope_key_squared.sem, rope_key_squared.tick())
                    elif s[0] == "stat":
                        t = s[1]
                        rsqrt_guess(l, MEAN_OF[t["kind"]], t["stat"])
                        if t["kind"] == "cq":
                            for k in range(2):
                                split_high(l, SP_CQ + k + 1, lath[:, k, :], tmp[:, k, :])
                        if t["kind"] == "ckv":
                            split_high(l, SP_CQ + 3, lath[:, 2, :], tmp[:, 0, :])
                    elif s[0] == "gemm":
                        t = s[1]
                        k = t["kind"]
                        src = full(t["slot"][0])
                        if k in SQUARED:
                            rows = SQUARED[k]
                            if t["prev"] is not None:
                                act.wait_ge(stat_ready.sem, stat_ready.at(l, stat_of[t["prev"]["g"]] + 1))
                            act.wait_ge(tile_ready.sem, tile_ready.at(l, t["g"] + 1))
                            dst = ksq if k in ("mk", "ckv") else sq
                            nc.scalar.activation(dst[0:rows, t["par"], :], src[0:rows, :], ACT.Square).then_inc(
                                    square_ready.sem, square_ready.tick())
                        elif k == "ff":
                            act.wait_ge(decay_logit.sem, decay_logit.at(l, 1))
                            nc.scalar.activation(fa[0:8, :], fz[0:8, :], ACT.Abs).then_inc(
                                    act_chain.sem, act_chain.tick())
                            act.wait_ge(act_chain.sem, act_chain.at(l, act_chain.n))
                            nc.scalar.activation(fe[0:8, :], fa[0:8, :], ACT.Exp, scale=-1.0).then_inc(
                                    act_chain.sem, act_chain.tick())
                            act.wait_ge(act_chain.sem, act_chain.at(l, act_chain.n))
                            nc.scalar.activation(fl[0:8, :], fe[0:8, :], ACT.Ln, bias=1.0).then_inc(
                                    decay_log1p.sem, decay_log1p.tick())
                        elif k == "fv":
                            act.wait_ge(decay_summed.sem, decay_summed.at(l, 1))
                            for dst, row, src in ((qt, HD, ld), (kt, HD + 1, nld)):
                                act.dma_start(dst[row:row + 1, :, :], src[0:8, :]).then_inc(
                                        decay_placed.sem, decay_placed.tick(16))
                        elif k == "g":
                            act.wait_ge(tile_ready.sem, tile_ready.at(l, t["g"] + 1))
                            i = gate_ready.n
                            before = i - 2 - KD
                            if before >= KD:
                                act.wait_ge(fp32_ready.sem, fp32_ready.at(l, SP_MERGED + before - KD + 1))
                            elif before >= 0:
                                act.wait_ge(gate_added.sem, gate_added.at(l, before + 1))
                            elif i == 0:
                                act.wait_ge(decay_placed.sem, decay_placed.at(l, 32))
                            dst = merged[:, i, :] if t["m"][0] == FOX else gsb[:, i % 2, :]
                            nc.scalar.activation(dst, src, ACT.Tanh, scale=0.5).then_inc(
                                    gate_ready.sem, gate_ready.tick())

                def square_residual(base, i, par):
                    act.wait_ge(residual_updated.sem, residual_updated.at(l, i + (base + 1)))
                    act.wait_ge(sum_ready.sem, sum_ready.at(l, i + (base - 1)))
                    nc.scalar.activation(hsq[:, par, :], tile_of(h, i), ACT.Square).then_inc(
                            residual_squared.sem, residual_squared.tick())

                with act.Fori(0, WO_TILES - 3, 4) as m:
                    for j in range(4):
                        square_residual(0, m + j, j % 2)
                        split_high(l, m + (SP_NORM2 + j + 1), tile_of(xh, m + j), tmp[:, j % 2, :])
                for s_ in (residual_squared, high_ready):
                    s_.skip(WO_TILES - 4)
                rsqrt_guess(l, D, n_stats)
                with act.Fori(0, FT - 1, 2) as f:
                    for j in range(2):
                        for side, dst in ((0, cg), (1, cv)):
                            act.wait_ge(up_tile_scaled.sem, up_tile_scaled.at(l, f * 2 + (2 * j + side + 1)))
                            cw = f * 3 + (PC_CW + 3 * (side * FT + j))
                            nc.scalar.activation(
                                dst[:, j, :], full(2 * j + side), ACT.Identity,
                                scale=prm[:, bass.ds(cw + 2, 1)], bias=prm[:, bass.ds(f + (PC_CB + side * FT + j), 1)]).then_inc(
                                        conv_scaled.sem, conv_scaled.tick())
                        act.wait_ge(tile_freed.sem, tile_freed.at(l, f * 2 + (n_free + 2 * j + 1)))
                        nc.scalar.activation(si[:, j, :], cg[:, j, :], ACT.Silu).then_inc(
                                silu_ready.sem, silu_ready.tick())
                        split_high(l, f + (SP_FFN + j + 1), tile_of(ah, f + j), am[:, j, :])
                for s_, n_ in ((conv_scaled, 4), (silu_ready, 2), (high_ready, 2)):
                    s_.skip(n_ * (FT // 2 - 1))
                act.wait_ge(low_ready.sem, low_ready.at(l, SP_FFN + FT))
                act.dma_start(prm[:, :], PRM[l + 1, :, :]).then_inc(s_prm, 16)
                with act.Fori(0, KD - 3, 4) as m:
                    for j in range(4):
                        square_residual(WO_TILES, m + j, j % 2)
                residual_squared.skip(KD - 4)
            act.wait_ge(s_prm, 16 * (DEPTH + 1))

        @blk.tensor
        def _(pe):
            pe.sem_inc(s_start, STARTED_BEFORE)
            pe.wait_ge(s_cst, 16)
            with pe.Fori(0, DEPTH) as l:
                cur = {"b": 0}

                def block_at(c, i, chunk_no):
                    if i == 0:
                        pe.wait_ge(s_w, chunk_no + 1)
                        cur["fresh"] = True
                    a = i * P
                    return wh[c][:, a:a + P], wl[c][:, a:a + P]

                def issued(ins):
                    if cur.get("fresh"):
                        ins.then_inc(s_start, 1)
                        cur["fresh"] = False

                def take():
                    b = cur["b"]
                    cur["b"] += 1
                    c = b // BLK
                    return block_at(c % SPLIT, b % BLK, l * CHUNKS + c)

                def take_padded():
                    if cur["b"] % BLK == BLK // 2:
                        cur["b"] += BLK // 2
                    return take()

                def rows_out(slot, blocks, xhi, xlo, nk):
                    ins = None
                    for k in range(nk):
                        a_hi, a_lo = blocks()
                        x_hi = xhi(k)
                        for j in range(2):
                            sl = slice(j * TH, (j + 1) * TH)
                            a = nc.tensor.matmul(half(slot, j), a_hi, x_hi[:, sl], start=(k == 0), stop=False)
                            issued(a)
                            nc.tensor.matmul(half(slot, j), a_hi, xlo(k)[:, sl], start=False, stop=False)
                        for j in range(2):
                            sl = slice(j * TH, (j + 1) * TH)
                            ins = nc.tensor.matmul(half(slot, j), a_lo, x_hi[:, sl], start=False, stop=(k == nk - 1))
                    return ins

                def tok(tt):
                    return slice(0, P) if tt == 0 else slice(META + (tt - 1) * P, META + tt * P)

                def tokens_out(xhi, xlo, nk, width):
                    ins = None
                    for k in range(nk):
                        nb_ = width // P
                        first = take()
                        b0 = cur["b"] - 1
                        for _ in range(nb_ - 1):
                            cur["b"] += 1
                        c = (b0 // BLK) % SPLIT
                        a = (b0 % BLK) * P
                        whi, wlo = wh[c][:, a:a + width], wl[c][:, a:a + width]
                        for tt in range(QTILES):
                            o = value_bank(tt)[:, 0:width]
                            i0 = nc.tensor.matmul(o, xhi(k)[:, tok(tt)], whi, start=(k == 0), stop=False)
                            issued(i0)
                            nc.tensor.matmul(o, xhi(k)[:, tok(tt)], wlo, start=False, stop=False)
                            ins = nc.tensor.matmul(o, xlo(k)[:, tok(tt)], whi, start=False, stop=(k == nk - 1))
                    return ins

                def xk(t):
                    return lambda k: t[:, k, :]

                def stat(rhs, lhs, rows, first=True, last=True):
                    for j in range(2):
                        ins = nc.tensor.matmul(half(3, j), lhs[0:rows, :], rhs[0:rows, j * TH:(j + 1) * TH],
                                               start=first, stop=last)
                    return ins

                def norm_stat(which):
                    pe.wait_ge(sum_ready.sem, sum_ready.at(l, KD * which))
                    stat(ssum, ones, P).then_inc(stat_ready.sem, stat_ready.tick())

                copied = {}

                norm_stat(0)

                def x_ready(t, base):
                    def f(k):
                        pe.wait_ge(low_ready.sem, low_ready.at(l, base + k + 1))
                        return t[:, k, :]
                    return f

                for s in steps:
                    if s[0] == "gemm":
                        t = s[1]
                        kind = t["kind"]
                        for name, count in t["after"]:
                            pe.wait_ge(by_name[name].sem, by_name[name].at(l, count))
                        slot = t["slot"][0]
                        if kind == "ff":
                            rows_out(slot, take_padded, x_ready(xh, 0), xk(xl), KD).then_inc(
                                    tile_ready.sem, tile_ready.tick())
                            cur["b"] += BLK // 2
                        elif kind in ("fq", "fk", "cq", "ckv", "kr", "sq", "sk", "sv", "g"):
                            rows_out(slot, take, xk(xh), xk(xl), KD).then_inc(tile_ready.sem, tile_ready.tick())
                        elif kind == "mq":
                            if t["m"] == 0:
                                pe.wait_ge(low_ready.sem, low_ready.at(l, SP_CQ + 2))
                            rows_out(slot, take, xk(lath), xk(latl), 2).then_inc(tile_ready.sem, tile_ready.tick())
                        elif kind == "mk":
                            if t["m"] == 0:
                                pe.wait_ge(low_ready.sem, low_ready.at(l, SP_CQ + 3))
                            rows_out(slot, take, lambda k: lath[:, 2, :], lambda k: latl[:, 2, :], 1).then_inc(
                                    tile_ready.sem, tile_ready.tick())
                        elif kind == "fv":
                            tokens_out(xk(xh), xk(xl), KD, 512).then_inc(tile_ready.sem, tile_ready.tick())
                        elif kind == "svt":
                            pe.wait_ge(window_values_copied.sem, window_values_copied.at(l, 1))
                            for tt in range(QTILES):
                                ins = nc.tensor.transpose(ps[slot][:, tt * P:(tt + 1) * P], tmp[:, 0, tok(tt)], ident)
                            ins.then_inc(tile_ready.sem, tile_ready.tick())
                        elif kind == "mv":
                            pe.wait_ge(low_ready.sem, low_ready.at(l, SP_CQ + 3))
                            tokens_out(lambda k: lath[:, 2, :], lambda k: latl[:, 2, :], 1, 512).then_inc(
                                    tile_ready.sem, tile_ready.tick())
                            cur["b"] += 4
                        elif kind == "y":
                            if t["m"][1] == 0:
                                pe.wait_ge(heads_low.sem, heads_low.at(l, QTILES * (t["m"][0] + 1)))
                            rows_out(slot, take, xk(oth), xk(otl), BRANCH_TILES).then_inc(
                                    tile_ready.sem, tile_ready.tick())
                            if t["m"] == PADDED:
                                cur["b"] += 4
                    elif s[0] == "stat":
                        t = s[1]
                        kind = t["kind"]
                        i = t["stat"]
                        pe.wait_ge(statistic_read.sem, statistic_read.at(l, i))
                        pe.wait_ge(square_ready.sem, square_ready.at(l, t["sqn"] + 1))
                        if kind == "cq":
                            stat(sq[:, 1 - t["par"], :], ones, P, True, False)
                            stat(sq[:, t["par"], :], ones, P, False, True).then_inc(stat_ready.sem, stat_ready.tick())
                        elif kind == "mk":
                            if t["m"] == 0:
                                pe.wait_ge(rope_key_squared.sem, rope_key_squared.at(l, 1))
                            stat(ksq[:, t["par"], :], pair, P, True, False)
                            for j in range(2):
                                ins = nc.tensor.matmul(half(3, j), ones[HD:MQ, :], rope_square[HD:MQ, j * TH:(j + 1) * TH],
                                                       start=False, stop=True)
                            ins.then_inc(stat_ready.sem, stat_ready.tick())
                        elif kind == "mq":
                            stat(sq[:, t["par"], :], ones, MQ).then_inc(stat_ready.sem, stat_ready.tick())
                        elif kind == "ckv":
                            stat(ksq[:, t["par"], :], ones, P).then_inc(stat_ready.sem, stat_ready.tick())
                        else:
                            stat(sq[:, t["par"], :], pair, P).then_inc(stat_ready.sem, stat_ready.tick())
                    elif s[0] == "S":
                        u = s[1]
                        if u.h == 0 and u.b == QTILES - 1:
                            pe.wait_ge(qkv_written.sem, qkv_written.at(l, qkv_end[u.br]))
                            if u.br == FOX:
                                pe.wait_ge(decay_placed.sem, decay_placed.at(l, 32))
                        if u.i % (QTILES * HEADS) < 2:
                            name, count = u.slot_free
                            pe.wait_ge(by_name[name].sem, by_name[name].at(l, count))
                        if u.i >= 2:
                            pe.wait_ge(probs_ready.sem, probs_ready.at(l, u.i - 1))
                        rows = {FOX: HD + 2, MLA: P, SWA: HD}[u.br]
                        kh = u.h // 4 if u.br == SWA else u.h
                        for k0, kn, col in u.ranges:
                            ins = nc.tensor.matmul(ps[u.i % 2][0:u.nq, u.base + col:u.base + col + kn],
                                                   qt[0:rows, u.h, u.q0:u.q0 + P], kt[0:rows, kh, k0:k0 + kn],
                                                   start=True, stop=True)
                        ins.then_inc(scores_ready.sem, scores_ready.tick())
                    elif s[0] == "T":
                        u, p = s[1], s[2]
                        i = u.part_ids[p]
                        pe.wait_ge(probs_ready.sem, probs_ready.at(l, u.i + 1))
                        bank = 0 if u.base == 0 and i % 2 else 3
                        if bank in copied:
                            pe.wait_ge(transposed_copied.sem, transposed_copied.at(l, copied[bank]))
                        copied[bank] = i + 1
                        for j, (kt_i, col) in enumerate(u.parts[p]):
                            ins = nc.tensor.transpose(probs_bank(u, i)[:, j * P:(j + 1) * P],
                                                      probs[:, u.i % 2, col:col + P],
                                                      ident[0:u.nq, 0:u.nq])
                        ins.then_inc(probs_transposed.sem, probs_transposed.tick())
                    elif s[0] == "PV":
                        u, p = s[1], s[2]
                        i = u.part_ids[p]
                        pe.wait_ge(transposed_copied.sem, transposed_copied.at(l, i + 1))
                        gi = group_of[(u.br, u.b)]
                        if p == 0 and u.h == 0 and gi > 0:
                            pe.wait_ge(heads_normalised.sem, heads_normalised.at(l, gi))
                        vh = u.h // 4 if u.br == SWA else u.h
                        for j, (kt_i, col) in enumerate(u.parts[p]):
                            kn = META if kt_i == 0 else P
                            first = p == 0 and j == 0
                            final = p == len(u.parts) - 1 and j == len(u.parts[p]) - 1
                            ins = nc.tensor.matmul(ps[3][0:u.nq, u.h * HD:(u.h + 1) * HD],
                                                   pts[0:kn, i % 2, j * u.nq:(j + 1) * u.nq],
                                                   v[0:kn, kt_i, vh * HD:(vh + 1) * HD], start=first, stop=final)
                        ins.then_inc(pv_done.sem, pv_done.tick())
                    elif s[0] == "OT":
                        u = s[1]
                        gi = group_of[(u.br, u.b)]
                        pe.wait_ge(heads_normalised.sem, heads_normalised.at(l, gi + 1))
                        if u.b < QTILES - 2:
                            pe.wait_ge(heads_low.sem, heads_low.at(l, gi - 1))
                        if u.slot_free:
                            name, count = u.slot_free
                            pe.wait_ge(by_name[name].sem, by_name[name].at(l, count))
                        for c in range(BRANCH_TILES):
                            ins = nc.tensor.transpose(heads_bank(gi)[:, c * P:c * P + u.nq],
                                                      osb[0:u.nq, u.b, c * P:(c + 1) * P], ident[0:u.nq, 0:u.nq])
                        ins.then_inc(heads_transposed.sem, heads_transposed.tick())
                    elif s[0] == "end":
                        pe.wait_ge(probs_ready.sem, probs_ready.at(l, max(u.i for u in units if u.br == s[1]) + 1))
                        pe.wait_ge(heads_low.sem, heads_low.at(l, QTILES * (s[1] + 1)))
                c0 = cur["b"] // BLK
                assert cur["b"] % BLK == 0

                def loop_tile(n, c, first_chunk, slot, x_hi, x_lo, nk, start_chunk):
                    pos = {"b": 0}

                    def blocks():
                        b = pos["b"]
                        pos["b"] += 1
                        cc = c + b // BLK
                        return block_at(cc % SPLIT, b % BLK, n + (start_chunk + cc))
                    return rows_out(slot, blocks, x_hi, x_lo, nk)

                assert c0 % SPLIT == 0, c0
                with pe.Fori(0, WO_TILES - 3, 4) as m:
                    nbase = pe.snap(l * CHUNKS + m)
                    for j in range(4):
                        if j == 1:
                            pe.wait_ge(fp32_ready.sem, fp32_ready.at(l, SP_MERGED + KD))
                        pe.wait_ge(residual_updated.sem, residual_updated.at(l, m + (j - 3)))
                        loop_tile(nbase, j, 0, 3 - j, x_ready(mh, SP_MERGED) if j == 0 else xk(mh), xk(ml), KD, c0).then_inc(
                                tile_ready.sem, tile_ready.tick())
                tile_ready.skip(WO_TILES - 4)
                norm_stat(1)
                c_up = c0 + KD
                with pe.Fori(0, FT - 1, 2) as f:
                    nbase = pe.snap(l * CHUNKS + f * 2)
                    for j in range(4):
                        pe.wait_ge(tile_freed.sem, tile_freed.at(l, f * 2 + (n_free + j - 3)))
                        if j == 3:
                            pe.wait_ge(statistic_read.sem, statistic_read.at(l, n_stats + 1))
                        loop_tile(nbase, j, 0, j, x_ready(xh, SP_NORM2) if j == 0 else xk(xh), xk(xl), KD,
                                  c_up).then_inc(tile_ready.sem, tile_ready.tick())
                tile_ready.skip(UP_TILES - 4)
                c_dn = c_up + 2 * FT

                def last_ready(k):
                    if k == FT - 1:
                        pe.wait_ge(low_ready.sem, low_ready.at(l, SP_FFN + FT))
                    return ah[:, k, :]

                with pe.Fori(0, KD - 3, 4) as m:
                    nbase = pe.snap(l * CHUNKS + m * 3)
                    pe.wait_ge(low_ready.sem, low_ready.at(l, SP_FFN + FT - 1))
                    for j in range(4):
                        pe.wait_ge(residual_updated.sem, residual_updated.at(l, m + (WO_TILES + j - 3)))
                        loop_tile(nbase, 3 * j, 0, j, last_ready if j == 0 else xk(ah), xk(al), FT, c_dn).then_inc(
                                tile_ready.sem, tile_ready.tick())
                tile_ready.skip(KD - 4)
                assert c_dn + 3 * KD == CHUNKS

        @blk.vector
        def _(dve):
            def high_part(base, c):
                dve.wait_ge(s_raw[c % RAW], base * (16 // RAW) + 16 * (c // RAW + 1))
                if c >= AHEAD:
                    dve.wait_ge(s_start, base + (c + 2 - SPLIT + STARTED_BEFORE))
                nc.vector.tensor_copy(wh[c % SPLIT][:, :], raw[:, c % RAW, :]).then_inc(s_hi, 1)

            nc.vector.memset(gts[:, 2:3], EPS)
            nc.vector.memset(gts[:, 3:4], -EPS).then_inc(s_ini, 1)
            for k in range(KD):
                dve.wait_ge(residual_squared.sem, k + 1)
                if k == 0:
                    nc.vector.tensor_copy(ssum[:, :], hsq[:, 0, :]).then_inc(sum_ready.sem, 1)
                else:
                    dve.wait_ge(sum_ready.sem, k)
                    nc.vector.tensor_tensor(ssum[:, :], ssum[:, :], hsq[:, k % 2, :], ALU.add).then_inc(
                            sum_ready.sem, 1)
            for i in range(KD // 2):
                dve.wait_ge(s_hin[i], 16)
            dve.sem_inc(residual_updated.sem, KD)
            dve.wait_ge(s_cst, 16)
            for n in range(AHEAD):
                high_part(0, n)
            with dve.Fori(0, DEPTH) as l:

                rstd_used = []
                split = {"next": AHEAD}

                def split_to(c):
                    for n in range(split["next"], c + AHEAD + 1):
                        high_part(l * CHUNKS, n)
                    split["next"] = max(split["next"], c + AHEAD + 1)

                def newton(stat):
                    dve.wait_ge(guess_ready.sem, guess_ready.at(l, stat + 1))
                    s_ = stat % 2
                    nc.vector.scalar_tensor_tensor(
                        out=negmean[:, s_, :], in0=negmean[:, s_, :], scalar=0.5, in1=guess2[:, s_, :],
                        op0=ALU.mult, op1=ALU.mult).then_inc(dve_chain.sem, dve_chain.tick())
                    dve.wait_ge(dve_chain.sem, dve_chain.at(l, dve_chain.n))
                    for used in rstd_used:
                        dve.wait_ge(used.sem, used.at(l, used.n))
                    rstd_used.clear()
                    nc.vector.scalar_tensor_tensor(
                        out=rstd[:, :], in0=negmean[:, s_, :], scalar=1.5, in1=guess[:, s_, :],
                        op0=ALU.add, op1=ALU.mult).then_inc(rsqrt_ready.sem, rsqrt_ready.tick())
                    dve.wait_ge(rsqrt_ready.sem, rsqrt_ready.at(l, rsqrt_ready.n))

                def low(out, hi, tile):
                    dve.wait_ge(high_ready.sem, high_ready.at(l, low_ready.n + 1))
                    return nc.vector.tensor_tensor(out, tile, hi.bitcast(F32), ALU.subtract).then_inc(
                            low_ready.sem, low_ready.tick())

                def sum_again(stat):
                    dve.wait_ge(guess_ready.sem, guess_ready.at(l, stat + 1))
                    nc.vector.memset(ssum[:, :], 0.0)

                def norm_input():
                    newton(0)
                    rstd_used.append(fp32_ready)

                    def scale(k):
                        if k >= 2:
                            dve.wait_ge(low_ready.sem, low_ready.at(l, k - 1))
                        nc.vector.scalar_tensor_tensor(
                            out=tmp[:, k % 2, :], in0=h[:, k, :], scalar=prm[:, PC_N1 + k:PC_N1 + k + 1],
                            in1=rstd[:, :], op0=ALU.mult, op1=ALU.mult).then_inc(fp32_ready.sem, fp32_ready.tick())
                    scale(0)
                    for k in range(KD):
                        if k + 1 < KD:
                            scale(k + 1)
                        low(xl[:, k, :], xh[:, k, :], tmp[:, k % 2, :])
                    sum_again(0)

                dve.wait_ge(s_prm, l * 16 + 16)
                dve.wait_ge(s_ini, 1)
                nc.vector.tensor_scalar(gts[:, 0:1], prm[:, PC_FQ:PC_FQ + 1], HD ** -0.5, None, ALU.mult)
                nc.vector.tensor_scalar(gts[:, 1:2], prm[:, PC_SQ:PC_SQ + 1], HD ** -0.5, None, ALU.mult)
                nc.vector.tensor_scalar(nsink[:, :], prm[:, PC_SINK:PC_SINK + HEADS], -1.0, None, ALU.mult).then_inc(
                        dve_chain.sem, dve_chain.tick())
                dve.wait_ge(dve_chain.sem, dve_chain.at(l, dve_chain.n))
                norm_input()
                for s in steps:
                    if s[0] == "stat":
                        t = s[1]
                        kind = t["kind"]
                        src = full(t["slot"][0])
                        newton(t["stat"])
                        rstd_used.append(fp32_ready if kind in ("cq", "ckv") else qkv_written)
                        if kind in ("fq", "fk", "sq", "sk"):
                            dst = qt if kind in ("fq", "sq") else kt
                            g = {"fq": gts[:, 0:1], "sq": gts[:, 1:2], "fk": prm[:, PC_FK:PC_FK + 1],
                                 "sk": prm[:, PC_SK:PC_SK + 1]}[kind]
                            for e in range(2):
                                r = slice(e * HD, (e + 1) * HD)
                                ins = nc.vector.scalar_tensor_tensor(
                                    out=dst[0:HD, 2 * t["m"] + e, :], in0=src[r, :], scalar=g[r, :],
                                    in1=rstd[r, :], op0=ALU.mult, op1=ALU.mult)
                            ins.then_inc(qkv_written.sem, qkv_written.tick())
                        elif kind == "cq":
                            for k in range(2):
                                nc.vector.scalar_tensor_tensor(
                                    out=tmp[:, k, :], in0=latent[:, k, :],
                                    scalar=prm[:, PC_QA + k:PC_QA + k + 1], in1=rstd[:, :],
                                    op0=ALU.mult, op1=ALU.mult).then_inc(fp32_ready.sem, fp32_ready.tick())
                            for k in range(2):
                                low(latl[:, k, :], lath[:, k, :], tmp[:, k, :])
                        elif kind == "ckv":
                            dve.wait_ge(low_ready.sem, low_ready.at(l, low_ready.n))
                            nc.vector.scalar_tensor_tensor(
                                out=tmp[:, 0, :], in0=latent[:, 2, :], scalar=prm[:, PC_KVA:PC_KVA + 1], in1=rstd[:, :],
                                op0=ALU.mult, op1=ALU.mult).then_inc(fp32_ready.sem, fp32_ready.tick())
                            low(latl[:, 2, :], lath[:, 2, :], tmp[:, 0, :])
                        elif kind == "mq":
                            nc.vector.tensor_tensor(tmp[:, t["m"] % 2, :], src, gq[:, :],
                                                                               ALU.mult).then_inc(
                                                                                       tile_freed.sem, tile_freed.tick())
                            dve.wait_ge(tile_freed.sem, tile_freed.at(l, tile_freed.n))
                            nc.vector.tensor_tensor(qt[:, t["m"], :], tmp[:, t["m"] % 2, :], rstd[:, :],
                                                            ALU.mult).then_inc(qkv_written.sem, qkv_written.tick())
                        elif kind == "mk":
                            for e in range(2):
                                r = slice(e * HD, (e + 1) * HD)
                                nc.vector.tensor_tensor(kt[HD:P, 2 * t["m"] + e, :], krr[r, :], rstd[r, :], ALU.mult)
                                ins = nc.vector.scalar_tensor_tensor(
                                    out=kt[0:HD, 2 * t["m"] + e, :], in0=src[r, :],
                                    scalar=prm[r, PC_MKN:PC_MKN + 1], in1=rstd[r, :], op0=ALU.mult, op1=ALU.mult)
                            ins.then_inc(qkv_written.sem, qkv_written.tick())
                    elif s[0] == "gemm":
                        t = s[1]
                        kind = t["kind"]
                        src = full(t["slot"][0])
                        split_to(t["chunk"])
                        if kind == "ff":
                            dve.wait_ge(tile_ready.sem, tile_ready.at(l, t["g"] + 1))
                            nc.vector.tensor_scalar(fz[0:8, :], src[0:8, :], prm[0:8, PC_FB:PC_FB + 1], None,
                                                             ALU.add).then_inc(tile_freed.sem, tile_freed.tick())
                            dve.wait_ge(tile_freed.sem, tile_freed.at(l, tile_freed.n))
                            nc.vector.tensor_scalar(fm[0:8, :], fz[0:8, :], 0.0, None, ALU.min).then_inc(
                                    decay_logit.sem, decay_logit.tick())
                            dve.wait_ge(decay_log1p.sem, decay_log1p.at(l, 1))
                            dve.wait_ge(decay_logit.sem, decay_logit.at(l, 1))
                            nc.vector.tensor_tensor(fs[0:8, :], fm[0:8, :], fl[0:8, :], ALU.subtract).then_inc(
                                    dve_chain.sem, dve_chain.tick())
                            dve.wait_ge(dve_chain.sem, dve_chain.at(l, dve_chain.n))
                            nc.vector.tensor_tensor_scan(ld[0:8, :], cs[0:8, :], fs[0:8, :], 0.0,
                                                                 ALU.mult, ALU.add).then_inc(
                                                                         dve_chain.sem, dve_chain.tick())
                            dve.wait_ge(dve_chain.sem, dve_chain.at(l, dve_chain.n))
                            nc.vector.tensor_scalar(nld[0:8, :], ld[0:8, :], -1.0, None, ALU.mult).then_inc(
                                    dve_chain.sem, dve_chain.tick())
                            dve.wait_ge(dve_chain.sem, dve_chain.at(l, dve_chain.n))
                            nc.vector.memset(qt[HD:HD + 2, :, :], 1.0)
                            nc.vector.memset(kt[HD:HD + 2, :, :], 1.0).then_inc(decay_summed.sem, decay_summed.tick())
                        elif kind == "sv":
                            dve.wait_ge(tile_ready.sem, tile_ready.at(l, t["g"] + 1))
                            nc.vector.tensor_copy(tmp[:, 0, :], src).then_inc(
                                    window_values_copied.sem, window_values_copied.tick())
                        elif kind == "svt":
                            dve.wait_ge(tile_ready.sem, tile_ready.at(l, t["g"] + 1))
                            bank = ps[t["slot"][0]]
                            nc.vector.tensor_copy(v[0:META, 0, 0:P], bank[0:META, 0:P])
                            nc.vector.tensor_copy(
                                v[:, 1:4, 0:P], bank[:, P:4 * P].rearrange("p (a f) -> p a f", a=3))
                            nc.vector.tensor_copy(v[:, 4, 0:P], bank[:, 4 * P:5 * P]).then_inc(
                                    qkv_written.sem, qkv_written.tick())
                        elif kind in ("fv", "mv"):
                            width = HEADS * HD
                            dve.wait_ge(tile_ready.sem, tile_ready.at(l, t["g"] + 1))
                            for tt in range(QTILES):
                                rows = META if tt == 0 else P
                                ins = nc.vector.tensor_copy(v[0:rows, tt, 0:width], value_bank(tt)[0:rows, 0:width])
                            ins.then_inc(qkv_written.sem, qkv_written.tick())
                        elif kind in ("cq", "ckv", "kr"):
                            if latent_copied.n == 0:
                                dve.wait_ge(decay_placed.sem, decay_placed.at(l, 32))
                            if kind == "kr":
                                dve.wait_ge(tile_ready.sem, tile_ready.at(l, t["g"] + 1))
                            else:
                                dve.wait_ge(square_ready.sem, square_ready.at(l, t["sqn"] + 1))
                            nc.vector.tensor_copy(latent[:, latent_copied.n, :], src).then_inc(
                                    latent_copied.sem, latent_copied.tick())
                        elif kind == "y":
                            br, d = t["m"]
                            dve.wait_ge(tile_ready.sem, tile_ready.at(l, t["g"] + 1))
                            dve.wait_ge(gate_ready.sem, gate_ready.at(l, gate_used.n + 1))
                            gate = merged[:, d, :] if br == FOX else gsb[:, gate_used.n % 2, :]
                            nc.vector.scalar_tensor_tensor(out=gate, in0=gate, scalar=1.0, in1=src,
                                                                   op0=ALU.add, op1=ALU.mult).then_inc(
                                                                           gate_used.sem, gate_used.tick())
                            if br != FOX:
                                dve.wait_ge(gate_used.sem, gate_used.at(l, gate_used.n))
                                ins = nc.vector.tensor_tensor(merged[:, d, :], merged[:, d, :], gate,
                                                              ALU.add)
                                if br == MLA:
                                    ins.then_inc(gate_added.sem, gate_added.tick())
                                    dve.wait_ge(gate_added.sem, gate_added.at(l, gate_added.n))
                                else:
                                    ins.then_inc(fp32_ready.sem, fp32_ready.tick())
                    elif s[0] == "rope":
                        gk = tmp[:, 1, :]
                        dve.wait_ge(low_ready.sem, low_ready.at(l, low_ready.n))
                        nc.vector.tensor_scalar(gq[:, :], cs, prm[:, PC_MQ:PC_MQ + 1], MQ ** -0.5,
                                                ALU.mult, ALU.mult)
                        nc.vector.tensor_scalar(gk, cs, prm[:, PC_MK:PC_MK + 1], None, ALU.mult).then_inc(
                                dve_chain.sem, dve_chain.tick())
                        dve.wait_ge(dve_chain.sem, dve_chain.at(l, dve_chain.n))
                        t1, t2, key = latent[:, 0, :], rstd, latent[:, 3, :]
                        nc.vector.tensor_tensor(t1[HD:MQ, :], key[HD:MQ, :], gk[HD:MQ, :], ALU.mult)
                        nc.vector.tensor_tensor(t2[HD:MQ, :], key[MQ:P, :], gk[MQ:P, :], ALU.mult).then_inc(
                                dve_chain.sem, dve_chain.tick())
                        dve.wait_ge(dve_chain.sem, dve_chain.at(l, dve_chain.n))
                        for r in range(0, P, ROPE):
                            ins = nc.vector.tensor_tensor(krr[r:r + ROPE, :], t1[HD:MQ, :], t2[HD:MQ, :], ALU.add)
                        ins.then_inc(dve_chain.sem, dve_chain.tick())
                        dve.wait_ge(dve_chain.sem, dve_chain.at(l, dve_chain.n))
                    elif s[0] == "end":
                        dve.wait_ge(pv_done.sem, pv_done.at(l, parts_end[s[1]]))
                    elif s[0] == "merged":
                        low(ml[:, s[1], :], mh[:, s[1], :], merged[:, s[1], :])
                    elif s[0] == "S":
                        u = s[1]
                        gi = group_of[(u.br, u.b)]
                        dve.wait_ge(scores_ready.sem, scores_ready.at(l, u.i + 1))
                        sc = ps[u.i % 2][0:u.nq, u.base:u.base + u.nk]
                        if u.h == 0 and gi >= 2:
                            dve.wait_ge(heads_normalised.sem, heads_normalised.at(l, gi - 1))
                        if u.br == SWA:
                            if u.b == QTILES - 1 and u.h == 0:
                                dve.wait_ge(s_dist, l * 16 + 16)
                            nc.vector.scalar_tensor_tensor(
                                out=sc, in0=dist[0:u.nq, DIST_AT[u.b]:DIST_AT[u.b + 1]], scalar=-(2.0 ** -(u.h + 1)), in1=sc, op0=ALU.mult, op1=ALU.add).then_inc(
                                        dve_chain.sem, dve_chain.tick())
                            dve.wait_ge(dve_chain.sem, dve_chain.at(l, dve_chain.n))
                            nc.vector.tensor_reduce(nraw[0:u.nq, gi % 2, u.h:u.h + 1], sc, AX.X, ALU.max,
                                                            negate=True).then_inc(dve_chain.sem, dve_chain.tick())
                            dve.wait_ge(dve_chain.sem, dve_chain.at(l, dve_chain.n))
                            nc.vector.tensor_tensor(nmax[0:u.nq, gi % 2, u.h:u.h + 1],
                                                            nraw[0:u.nq, gi % 2, u.h:u.h + 1],
                                                            nsink[0:u.nq, u.h:u.h + 1], ALU.min).then_inc(
                                                                    max_ready.sem, max_ready.tick())
                        else:
                            w = u.end - u.q0
                            dg = sc[:, u.nk - w:u.nk]
                            nc.vector.tensor_tensor(dg, dg, mask[:, 0:w], ALU.add).then_inc(
                                    dve_chain.sem, dve_chain.tick())
                            dve.wait_ge(dve_chain.sem, dve_chain.at(l, dve_chain.n))
                            nc.vector.tensor_reduce(nmax[0:u.nq, gi % 2, u.h:u.h + 1], sc, AX.X, ALU.max,
                                                            negate=True).then_inc(max_ready.sem, max_ready.tick())
                    elif s[0] == "O":
                        u = s[1]
                        gi = group_of[(u.br, u.b)]
                        r = slice(0, u.nq)
                        dve.wait_ge(probs_ready.sem, probs_ready.at(l, u.i + 1))
                        total = rsum
                        if u.br == SWA:
                            nc.vector.tensor_tensor(skx[r, gi % 2, :], nmax[r, gi % 2, :],
                                                            nsink[r, :], ALU.subtract).then_inc(
                                                                    sink_shifted.sem, sink_shifted.tick())
                            dve.wait_ge(sink_exp_ready.sem, sink_exp_ready.at(l, sink_shifted.n))
                            nc.vector.tensor_tensor(rtot[r, gi % 2, :], ske[r, gi % 2, :],
                                                            rsum[r, gi % 2, :], ALU.add).then_inc(
                                                                    dve_chain.sem, dve_chain.tick())
                            dve.wait_ge(dve_chain.sem, dve_chain.at(l, dve_chain.n))
                            total = rtot
                        nc.vector.reciprocal(rinv[r, gi % 2, :], total[r, gi % 2, :]).then_inc(
                                dve_chain.sem, dve_chain.tick())
                        dve.wait_ge(dve_chain.sem, dve_chain.at(l, dve_chain.n))
                        dve.wait_ge(pv_done.sem, pv_done.at(l, u.part_ids[-1] + 1))
                        nc.vector.tensor_tensor(
                            osb[r, u.b, :].rearrange("p (h d) -> p h d", h=HEADS),
                            ps[3][r, 0:512].rearrange("p (h d) -> p h d", h=HEADS),
                            rinv[r, gi % 2, :].rearrange("p (h a) -> p h a", a=1).broadcast_to([u.nq, HEADS, HD]),
                            ALU.mult).then_inc(heads_normalised.sem, heads_normalised.tick())
                    elif s[0] == "OT":
                        u = s[1]
                        gi = group_of[(u.br, u.b)]
                        dve.wait_ge(heads_high.sem, heads_high.at(l, gi + 1))
                        src = heads_bank(gi)[:, :].rearrange("p (c q) -> p c q", c=BRANCH_TILES)[:, :, 0:u.end - u.q0]
                        nc.vector.tensor_tensor(otl[:, :, u.q0:u.end], src,
                                                        oth[:, :, u.q0:u.end].bitcast(F32), ALU.subtract).then_inc(
                                                                heads_low.sem, heads_low.tick())

                def residual(base_g, base, i, slot, scale):
                    dve.wait_ge(tile_ready.sem, tile_ready.at(l, i + (base_g + 1)))
                    nc.vector.scalar_tensor_tensor(out=tile_of(h, i), in0=full(slot), scalar=scale,
                                                   in1=tile_of(h, i), op0=ALU.mult, op1=ALU.add).then_inc(
                                                           residual_updated.sem, residual_updated.tick())

                def sum_square(base, i, par):
                    dve.wait_ge(residual_squared.sem, residual_squared.at(l, i + (base + 1)))
                    dve.wait_ge(sum_ready.sem, sum_ready.at(l, i + base))
                    nc.vector.tensor_tensor(ssum[:, :], ssum[:, :], hsq[:, par, :], ALU.add).then_inc(
                            sum_ready.sem, sum_ready.tick())

                c_wo = split["next"]
                assert c_wo == c_out + AHEAD
                assert fp32_ready.n == SP_NORM2 and low_ready.n == SP_NORM2
                with dve.Fori(0, WO_TILES - 3, 4) as m:
                    for j in range(4):
                        high_part(l * CHUNKS + m, c_wo + j)
                        residual(g_wo, 0, m + j, 3 - j, 0.5)
                        dve.wait_ge(residual_updated.sem, residual_updated.at(l, m + (j + 1)))
                        nc.vector.tensor_scalar(tmp[:, j % 2, :], tile_of(h, m + j), prm[:, bass.ds(m + (PC_N2 + j), 1)],
                                                None, ALU.mult).then_inc(fp32_ready.sem, fp32_ready.tick())
                        sum_square(0, m + j, j % 2)
                        dve.wait_ge(high_ready.sem, high_ready.at(l, m + (SP_NORM2 + j + 1)))
                        nc.vector.tensor_tensor(tile_of(xl, m + j), tmp[:, j % 2, :], tile_of(xh, m + j).bitcast(F32),
                                                ALU.subtract).then_inc(low_ready.sem, low_ready.tick())
                for s_ in (fp32_ready, low_ready):
                    s_.skip(WO_TILES - 4)
                for s_ in (residual_updated, sum_ready):
                    s_.skip(WO_TILES - 4)
                newton(n_stats)
                sum_again(n_stats)
                tm0, x0 = fp32_ready.n, low_ready.n
                assert tm0 == SP_FFN and x0 == SP_FFN, (tm0, x0)
                with dve.Fori(0, FT - 1, 2) as f:
                    for j in range(2):
                        for side, dst in ((0, cg), (1, cv)):
                            slot = 2 * j + side
                            high_part(l * CHUNKS + f * 2, c_wo + WO_TILES + slot)
                            src = full(slot)
                            cw = f * 3 + (PC_CW + 3 * (side * FT + j))
                            dve.wait_ge(tile_ready.sem, tile_ready.at(l, f * 2 + (g_up + slot + 1)))
                            nc.vector.tensor_tensor(src, src, rstd[:, :], ALU.mult).then_inc(
                                    up_tile_scaled.sem, up_tile_scaled.tick())
                            dve.wait_ge(conv_scaled.sem, conv_scaled.at(l, f * 2 + (2 * j + side + 1)))
                            nc.vector.scalar_tensor_tensor(
                                out=dst[:, j, 1:T], in0=src[:, 0:T - 1], scalar=prm[:, bass.ds(cw + 1, 1)],
                                in1=dst[:, j, 1:T], op0=ALU.mult, op1=ALU.add).then_inc(
                                        dve_chain.sem, dve_chain.tick())
                            dve.wait_ge(dve_chain.sem, dve_chain.at(l, f * 2 + dve_chain.n))
                            ins = nc.vector.scalar_tensor_tensor(
                                out=dst[:, j, 2:T], in0=src[:, 0:T - 2], scalar=prm[:, bass.ds(cw, 1)],
                                in1=dst[:, j, 2:T], op0=ALU.mult, op1=ALU.add)
                            ins.then_inc(tile_freed.sem, tile_freed.tick())
                        dve.wait_ge(tile_freed.sem, tile_freed.at(l, f * 2 + (n_free + 2 * j + 2)))
                        dve.wait_ge(silu_ready.sem, silu_ready.at(l, f + (j + 1)))
                        nc.vector.tensor_tensor(am[:, j, :], si[:, j, :], cv[:, j, :], ALU.mult).then_inc(
                                fp32_ready.sem, fp32_ready.tick())
                        dve.wait_ge(fp32_ready.sem, fp32_ready.at(l, f + (tm0 + j + 1)))
                        dve.wait_ge(high_ready.sem, high_ready.at(l, f + (x0 + j + 1)))
                        nc.vector.tensor_tensor(tile_of(al, f + j), am[:, j, :],
                                                        tile_of(ah, f + j).bitcast(F32), ALU.subtract).then_inc(
                                                                low_ready.sem, low_ready.tick())
                for s_, n_ in ((up_tile_scaled, 4), (dve_chain, 4), (tile_freed, 4), (fp32_ready, 2), (low_ready, 2)):
                    s_.skip(n_ * (FT // 2 - 1))
                with dve.Fori(0, KD - 3, 4) as m:
                    for j in range(4):
                        for i in range(3):
                            high_part(l * CHUNKS + m * 3, c_wo + WO_TILES + UP_TILES + 3 * j + i)
                        residual(g_dn, WO_TILES, m + j, j, 1.0)
                        sum_square(WO_TILES, m + j, j % 2)
                for s_ in (residual_updated, sum_ready):
                    s_.skip(KD - 4)

    return {s.name: s.n for s in signals}


def pack_weights(inp):
    zero = np.zeros((P, P), np.float32)
    half = ROPE // 2

    def block(l, what, k, m):
        w_in = inp["w_in"][l]
        r = slice(k * P, (k + 1) * P)
        at = {"fq": O_FQ, "fk": O_FK, "fv": O_FV, "cq": O_CQ, "ckv": O_CKV, "sq": O_SQ, "sk": O_SK, "sv": O_SV}
        if what == "pad":
            return zero
        if what in at:
            return w_in[r, at[what] + m * P:at[what] + (m + 1) * P]
        out = zero.copy()
        if what == "ff":
            out[:, 0:HEADS] = w_in[r, O_FF:O_FF + HEADS]
        elif what == "kr":
            out[:, HD:MQ] = w_in[r, O_KR:O_KR + ROPE]
            out[:, MQ:MQ + half] = w_in[r, O_KR + half:O_KR + ROPE]
            out[:, MQ + half:P] = w_in[r, O_KR:O_KR + half]
        elif what == "mq":
            w = inp["mla_w_q_up"][l][r, m * MQ:(m + 1) * MQ]
            out[:, 0:MQ] = w
            out[:, MQ:MQ + half] = w[:, HD + half:MQ]
            out[:, MQ + half:P] = w[:, HD:HD + half]
        elif what == "mk":
            for e in range(2):
                c = (2 * m + e) * 2 * HD
                out[:, e * HD:(e + 1) * HD] = inp["mla_w_kv_up"][l][:, c:c + HD]
        elif what == "mv":
            for e in range(2):
                c = (2 * m + e) * 2 * HD + HD
                out[:, e * HD:(e + 1) * HD] = inp["mla_w_kv_up"][l][:, c:c + HD]
        elif what[0] == "g":
            c = O_GATE + int(what[1]) * D + m * P
            out = w_in[r, c:c + P]
        elif what[0] == "y":
            out = inp["w_branch"][l][int(what[1])][r, m * P:(m + 1) * P]
        elif what == "wo":
            out = inp["w_o"][l][r, m * P:(m + 1) * P]
        elif what == "up":
            out = inp["ffn_w_up"][l][r, m * P:(m + 1) * P]
        elif what == "dn":
            out = inp["ffn_w_down"][l][r, m * P:(m + 1) * P]
        return out

    W = np.zeros((DEPTH * CHUNKS + AHEAD, P, CW), np.float32)
    for l in range(DEPTH):
        for i, (what, k, m) in enumerate(PLAN):
            W[l * CHUNKS + i // BLK, :, (i % BLK) * P:(i % BLK + 1) * P] = block(l, what, k, m)
    return W


def pack_params(inp):
    p = np.zeros((DEPTH + 1, P, PC_ALL), np.float32)
    half = ROPE // 2

    def cols(x, n):
        return x.reshape(n, P).T

    for l in range(DEPTH):
        p[l, :, PC_N1:PC_N1 + KD] = cols(inp["norm1_g"][l], KD)
        p[l, :, PC_N2:PC_N2 + KD] = cols(inp["norm2_g"][l], KD)
        for c, name in ((PC_FQ, "fox_q_g"), (PC_FK, "fox_k_g"), (PC_SQ, "swa_q_g"), (PC_SK, "swa_k_g")):
            p[l, :HD, c] = inp[name][l]
            p[l, HD:, c] = inp[name][l]
        p[l, :, PC_QA:PC_QA + 2] = cols(inp["mla_q_a_g"][l], 2)
        p[l, :, PC_KVA] = inp["mla_kv_a_g"][l]
        for c, name in ((PC_MQ, "mla_q_g"), (PC_MK, "mla_k_g")):
            g = inp[name][l]
            p[l, :MQ, c] = g
            p[l, MQ:MQ + half, c] = g[HD + half:]
            p[l, MQ + half:, c] = g[HD:HD + half]
        for e in range(2):
            p[l, e * HD:(e + 1) * HD, PC_MKN] = inp["mla_k_g"][l][:HD]
        p[l, :HEADS, PC_FB] = inp["fox_forget_b"][l]
        p[l, :, PC_SINK:PC_SINK + HEADS] = inp["swa_sinks"][l][None, :]
        for i in range(3):
            p[l, :, PC_CW + i:PC_CB:3] = cols(inp["ffn_conv_w"][l][i], 2 * FT)
        p[l, :, PC_CB:PC_ALL] = cols(inp["ffn_conv_b"][l], 2 * FT)
    return p


def kernel(**inputs):
    import concourse.bacc as bacc
    from concourse.bass_utils import run_bass_kernel_spmd

    inp = {k: np.asarray(v) for k, v in inputs.items()}
    tokens = np.concatenate([inp["meta_tokens"], inp["x"][0]], axis=0)
    arrays = {
        "weights": pack_weights(inp),
        "tokens": np.ascontiguousarray(tokens.T.reshape(KD, P, T).transpose(1, 0, 2)),
        "params": pack_params(inp),
        "constants": constants(),
        "distances": alibi_tables(),
    }

    def program(counts):
        nc = bacc.Bacc("TRN2", target_bir_lowering=False, num_devices=1, dynamic_dma_scratch_size=2048)
        args = [nc.dram_tensor(n, a.shape, F32, kind="ExternalInput").ap() for n, a in arrays.items()]
        args.append(nc.dram_tensor("out", (P, KD, SEQ), F32, kind="ExternalOutput").ap())
        return nc, build(nc, *args, counts)

    _, counts = program({})
    nc, again = program(counts)
    assert again == counts
    r = run_bass_kernel_spmd(nc, [arrays], core_ids=[0])
    out = r.results[0]["out"]
    return np.ascontiguousarray(out.transpose(2, 1, 0)).reshape(1, SEQ, D)
```
